# Optimizing a Trainium2 kernel written in Bass

```python
import jax, jax.numpy as jnp
from jax import lax
import numpy as np

D_MODEL = 1024
BATCH = 1
SEQ = 1024
DEPTH = 1
DEC_BATCH = 8
DEC_SEQ = 4
PAST_LEN = 1024
PAGE_SIZE = 128

N_HEADS = 8
HEAD_DIM = 64
N_KV_HEADS = 2
GROUP = N_HEADS // N_KV_HEADS
NSA_WIDTH = N_HEADS * HEAD_DIM
KV_WIDTH = N_KV_HEADS * HEAD_DIM
CMP_LEN = 32
CMP_STRIDE = 16
CMP_HIDDEN = 128
SLC_BLK = 64
TOP_N = 16
WINDOW = 512
Q_BLOCK = 128
ROPE_THETA = 10000.0
ATTN_SCALE = HEAD_DIM ** -0.5
FORCE_BONUS = 1e4
NEG_INF = -1e30
GMLP_WIDTH = 512
GMLP_GROUPS = 8
GMLP_GROUP_DIM = GMLP_WIDTH // GMLP_GROUPS
GMLP_CHUNK = 128
N_MEM = 256
CROSS_HEADS = 4
CROSS_HEAD_DIM = D_MODEL // CROSS_HEADS
CROSS_SCALE = CROSS_HEAD_DIM ** -0.5
D_FF = -(-8 * D_MODEL // (3 * 256)) * 256
NORM_EPS = 1e-6
IN_SIZES = (NSA_WIDTH, KV_WIDTH, KV_WIDTH, KV_WIDTH, KV_WIDTH, KV_WIDTH, KV_WIDTH, N_HEADS * 3,
            GMLP_WIDTH, GMLP_WIDTH, D_MODEL, D_MODEL)
IN_WIDTH = sum(IN_SIZES)
IN_SPLITS = tuple(sum(IN_SIZES[:i + 1]) for i in range(len(IN_SIZES) - 1))

kernel_name = 'nsa_gmlp_hybrid_step'

def rms_norm(x, g):
    xf = x.astype(jnp.float32)
    y = xf * lax.rsqrt(jnp.mean(xf * xf, axis=-1, keepdims=True) + NORM_EPS)
    return (y * g.astype(jnp.float32)).astype(x.dtype)

def layer_norm(x, g, b):
    xf = x.astype(jnp.float32)
    xc = xf - jnp.mean(xf, axis=-1, keepdims=True)
    var = jnp.mean(xc * xc, axis=-1, keepdims=True)
    return (xc * lax.rsqrt(var + NORM_EPS) * g.astype(jnp.float32) + b.astype(jnp.float32)).astype(x.dtype)

def rope(x, pos):
    half = HEAD_DIM // 2
    inv_freq = ROPE_THETA ** (-jnp.arange(half, dtype=jnp.float32) / half)
    ang = pos.astype(jnp.float32)[:, None] * inv_freq[None, :]
    shape = (pos.shape[0],) + (1,) * (x.ndim - 3) + (half,)
    cos, sin = jnp.cos(ang).reshape(shape), jnp.sin(ang).reshape(shape)
    xf = x.astype(jnp.float32)
    x1, x2 = xf[..., :half], xf[..., half:]
    return jnp.concatenate([x1 * cos - x2 * sin, x2 * cos + x1 * sin], axis=-1).astype(x.dtype)

def mixer_inputs(h, w_in, pos):
    B, S, _ = h.shape
    q, kc, vc, ks, vs, kw, vw, gn, u, v, ga, gb = jnp.split(h @ w_in, IN_SPLITS, axis=-1)
    heads = lambda t: t.reshape(B, S, N_KV_HEADS, HEAD_DIM)
    q = rope(q.reshape(B, S, N_KV_HEADS, GROUP, HEAD_DIM), pos)
    gn = jax.nn.sigmoid(gn.reshape(B, S, N_KV_HEADS, GROUP, 3))
    return (q, rope(heads(kc), pos), heads(vc), rope(heads(ks), pos), heads(vs),
            rope(heads(kw), pos), heads(vw), gn, jax.nn.gelu(u), jax.nn.gelu(v), ga, gb)

def masked_softmax(s, mask):
    s = jnp.where(mask, s, NEG_INF)
    e = jnp.where(mask, jnp.exp(s - jnp.max(s, axis=-1, keepdims=True)), 0.0)
    return e / jnp.maximum(jnp.sum(e, axis=-1, keepdims=True), 1e-30)

def attend_shared(q, k, v, mask):
    s = jnp.einsum('bqhgd,bkhd->bhgqk', q, k).astype(jnp.float32) * ATTN_SCALE
    p = masked_softmax(s, mask)
    return jnp.einsum('bhgqk,bkhd->bqhgd', p.astype(v.dtype), v), p

def attend_gathered(q, k, v, mask):
    s = jnp.einsum('bqhgd,bqhkd->bqhgk', q, k).astype(jnp.float32) * ATTN_SCALE
    p = masked_softmax(s, mask[:, :, :, None, :])
    return jnp.einsum('bqhgk,bqhkd->bqhgd', p.astype(v.dtype), v)

def cmp_chunk_proj(rows, w1):
    B, L = rows.shape[:2]
    c = rows.reshape(B, L // CMP_STRIDE, CMP_STRIDE, N_KV_HEADS, HEAD_DIM)
    lead = jnp.einsum('bcshd,sdf->bchf', c, w1[:CMP_STRIDE])
    trail = jnp.einsum('bcshd,sdf->bchf', c, w1[CMP_STRIDE:])
    return lead, trail

def cmp_finish(lead, trail, pe, w1, w2):
    pre = lead[:, :-1] + trail[:, 1:] + jnp.einsum('sd,sdf->f', pe, w1)
    return jnp.einsum('bnhf,fd->bnhd', jax.nn.gelu(pre), w2)

def cmp_to_slc_weights(n_cmp, n_slc):
    cs = jnp.arange(n_cmp)[:, None] * CMP_STRIDE
    ss = jnp.arange(n_slc)[None, :] * SLC_BLK
    shared = jnp.minimum(cs + CMP_LEN, ss + SLC_BLK) - jnp.maximum(cs, ss)
    return jnp.maximum(shared, 0).astype(jnp.float32) / CMP_LEN

def nsa_attend(q, qpos, gn, ck, cv, cend, n_slc, gather_sel, kw, vw, kwpos):
    B, Q = q.shape[:2]
    o_cmp, p_cmp = attend_shared(q, ck, cv, cend[None, :] <= qpos[:, None])
    score = jnp.einsum('bhqn,nm->bqhm', p_cmp.sum(axis=2), cmp_to_slc_weights(ck.shape[1], n_slc))
    blk = jnp.arange(n_slc)
    qblk = (qpos // SLC_BLK)[:, None]
    forced = (blk == 0) | (blk == qblk) | (blk == qblk - 1)
    score = jnp.where((blk <= qblk)[:, None], score + FORCE_BONUS * forced[:, None], NEG_INF)
    _, idx = lax.top_k(score, min(TOP_N, n_slc))
    k_sel, v_sel = gather_sel(idx)
    kpos = (idx[..., None] * SLC_BLK + jnp.arange(SLC_BLK)).reshape(B, Q, N_KV_HEADS, -1)
    o_sel = attend_gathered(q, k_sel, v_sel, kpos <= qpos[None, :, None, None])
    wmask = ((kwpos[None, :] >= 0) & (kwpos[None, :] <= qpos[:, None])
             & (kwpos[None, :] > qpos[:, None] - WINDOW))
    o_win, _ = attend_shared(q, kw, vw, wmask)
    o = gn[..., 0:1] * o_cmp + gn[..., 1:2] * o_sel + gn[..., 2:3] * o_win
    return o.reshape(B, Q, NSA_WIDTH)

def nsa_prompt(q, gn, kc, vc, ks, vs, kw, vw, pe, w1, w2):
    B, S = q.shape[:2]
    ck = cmp_finish(*cmp_chunk_proj(kc, w1[0]), pe[0], w1[0], w2[0])
    cv = cmp_finish(*cmp_chunk_proj(vc, w1[1]), pe[1], w1[1], w2[1])
    cend = jnp.arange(ck.shape[1], dtype=jnp.int32) * CMP_STRIDE + (CMP_LEN - 1)
    n_slc = S // SLC_BLK
    kb = ks.reshape(B, n_slc, SLC_BLK, N_KV_HEADS, HEAD_DIM)
    vb = vs.reshape(B, n_slc, SLC_BLK, N_KV_HEADS, HEAD_DIM)
    bi = jnp.arange(B)[:, None, None, None, None]
    hi = jnp.arange(N_KV_HEADS)[None, None, :, None, None]
    r = jnp.arange(SLC_BLK)

    def gather_sel(idx):
        i5 = idx[..., None]
        shape = idx.shape[:3] + (-1, HEAD_DIM)
        return kb[bi, i5, r, hi].reshape(shape), vb[bi, i5, r, hi].reshape(shape)

    kw_pad = jnp.pad(kw, ((0, 0), (WINDOW, 0), (0, 0), (0, 0)))
    vw_pad = jnp.pad(vw, ((0, 0), (WINDOW, 0), (0, 0), (0, 0)))

    def query_block(q0):
        qpos = q0 + jnp.arange(Q_BLOCK, dtype=jnp.int32)
        take = lambda t, n: lax.dynamic_slice_in_dim(t, q0, n, axis=1)
        kwpos = q0 - WINDOW + jnp.arange(WINDOW + Q_BLOCK, dtype=jnp.int32)
        return nsa_attend(take(q, Q_BLOCK), qpos, take(gn, Q_BLOCK), ck, cv, cend, n_slc, gather_sel,
                          take(kw_pad, WINDOW + Q_BLOCK), take(vw_pad, WINDOW + Q_BLOCK), kwpos)

    o = lax.map(query_block, jnp.arange(0, S, Q_BLOCK, dtype=jnp.int32))
    return jnp.swapaxes(o, 0, 1).reshape(B, S, NSA_WIDTH)

def nsa_sample(l, q, gn, kc, vc, ks, vs, kw, vw, pool_ck, pool_cv, pool_sk, pool_sv,
               page_table, win_k, win_v, pe, w1, w2):
    DB, DS = q.shape[:2]
    past = page_table.shape[1] * PAGE_SIZE
    qpos = past + jnp.arange(DS, dtype=jnp.int32)
    n_new_rows = (DS // CMP_STRIDE) * CMP_STRIDE

    def compressed(pool, new_rows, j):
        rows = pool[l, page_table].reshape(DB, past, N_KV_HEADS, HEAD_DIM)
        lead, trail = cmp_chunk_proj(rows, w1[j])
        if n_new_rows:
            lead_n, trail_n = cmp_chunk_proj(new_rows[:, :n_new_rows], w1[j])
            lead = jnp.concatenate([lead, lead_n], axis=1)
            trail = jnp.concatenate([trail, trail_n], axis=1)
        return cmp_finish(lead, trail, pe[j], w1[j], w2[j])

    ck, cv = compressed(pool_ck, kc, 0), compressed(pool_cv, vc, 1)
    cend = jnp.arange(ck.shape[1], dtype=jnp.int32) * CMP_STRIDE + (CMP_LEN - 1)

    n_past_blk = past // SLC_BLK
    n_slc = -(-(past + DS) // SLC_BLK)
    n_new_blk = n_slc - n_past_blk
    pad = ((0, 0), (0, n_new_blk * SLC_BLK - DS), (0, 0), (0, 0))
    kb_new = jnp.pad(ks, pad).reshape(DB, n_new_blk, SLC_BLK, N_KV_HEADS, HEAD_DIM)
    vb_new = jnp.pad(vs, pad).reshape(DB, n_new_blk, SLC_BLK, N_KV_HEADS, HEAD_DIM)
    bi = jnp.arange(DB)[:, None, None, None, None]
    hi = jnp.arange(N_KV_HEADS)[None, None, :, None, None]
    r = jnp.arange(SLC_BLK)

    def gather_sel(idx):
        i5 = idx[..., None]
        row = jnp.minimum(i5, n_past_blk - 1) * SLC_BLK + r
        phys, off = page_table[bi, row // PAGE_SIZE], row % PAGE_SIZE
        nb = jnp.clip(i5 - n_past_blk, 0, n_new_blk - 1)
        in_past = (i5 < n_past_blk)[..., None]
        shape = idx.shape[:3] + (-1, HEAD_DIM)
        pick = lambda pool, new_blocks: jnp.where(
            in_past, pool[l, phys, off, hi], new_blocks[bi, nb, r, hi]).reshape(shape)
        return pick(pool_sk, kb_new), pick(pool_sv, vb_new)

    kwin = jnp.concatenate([win_k, kw], axis=1)
    vwin = jnp.concatenate([win_v, vw], axis=1)
    wb = win_k.shape[1]
    kwpos = past - wb + jnp.arange(wb + DS, dtype=jnp.int32)
    o = nsa_attend(q, qpos, gn, ck, cv, cend, n_slc, gather_sel, kwin, vwin, kwpos)
    return o, kwin[:, DS:], vwin[:, DS:]

def gmlp_spatial(u, v, ln_g, ln_b, ws, bs):
    B, S, _ = u.shape
    L = min(S, GMLP_CHUNK)
    vn = layer_norm(v, ln_g, ln_b).reshape(B, S // L, L, GMLP_GROUPS, GMLP_GROUP_DIM)
    w = jnp.tril(ws[:, :L, :L])
    s = jnp.einsum('gij,bcjgd->bcigd', w, vn) + bs[:, :L].T[None, None, :, :, None]
    return u * s.reshape(B, S, GMLP_WIDTH)

def merge_branches(o_a, o_b, ga, gb, w_a, w_b, w_out):
    m = jax.nn.sigmoid(ga) * (o_a @ w_a) + jax.nn.sigmoid(gb) * (o_b @ w_b)
    return m @ w_out

def memory_kv(mem, g_mem, w_ck, w_cv):
    B, M, _ = mem.shape
    hm = rms_norm(mem, g_mem)
    return ((hm @ w_ck).reshape(B, M, CROSS_HEADS, CROSS_HEAD_DIM),
            (hm @ w_cv).reshape(B, M, CROSS_HEADS, CROSS_HEAD_DIM))

def cross_attend(h, mk, mv, w_cq, w_co):
    B, S, _ = h.shape
    q = (h @ w_cq).reshape(B, S, CROSS_HEADS, CROSS_HEAD_DIM)
    s = jnp.einsum('bqhd,bmhd->bhqm', q, mk).astype(jnp.float32) * CROSS_SCALE
    p = jax.nn.softmax(s, axis=-1).astype(mv.dtype)
    return jnp.einsum('bhqm,bmhd->bqhd', p, mv).reshape(B, S, D_MODEL) @ w_co

def swiglu(h, w_gate, w_up, w_down):
    return (jax.nn.silu(h @ w_gate) * (h @ w_up)) @ w_down

def setup_inputs(seed: int = 0) -> dict:
    key = jax.random.key(seed)
    keys = iter(jax.random.split(key, 48))
    nrm = lambda shape, scale=1.0: scale * jax.random.normal(next(keys), shape, jnp.float32)
    gain = lambda shape: 1.0 + 0.02 * jax.random.normal(next(keys), shape, jnp.float32)
    n_pages = PAST_LEN // PAGE_SIZE
    n_used = DEC_BATCH * n_pages
    n_pool = n_used + n_used // 4
    wbuf = min(WINDOW, PAST_LEN)
    pool_shape = (DEPTH, n_pool, PAGE_SIZE, N_KV_HEADS, HEAD_DIM)
    win_shape = (DEPTH, DEC_BATCH, wbuf, N_KV_HEADS, HEAD_DIM)
    mem_shape = (DEPTH, DEC_BATCH, N_MEM, CROSS_HEADS, CROSS_HEAD_DIM)
    page_table = jax.random.permutation(next(keys), n_pool)[:n_used].reshape(DEC_BATCH, n_pages).astype(jnp.int32)
    dd = D_MODEL ** -0.5
    return {
        'x_prompt': nrm((BATCH, SEQ, D_MODEL)),
        'x_sample': nrm((DEC_BATCH, DEC_SEQ, D_MODEL)),
        'mem_prompt': nrm((BATCH, N_MEM, D_MODEL)),
        'cache_cmp_k': nrm(pool_shape),
        'cache_cmp_v': nrm(pool_shape),
        'cache_slc_k': nrm(pool_shape),
        'cache_slc_v': nrm(pool_shape),
        'page_table': page_table,
        'state_win_k': nrm(win_shape),
        'state_win_v': nrm(win_shape),
        'cache_mem_k': nrm(mem_shape),
        'cache_mem_v': nrm(mem_shape),
        'g_mix': gain((DEPTH, D_MODEL)),
        'w_in': nrm((DEPTH, D_MODEL, IN_WIDTH), dd),
        'cmp_pe': nrm((DEPTH, 2, CMP_LEN, HEAD_DIM), 0.1),
        'cmp_w1': nrm((DEPTH, 2, CMP_LEN, HEAD_DIM, CMP_HIDDEN), (CMP_LEN * HEAD_DIM) ** -0.5),
        'cmp_w2': nrm((DEPTH, 2, CMP_HIDDEN, HEAD_DIM), CMP_HIDDEN ** -0.5),
        'gmlp_ln_g': gain((DEPTH, GMLP_WIDTH)),
        'gmlp_ln_b': nrm((DEPTH, GMLP_WIDTH), 0.02),
        'gmlp_ws': nrm((DEPTH, GMLP_GROUPS, GMLP_CHUNK, GMLP_CHUNK), GMLP_CHUNK ** -0.5),
        'gmlp_bs': gain((DEPTH, GMLP_GROUPS, GMLP_CHUNK)),
        'w_branch_a': nrm((DEPTH, NSA_WIDTH, D_MODEL), NSA_WIDTH ** -0.5),
        'w_branch_b': nrm((DEPTH, GMLP_WIDTH, D_MODEL), GMLP_WIDTH ** -0.5),
        'w_out': nrm((DEPTH, D_MODEL, D_MODEL), dd),
        'g_cross': gain((DEPTH, D_MODEL)),
        'g_mem': gain((DEPTH, D_MODEL)),
        'w_cq': nrm((DEPTH, D_MODEL, D_MODEL), dd),
        'w_ck': nrm((DEPTH, D_MODEL, D_MODEL), dd),
        'w_cv': nrm((DEPTH, D_MODEL, D_MODEL), dd),
        'w_co': nrm((DEPTH, D_MODEL, D_MODEL), dd),
        'g_ffn': gain((DEPTH, D_MODEL)),
        'w_gate': nrm((DEPTH, D_MODEL, D_FF), dd),
        'w_up': nrm((DEPTH, D_MODEL, D_FF), dd),
        'w_down': nrm((DEPTH, D_FF, D_MODEL), D_FF ** -0.5),
        'g_final': gain((D_MODEL,)),
    }

def reference(x_prompt, x_sample, mem_prompt, cache_cmp_k, cache_cmp_v, cache_slc_k, cache_slc_v,
              page_table, state_win_k, state_win_v, cache_mem_k, cache_mem_v,
              g_mix, w_in, cmp_pe, cmp_w1, cmp_w2, gmlp_ln_g, gmlp_ln_b, gmlp_ws, gmlp_bs,
              w_branch_a, w_branch_b, w_out, g_cross, g_mem, w_cq, w_ck, w_cv, w_co,
              g_ffn, w_gate, w_up, w_down, g_final):
    S, DS = x_prompt.shape[1], x_sample.shape[1]
    pos_p = jnp.arange(S, dtype=jnp.int32)
    pos_s = page_table.shape[1] * PAGE_SIZE + jnp.arange(DS, dtype=jnp.int32)
    wb_p = min(WINDOW, S)
    xp, xs = x_prompt, x_sample
    per_layer = []
    for l in range(DEPTH):
        gm = (gmlp_ln_g[l], gmlp_ln_b[l], gmlp_ws[l], gmlp_bs[l])
        mw = (w_branch_a[l], w_branch_b[l], w_out[l])
        q, kc, vc, ks, vs, kw, vw, gn, u, v, ga, gb = mixer_inputs(rms_norm(xp, g_mix[l]), w_in[l], pos_p)
        o_a = nsa_prompt(q, gn, kc, vc, ks, vs, kw, vw, cmp_pe[l], cmp_w1[l], cmp_w2[l])
        xp = xp + merge_branches(o_a, gmlp_spatial(u, v, *gm), ga, gb, *mw)
        mk, mv = memory_kv(mem_prompt, g_mem[l], w_ck[l], w_cv[l])
        xp = xp + cross_attend(rms_norm(xp, g_cross[l]), mk, mv, w_cq[l], w_co[l])
        xp = xp + swiglu(rms_norm(xp, g_ffn[l]), w_gate[l], w_up[l], w_down[l])
        prompt_new = (kc, vc, ks, vs, kw[:, S - wb_p:], vw[:, S - wb_p:], mk, mv)
        q, kc, vc, ks, vs, kw, vw, gn, u, v, ga, gb = mixer_inputs(rms_norm(xs, g_mix[l]), w_in[l], pos_s)
        o_a, win_k, win_v = nsa_sample(l, q, gn, kc, vc, ks, vs, kw, vw, cache_cmp_k, cache_cmp_v,
                                       cache_slc_k, cache_slc_v, page_table, state_win_k[l], state_win_v[l],
                                       cmp_pe[l], cmp_w1[l], cmp_w2[l])
        xs = xs + merge_branches(o_a, gmlp_spatial(u, v, *gm), ga, gb, *mw)
        xs = xs + cross_attend(rms_norm(xs, g_cross[l]), cache_mem_k[l], cache_mem_v[l], w_cq[l], w_co[l])
        xs = xs + swiglu(rms_norm(xs, g_ffn[l]), w_gate[l], w_up[l], w_down[l])
        per_layer.append(prompt_new + (kc, vc, ks, vs, win_k, win_v, v))
    (ck_p, cv_p, sk_p, sv_p, wk_p, wv_p, mk_p, mv_p,
     ck_s, cv_s, sk_s, sv_s, wk_s, wv_s, gv_s) = [jnp.stack(t) for t in zip(*per_layer)]
    y_prompt = rms_norm(xp, g_final)
    y_sample = rms_norm(xs, g_final)
    return (y_prompt, y_sample, ck_p, cv_p, sk_p, sv_p, wk_p, wv_p, mk_p, mv_p,
            ck_s, cv_s, sk_s, sv_s, wk_s, wv_s, gv_s)


_drawn_inputs = setup_inputs


def setup_inputs(seed=0):
    import zlib

    import numpy as np

    out = dict(_drawn_inputs(seed))
    spreads = {}
    factors = {'cache_cmp_k': 3.877,
     'cache_slc_k': 4.151,
     'cache_slc_v': 3.322,
     'g_mix': 2.729,
     'cmp_pe': 3.177,
     'gmlp_ln_g': 23.188,
     'gmlp_ln_b': 61.63,
     'gmlp_bs': 7.15,
     'g_cross': 29.394,
     'g_mem': 7.79,
     'g_ffn': 3.944,
     'g_final': 22.998}
    for name, (base, spread) in spreads.items():
        noise = np.random.default_rng([zlib.crc32(name.encode()), seed]).standard_normal(out[name].shape)
        drawn = base * np.exp(spread * noise) if base else spread * noise
        out[name] = __import__('jax').numpy.asarray(drawn.astype(out[name].dtype))
    for name, factor in factors.items():
        out[name] = (out[name] * factor).astype(out[name].dtype)
    return out
```

```python
from contextlib import ExitStack

import numpy as np

import concourse.bass as bass
from concourse import mybir

ALU = mybir.AluOpType
ACT = mybir.ActivationFunctionType
F32 = mybir.dt.float32
I32 = mybir.dt.int32
X = mybir.AxisListType.X

P = 128
D = 1024
KD = D // P
NP = 1024
NB = 8
NS = 4
TS = NB * NS
T = NP + TS
NT = NP // P
CH = 3
C = T // CH
HD = 64
G = 4
CMP = 63
SRC = NB + 1
PAIRS = 512
PAGES = 8
N_POOL = 80
WIN = 512
NM = 256
FF = 2816
KF = FF // P
EPS = 1e-6
NEG = -1e30
U_COL = 1304
GN_COL = 1280
GA_COL = 2328
GB_COL = 3352


def consts():
    half = HD // 2
    inv = (np.float32(10000.0) ** (-np.arange(half, dtype=np.float32) / np.float32(half))).astype(np.float32)
    pos = np.concatenate([np.arange(NP), np.tile(NP + np.arange(NS), NB)]).astype(np.float32)
    ang = (pos[None, :] * inv[:, None]).astype(np.float32)
    rot = np.zeros((P, P), np.float32)
    for m in range(P):
        if m % HD < half:
            rot[m + half, m] = -1.0
        else:
            rot[m - half, m] = 1.0
    a = np.arange(P)
    cend = 16 * np.arange(CMP) + 31
    seen = (cend[None, None, :] <= (P * np.arange(NT)[None, :, None] + a[:, None, None])).astype(np.float32)
    rb, rh, rg, rs = a // 32, a // 16 % 2, a // 4 % 4, a % 4
    same = (rb[:, None] == rb) & (rh[:, None] == rh) & (rs[:, None] == rs)
    shared = np.zeros((CMP, 16), np.float32)
    for n in range(CMP):
        for m in range(16):
            shared[n, m] = max(min(16 * n + 32, 64 * m + 64) - max(16 * n, 64 * m), 0) / 32
    s4 = np.arange(4)
    row_of = np.zeros((TS, 2, P), np.float32)
    for grp in range(2):
        row_of[(4 * grp + rb) * 4 + rs, grp, a] = 1.0
    hg = np.zeros((P, 8, 3), np.float32)
    hg[a, rh * 4 + rg, :] = 1.0
    lane = np.zeros((TS, 8, TS), np.float32)
    for j in range(TS):
        for k in range(TS):
            if j // 4 == k // 4 and j % 4 <= k % 4:
                lane[j, :, k] = 1.0
    return {
        "c_ident": np.eye(P, dtype=np.float32),
        "c_cos": np.tile(np.cos(ang), (4, 1)).astype(np.float32),
        "c_sin": np.tile(np.sin(ang), (4, 1)).astype(np.float32),
        "c_rot": rot,
        "c_tril": (a[:, None] <= a[None, :]).astype(np.float32),
        "c_lane": lane,
        "c_diag": np.where(a[None, :] <= a[:, None], 0.0, NEG).astype(np.float32),
        "c_far": np.where(a[None, :] > a[:, None], 0.0, NEG).astype(np.float32),
        "c_seen": seen,
        "c_hidden": np.where(seen > 0, 0.0, NEG).astype(np.float32),
        "c_same": same.astype(np.float32),
        "c_shared": shared,
        "c_new": np.where(s4[None, :] <= rs[:, None], 0.0, NEG).astype(np.float32),
        "c_old": np.where(s4[None, :] > rs[:, None], 0.0, NEG).astype(np.float32),
        "c_row_of": row_of,
        "c_hg": hg,
        "c_block": np.tile(np.arange(16, dtype=np.float32), (P, 1)),
    }


class Chain:

    def __init__(self, eng, sem):
        self.eng, self.sem, self.n = eng, sem, 0

    def __call__(self, ins):
        self.n += 1
        ins.then_inc(self.sem, 1)
        self.eng.wait_ge(self.sem, self.n)


class Stream:

    def __init__(self, sem, name, tiles, sets, loads=1):
        self.tiles, self.sets, self.loads = tiles, sets, loads
        self.w_in = [sem(f"{name}_w{s}") for s in range(2)]
        self.done = sem(f"{name}_done")
        self.freed = sem(f"{name}_freed")

    def load(self, sp, copies):
        with sp.Fori(0, self.tiles // 2) as it:
            for s in range(2):
                sp.wait_ge(self.done, 6 * it + 3 * s + 3)
                for dst, src in copies(2 * it + s, s):
                    sp.dma_start(dst, src).then_inc(self.w_in[s], 16)

    def multiply(self, pe, groups):
        pe.sem_inc(self.done, 6)
        with pe.Fori(0, self.tiles // 2) as it:
            for s in range(2):
                pe.wait_ge(self.w_in[s], 16 * self.loads * it + 16 * self.loads)
                for c in range(CH):
                    pe.wait_ge(self.freed, 6 * it + 3 * s + c + 1)
                    for out, terms in groups((3 * s + c) % self.sets, s, c):
                        for j, (lhsT, rhs) in enumerate(terms):
                            last = pe.matmul(out, lhsT, rhs, start=j == 0, stop=j == len(terms) - 1)
                    last.then_inc(self.done, 1)

    def take(self, eng, use):
        eng.sem_inc(self.freed, self.sets)
        with eng.Fori(0, self.tiles // 2) as it:
            for s in range(2):
                for c in range(CH):
                    eng.wait_ge(self.done, 6 * it + 3 * s + c + 7)
                    use(2 * it + s, (3 * s + c) % self.sets, c).then_inc(self.freed, 1)


def cols(c):
    return slice(c * C, c * C + C)


def build(nc, i, o):
    with ExitStack() as top, nc.allow_non_contiguous_dma(reason="small tables"):
        taken = []

        def sem(name):
            taken.append(nc.alloc_semaphore(name))
            return taken[-1]

        def clear_semaphores():
            nc.clear_and_free_semaphores(taken)
            nc.all_engine_barrier()
            taken.clear()

        def sb(ctx, name, shape, dt=F32):
            return ctx.enter_context(nc.sbuf_tensor(name, shape, dt))

        def banks(ctx, n):
            return [ctx.enter_context(nc.psum_tensor(f"bank{k}_{nc.next_id()}", [P, 512], F32)) for k in range(n)]

        xT = sb(top, "xT", [P, KD, T])
        hT = sb(top, "hT", [P, KD, T])
        ident = sb(top, "ident", [P, P])
        ones = sb(top, "ones", [P, P])
        gains = sb(top, "gains", [P, 5, KD])
        G_MIX, G_CROSS, G_MEM, G_FFN, G_FINAL = range(5)

        load_x(nc, i, sem, sb, banks, xT, ident, ones, gains)
        norm(nc, "mix", sem, sb, banks, xT, hT, T, CH, gains, G_MIX, ones)
        with ExitStack() as mid:
            qk = sb(mid, "qk", [P, 10, T])
            uv = sb(mid, "uv", [P, 8, T])
            with ExitStack() as att:
                vtok = sb(att, "vtok", [P, NT, 2, P])
                gates = sb(att, "gates", [P, NT + 1, 24])
                project(nc, i, sem, sb, banks, hT, qk, uv)
                rope(nc, i, sem, sb, banks, qk)
                rows_and_gmlp(nc, i, o, sem, sb, banks, hT, qk, uv, vtok, gates, ident)
                ck = sb(att, "ck", [P, SRC, CMP])
                cv = sb(att, "cv", [CMP, SRC, P])
                compress(nc, i, o, sem, sb, banks, uv, ck, cv, ident)
                oT = sb(att, "oT", [P, G, T])
                attend_prompt(nc, i, sem, sb, banks, qk, vtok, gates, ck, cv, oT, ident)
                attend_sample(nc, i, o, sem, sb, banks, qk, uv, gates, ck, cv, oT, ident)
                clear_semaphores()
                merge(nc, i, sem, sb, banks, hT, oT, uv, qk)
            add_product(nc, "out", sem, sb, banks, i["w_out"][0], qk, xT, KD)
            norm(nc, "cross", sem, sb, banks, xT, hT, T, CH, gains, G_CROSS, ones)
            plain_product(nc, "cq", sem, sb, banks, i["w_cq"][0], hT, uv)
            with ExitStack() as mem:
                mkT = sb(mem, "mkT", [P, KD, NM])
                mv = sb(mem, "mv", [P, 2, D])
                memory(nc, i, o, sem, sb, banks, mkT, mv, ident, ones, gains, G_MEM)
                cross_prompt(nc, sem, sb, banks, uv, qk, mkT, mv, ident)
            cross_sample(nc, i, sem, sb, banks, uv, qk, ident)
            add_product(nc, "co", sem, sb, banks, i["w_co"][0], qk, xT, KD)
        norm(nc, "ffn", sem, sb, banks, xT, hT, T, CH, gains, G_FFN, ones)
        with ExitStack() as ffn:
            aT = sb(ffn, "aT", [P, KF, T])
            gate_up(nc, i, sem, sb, banks, hT, aT)
            add_product(nc, "down", sem, sb, banks, i["w_down"][0], aT, xT, KF)
        norm(nc, "final", sem, sb, banks, xT, hT, T, CH, gains, G_FINAL, ones)
        store_y(nc, o, sem, sb, banks, hT, ident)


def load_x(nc, i, sem, sb, banks, xT, ident, ones, gains):
    with ExitStack() as ctx:
        xin = sb(ctx, "xin", [P, 3, D])
        tp = banks(ctx, 4)
        const_in, ones_set = sem("const_in"), sem("ones_set")
        x_in = [sem(f"x_in{s}") for s in range(3)]
        turned = [sem(f"x_turned{h}") for h in range(2)]
        taken = [sem(f"x_taken{h}") for h in range(2)]
        with nc.Block() as block:
            @block.sync
            def _(sp):
                sp.dma_start(ident[:], i["c_ident"]).then_inc(const_in, 16)
                sp.dma_start(xin[0:TS, 2, :], i["x_sample"].rearrange("b s d -> (b s) d")).then_inc(x_in[2], 16)
                with sp.Fori(0, NT // 2) as it:
                    for s in range(2):
                        sp.wait_ge(turned[1], 2 * it + s + 1)
                        sp.dma_start(xin[:, s, :], i["x_prompt"][0, bass.ds((2 * it + s) * P, P), :]).then_inc(x_in[s], 16)

            @block.gpsimd
            def _(pool):
                pool.memset(ones[:], 1.0).then_inc(ones_set, 1)

            def turn(pe, h, s, rows, src):
                for k in range(4):
                    last = pe.transpose(tp[2 * h + s][:, k * P:k * P + rows], src[:, (4 * h + k) * P:(4 * h + k + 1) * P],
                                        ident[0:rows, 0:rows])
                last.then_inc(turned[h], 1)

            @block.tensor
            def _(pe):
                pe.wait_ge(const_in, 16 * 6)
                pe.sem_inc(turned[0], 2)
                pe.sem_inc(turned[1], 2)
                with pe.Fori(0, NT // 2) as it:
                    for s in range(2):
                        pe.wait_ge(x_in[s], 16 * it + 16)
                        for h in range(2):
                            pe.wait_ge(taken[h], 2 * it + s + 1)
                            turn(pe, h, s, P, xin[:, s, :])
                pe.wait_ge(x_in[2], 16)
                for h in range(2):
                    pe.wait_ge(taken[h], NT + 1)
                    turn(pe, h, 0, TS, xin[0:TS, 2, :])

            def take(eng, h, copy):
                eng.sem_inc(taken[h], 2)
                with eng.Fori(0, NT // 2) as it:
                    for s in range(2):
                        eng.wait_ge(turned[h], 2 * it + s + 3)
                        copy(xT[:, 4 * h:4 * h + 4, bass.ds((2 * it + s) * P, P)],
                             tp[2 * h + s][:].rearrange("p (k c) -> p k c", k=4)).then_inc(taken[h], 1)
                eng.wait_ge(turned[h], NT + 3)
                copy(xT[:, 4 * h:4 * h + 4, NP:T],
                     tp[2 * h][:].rearrange("p (k c) -> p k c", k=4)[:, :, 0:TS]).then_inc(taken[h], 1)

            @block.scalar
            def _(act):
                for n, name in enumerate(("g_mix", "g_cross", "g_mem", "g_ffn")):
                    act.dma_start(gains[:, n, :], i[name][0].rearrange("(k p) -> p k", p=P)).then_inc(const_in, 16)
                act.dma_start(gains[:, 4, :], i["g_final"].rearrange("(k p) -> p k", p=P)).then_inc(const_in, 16)
                take(act, 0, act.copy)

            @block.vector
            def _(dve):
                take(dve, 1, dve.tensor_copy)


def norm(nc, name, sem, sb, banks, src, dst, width, chunks, gains, g, ones):
    n = width // chunks
    with ExitStack() as ctx:
        sq = sb(ctx, f"{name}_sq", [P, 2, KD, n])
        part = sb(ctx, f"{name}_part", [P, chunks, n])
        std = sb(ctx, f"{name}_std", [P, chunks, n])
        ps = banks(ctx, chunks)
        squared, summed, spread, rooted, chain = (sem(f"{name}_{x}") for x in ("squared", "summed", "spread", "rooted", "chain"))
        with nc.Block() as block:
            @block.scalar
            def _(act):
                for c in range(chunks):
                    if c >= 2:
                        act.wait_ge(summed, c - 1)
                    act.square(sq[:, c % 2], src[:, 0:KD, c * n:(c + 1) * n]).then_inc(squared, 1)
                for c in range(chunks):
                    act.wait_ge(chain, c + 1)
                    act.sqrt(std[:, c], std[:, c]).then_inc(rooted, 1)

            @block.tensor
            def _(pe):
                for c in range(chunks):
                    pe.wait_ge(summed, c + 1)
                    pe.matmul(ps[c][:, 0:n], ones[:], part[:, c], start=True, stop=True).then_inc(spread, 1)

            @block.vector
            def _(dve):
                for c in range(chunks):
                    dve.wait_ge(squared, c + 1)
                    dve.tensor_reduce(part[:, c], sq[:, c % 2].rearrange("p k t -> p t k"), X, ALU.add).then_inc(summed, 1)
                ch = Chain(dve, chain)
                for c in range(chunks):
                    dve.wait_ge(spread, c + 1)
                    ch(dve.tensor_scalar(std[:, c], ps[c][:, 0:n], 1.0 / D, EPS, ALU.mult, ALU.add))
                for c in range(chunks):
                    dve.wait_ge(rooted, c + 1)
                    ch(dve.reciprocal(part[:, c], std[:, c]))
                    for k in range(KD):
                        dve.scalar_tensor_tensor(dst[:, k, c * n:(c + 1) * n], src[:, k, c * n:(c + 1) * n], gains[:, g, k:k + 1],
                                                 part[:, c], ALU.mult, ALU.mult)


def project(nc, i, sem, sb, banks, hT, qk, uv):
    w = i["w_in"][0].rearrange("(k p) n -> p k n", p=P)
    with ExitStack() as ctx:
        slots = sb(ctx, "in_w", [P, 4, KD, P])
        ps = banks(ctx, 6)
        parts = [(Stream(sem, "q", 4, 6, loads=2), qk, ACT.Copy, 0), (Stream(sem, "kv", 6, 6), qk[:, 4:10], ACT.Copy, 2),
                 (Stream(sem, "uv", 8, 6), uv, ACT.Gelu_apprx_tanh, 0)]

        def q_load(n, s):
            return [(slots[:, s, :, HD * h:HD * h + HD], w[:, :, bass.ds(n * HD + G * HD * h, HD)]) for h in range(2)]

        with nc.Block() as block:
            @block.sync
            def _(sp):
                parts[0][0].load(sp, q_load)
                parts[1][0].load(sp, lambda n, s: [(slots[:, 2 + s], w[:, :, bass.ds(4 * P + n * P, P)])])
                sp.wait_ge(parts[0][0].done, 6 + 3 * 4)
                parts[2][0].load(sp, lambda n, s: [(slots[:, s], w[:, :, bass.ds(U_COL + n * P, P)])])

            @block.tensor
            def _(pe):
                for n, (st, _, _, slot) in enumerate(parts):
                    if n:
                        before = parts[n - 1][0]
                        pe.wait_ge(before.freed, before.sets + 3 * before.tiles)
                    st.multiply(pe, lambda b, s, c: [(ps[b][:, 0:C], [(slots[:, slot + s, k, :], hT[:, k, cols(c)]) for k in range(KD)])])

            @block.scalar
            def _(act):
                for st, dst, func, _ in parts:
                    st.take(act, lambda n, b, c: act.activation(dst[:, bass.ds(n, 1), cols(c)].rearrange("p a t -> p (a t)"),
                                                                ps[b][:, 0:C], func))


ROPED = (0, 1, 2, 3, 4, 6, 8)


def rope(nc, i, sem, sb, banks, qk):
    with ExitStack() as ctx:
        cos = sb(ctx, "cos", [P, T])
        sin = sb(ctx, "sin", [P, T])
        rot = sb(ctx, "rot", [P, P])
        t = sb(ctx, "rope_t", [P, 2, 2, C])
        ps = banks(ctx, 2)
        table_in, rotated, done, sin_done = sem("table_in"), sem("rotated"), sem("roped"), sem("rope_sin")
        cos_done = sem("rope_cos")
        units = [(tile, c) for tile in ROPED for c in range(CH)]
        with nc.Block() as block:
            @block.sync
            def _(sp):
                for dst, name in ((cos, "c_cos"), (sin, "c_sin"), (rot, "c_rot")):
                    sp.dma_start(dst[:], i[name]).then_inc(table_in, 16)

            @block.tensor
            def _(pe):
                pe.wait_ge(table_in, 48)
                for u, (tile, c) in enumerate(units):
                    if u >= 2:
                        pe.wait_ge(sin_done, u - 1)
                    pe.matmul(ps[u % 2][:, 0:C], rot[:], qk[:, tile, cols(c)], start=True, stop=True).then_inc(rotated, 1)

            @block.gpsimd
            def _(pool):
                pool.wait_ge(table_in, 48)
                for u, (tile, c) in enumerate(units):
                    if u >= 2:
                        pool.wait_ge(done, u - 1)
                    pool.tensor_tensor(t[:, u % 2, 1], qk[:, tile, cols(c)], cos[:, cols(c)], ALU.mult).then_inc(cos_done, 1)

            @block.vector
            def _(dve):
                dve.wait_ge(table_in, 48)
                for u, (tile, c) in enumerate(units):
                    dve.wait_ge(rotated, u + 1)
                    dve.tensor_tensor(t[:, u % 2, 0], ps[u % 2][:, 0:C], sin[:, cols(c)], ALU.mult).then_inc(sin_done, 1)
                    dve.wait_ge(sin_done, u + 1)
                    dve.wait_ge(cos_done, u + 1)
                    dve.tensor_tensor(qk[:, tile, cols(c)], t[:, u % 2, 0], t[:, u % 2, 1], ALU.add).then_inc(done, 1)
                for g in range(4):
                    dve.wait_ge(done, 3 * g + 3)
                    dve.tensor_scalar(qk[:, g, :], qk[:, g, :], HD ** -0.5, None, ALU.mult)


def rows_and_gmlp(nc, i, o, sem, sb, banks, hT, qk, uv, vtok, gates, ident):
    with ExitStack() as ctx:
        w_gn = sb(ctx, "w_gn", [P, KD, 24])
        ws = sb(ctx, "ws", [P, 8, P])
        wsT = sb(ctx, "wsT", [P, 8, P])
        wlane = sb(ctx, "wlane", [TS, 8, TS])
        tril = sb(ctx, "tril", [P, P])
        lane = sb(ctx, "lane", [TS, 8, TS])
        bias = sb(ctx, "bias", [P, 4, P])
        ln_g = sb(ctx, "ln_g", [P, 512])
        ln_b = sb(ctx, "ln_b", [P, 512])
        kv = sb(ctx, "kv", [P, 2, 6, P])
        gv = sb(ctx, "gv", [TS, 512])
        vn = sb(ctx, "vn", [P, 2, 512])
        sp_t = sb(ctx, "sp_t", [P, 2, 4, P])
        stat = sb(ctx, "stat", [P, 2, 6])
        mom = sb(ctx, "mom", [P, 2, 2])
        dev = sb(ctx, "dev", [P, 2, 2])
        ps = banks(ctx, 8)
        loaded, lane0, lane_in, ws_turned, ws_kept = sem("gm_loaded"), sem("lane0"), sem("lane_in"), sem("ws_turned"), sem("ws_kept")
        a_full, b_full, v_full, s_full = (sem(f"rw_{x}_full") for x in "abvs")
        copied, v_kept, v_rooted, var_ready, chain, vn_ready, s_used = (
            sem(f"rw_{x}") for x in ("copied", "v_kept", "rooted", "var", "chain", "vn", "s_used"))
        gates_done, gv_copied, gv_out = sem("gates_done"), sem("gv_copied"), sem("gv_out")
        kv_out = [sem(f"kv_out{s}") for s in range(2)]
        win_out = sem("win_out")
        stored = [0, 0]
        after = []
        for t in range(NT + 1):
            stored[t % 2] += 6 if t >= 4 else 4
            after.append(stored[t % 2])

        def rows(t):
            return P if t < NT else TS

        def at(t):
            return slice(t * P, t * P + rows(t))

        with nc.Block() as block:
            @block.sync
            def _(sp):
                w = i["w_in"][0].rearrange("(k p) n -> p k n", p=P)
                sp.dma_start(ws[:], i["gmlp_ws"][0].rearrange("g i j -> i g j")).then_inc(loaded, 16)
                sp.dma_start(w_gn[:], w[:, :, GN_COL:GN_COL + 24]).then_inc(loaded, 16)
                sp.dma_start(tril[:], i["c_tril"]).then_inc(loaded, 16)
                sp.dma_start(lane[:], i["c_lane"]).then_inc(loaded, 16)
                bs = i["gmlp_bs"][0].rearrange("(t a) i -> a t i", a=2)
                for a in range(2):
                    sp.dma_start(bias[HD * a:HD * a + HD], bs[a].partition_broadcast(HD)).then_inc(loaded, 16)
                sp.dma_start(ln_g[:], i["gmlp_ln_g"][0].partition_broadcast(P)).then_inc(loaded, 16)
                sp.dma_start(ln_b[:], i["gmlp_ln_b"][0].partition_broadcast(P)).then_inc(loaded, 16)
                sp.wait_ge(lane0, 1)
                for b in range(NB):
                    for g in range(8):
                        sp.dma_start(wlane[NS * b:NS * b + NS, g, NS * b:NS * b + NS],
                                     i["gmlp_ws"][0, g, 0:NS, 0:NS].rearrange("i j -> j i")).then_inc(lane_in, 16)

            @block.gpsimd
            def _(pool):
                pool.memset(wlane[:], 0.0).then_inc(lane0, 1)
                for name, state in (("new_win_k_s", "state_win_k"), ("new_win_v_s", "state_win_v")):
                    pool.dma_start(o[name][0, :, 0:WIN - NS].rearrange("b t h d -> b (t h d)"),
                                   i[state][0, :, NS:WIN].rearrange("b t h d -> b (t h d)")).then_inc(win_out, 16)
                for t in range(NT + 1):
                    pool.wait_ge(copied, 2 * t + 2)
                    s = t % 2
                    flat = "t h d -> t (h d)"
                    for n, name in enumerate(("cmp_k", "cmp_v", "slc_k", "slc_v", "win_k", "win_v")):
                        if t < NT:
                            if n >= 4 and t < 4:
                                continue
                            dst = o[f"new_{name}_p"][0, 0].rearrange(flat)
                            r0 = t * P - (WIN if n >= 4 else 0)
                            dst = dst[r0:r0 + P]
                        elif n < 4:
                            dst = o[f"new_{name}_s"][0].rearrange("b s h d -> (b s) (h d)")
                        else:
                            dst = o[f"new_{name}_s"][0, :, WIN - NS:WIN].rearrange("b s h d -> b s (h d)")
                        pool.dma_start(dst, kv[0:rows(t), s, n]).then_inc(kv_out[s], 16)
                pool.wait_ge(gv_copied, 1)
                pool.dma_start(o["new_gmlp_v_s"][0].rearrange("b s c -> (b s) c"), gv[:]).then_inc(gv_out, 16)
                pool.wait_ge(gv_out, 16)
                pool.wait_ge(win_out, 32)
                for s in range(2):
                    pool.wait_ge(kv_out[s], 16 * stored[s])

            @block.tensor
            def _(pe):
                pe.wait_ge(loaded, 16 * 8)
                for h in range(2):
                    for g in range(4):
                        last = pe.transpose(ps[6 + h][:, g * P:(g + 1) * P], ws[:, 4 * h + g, :], ident[:])
                    last.then_inc(ws_turned, 1)

                def turn(t):
                    if t >= 2:
                        pe.wait_ge(copied, 2 * t - 2)
                        pe.wait_ge(v_kept, t - 1)
                        pe.wait_ge(gates_done, t - 1)
                    r = rows(t)
                    a, b, v = ps[t % 2], ps[2 + t % 2], ps[4 + t % 2]
                    for n in range(4):
                        last = pe.transpose(a[0:r, n * P:(n + 1) * P], qk[:, 4 + n, at(t)], ident[:])
                    last.then_inc(a_full, 1)
                    for n in range(2):
                        pe.transpose(b[0:r, n * P:(n + 1) * P], qk[:, 8 + n, at(t)], ident[:])
                    for k in range(KD):
                        last = pe.matmul(b[0:r, 256:280], hT[:, k, at(t)], w_gn[:, k, :], start=k == 0, stop=k == KD - 1)
                    last.then_inc(b_full, 1)
                    for n in range(4):
                        last = pe.transpose(v[0:r, n * P:(n + 1) * P], uv[:, 4 + n, at(t)], ident[:])
                    last.then_inc(v_full, 1)

                turn(0)
                for t in range(NT + 1):
                    if t < NT:
                        turn(t + 1)
                    pe.wait_ge(vn_ready, t + 1)
                    pe.wait_ge(ws_kept, 2)
                    if t >= 2:
                        pe.wait_ge(s_used, t - 1)
                    if t == NT:
                        pe.wait_ge(lane_in, 16 * 64)
                        pe.wait_ge(ws_kept, 3)
                    r = rows(t)
                    for g in range(8):
                        w = wsT[:, g, :] if t < NT else wlane[:, g, :]
                        a = HD * (g % 2)
                        last = pe.matmul(ps[6 + t % 2][a:a + HD, (g // 2) * P:(g // 2) * P + r], vn[0:r, t % 2, g * HD:(g + 1) * HD], w,
                                         start=True, stop=True, skip_group_check=True)
                    last.then_inc(s_full, 1)

            @block.scalar
            def _(act):
                for t in range(NT + 1):
                    r, s = rows(t), t % 2
                    if t >= 2:
                        act.wait_ge(kv_out[s], 16 * after[t - 2])
                    act.wait_ge(a_full, t + 1)
                    act.copy(kv[0:r, s, 0:4].rearrange("p a c -> p (a c)"), ps[s][0:r, :]).then_inc(copied, 1)
                    act.wait_ge(b_full, t + 1)
                    act.copy(kv[0:r, s, 4:6].rearrange("p a c -> p (a c)"), ps[2 + s][0:r, 0:256]).then_inc(copied, 1)
                    act.activation(gates[0:r, t, :], ps[2 + s][0:r, 256:280], ACT.Sigmoid).then_inc(gates_done, 1)
                    act.wait_ge(var_ready, t + 1)
                    act.sqrt(dev[0:r, s, 0:1], dev[0:r, s, 0:1]).then_inc(v_rooted, 1)

            @block.vector
            def _(dve):
                ch = Chain(dve, chain)
                for h in range(2):
                    dve.wait_ge(ws_turned, h + 1)
                    dve.tensor_tensor(wsT[:, 4 * h:4 * h + 4, :], ps[6 + h][:].rearrange("p (g c) -> p g c", g=4),
                                      tril[:].unsqueeze(1).to_broadcast([P, 4, P]), ALU.mult).then_inc(ws_kept, 1)
                dve.wait_ge(lane_in, 16 * 64)
                dve.tensor_tensor(wlane[:], wlane[:], lane[:], ALU.mult).then_inc(ws_kept, 1)

                def layer_norm(t):
                    r, s = rows(t), t % 2
                    v = ps[4 + s][0:r, :]
                    dve.wait_ge(v_full, t + 1)
                    ch(dve.bn_stats(stat[0:r, s], v))
                    ch(dve.bn_aggr(mom[0:r, s], stat[0:r, s]))
                    dve.tensor_scalar(dev[0:r, s, 0:1], mom[0:r, s, 1:2], EPS, None, ALU.add).then_inc(var_ready, 1)
                    if t < NT:
                        dve.wait_ge(copied, 2 * t + 2)
                        dve.tensor_copy(vtok[:, t], kv[:, s, 3:6:2])
                    else:
                        dve.tensor_copy(gv[:], v).then_inc(gv_copied, 1)
                    dve.wait_ge(v_rooted, t + 1)
                    ch(dve.reciprocal(dev[0:r, s, 1:2], dev[0:r, s, 0:1]))
                    if t >= 2:
                        dve.wait_ge(s_full, t - 1)
                    dve.tensor_scalar(vn[0:r, s], v, mom[0:r, s, 0:1], dev[0:r, s, 1:2], ALU.subtract, ALU.mult).then_inc(v_kept, 1)
                    dve.wait_ge(v_kept, t + 1)
                    ch(dve.tensor_tensor(vn[0:r, s], vn[0:r, s], ln_g[0:r], ALU.mult))
                    dve.tensor_tensor(vn[0:r, s], vn[0:r, s], ln_b[0:r], ALU.add).then_inc(vn_ready, 1)

                def spatial(t):
                    r, s = rows(t), t % 2
                    dve.wait_ge(s_full, t + 1)
                    y = ps[6 + s][:].rearrange("p (a c) -> p a c", a=4)
                    if t < NT:
                        dve.tensor_tensor(sp_t[:, s], y, bias[:], ALU.add).then_inc(s_used, 1)
                    else:
                        dve.tensor_tensor(sp_t[:, s, :, 0:TS].rearrange("p a (b i) -> p a b i", b=NB),
                                          y[:, :, 0:TS].rearrange("p a (b i) -> p a b i", b=NB),
                                          bias[:, :, 0:NS].unsqueeze(2).to_broadcast([P, 4, NB, NS]), ALU.add).then_inc(s_used, 1)
                    dve.wait_ge(s_used, t + 1)
                    dve.tensor_tensor(uv[:, 0:4, at(t)], sp_t[:, s, :, 0:r], uv[:, 0:4, at(t)], ALU.mult)

                dve.wait_ge(loaded, 16 * 8)
                layer_norm(0)
                for t in range(NT + 1):
                    if t < NT:
                        layer_norm(t + 1)
                    spatial(t)


def compress(nc, i, o, sem, sb, banks, uv, ck, cv, ident):
    with ExitStack() as ctx:
        w1 = uv[:, 4:8, :].rearrange("p a t -> p (a t)")[:, 0:2 * 16 * P].rearrange("p (k j f) -> p k j f", k=2, j=16)
        w2 = sb(ctx, "w2", [P, 2, HD])
        pe_in = sb(ctx, "pe_in", [P, 2, 16])
        pe_sum = sb(ctx, "pe_sum", [P, 2])
        table = sb(ctx, "table", [1, NB * PAGES], I32)
        page = sb(ctx, "page", [P, 2, 4, 2 * P])
        pairs = sb(ctx, "pairs", [P, 2, SRC, PAIRS])
        hid = sb(ctx, "hid", [P, 2, SRC * CMP])
        ps = banks(ctx, 8)
        loaded, table_in, chain = sem("cmp_loaded"), sem("cmp_table"), sem("cmp_chain")
        page_in = [[[sem(f"page_in{k}{s}{q}") for q in range(2)] for s in range(2)] for k in range(2)]
        turned = [sem(f"pair_turned{k}") for k in range(2)]
        kept = [[sem(f"pair_kept{k}{h}") for h in range(2)] for k in range(2)]
        summed, bias_sum, bias_kept, gelu_done, out_done = (sem(f"cmp_{x}") for x in ("summed", "bsum", "bias", "gelu", "out"))
        rest_kept = sem("cmp_rest")
        halves = [(0, 5), (5, SRC)]
        pools = ("cache_cmp_k", "cache_cmp_v")

        def gather(eng, q):
            eng.wait_ge(table_in, 16)
            for k in range(2):
                rows = i[pools[k]][0].rearrange("g (p a) h d -> g p (a h d)", a=2)
                with eng.Fori(0, NB // 2) as it:
                    for s in range(2):
                        eng.wait_ge(turned[k], 4 * it + 2 * s + 2)
                        if k == 1:
                            eng.wait_ge(turned[0], 4 + 2 * SRC)
                        for j in range(q, PAGES, 2):
                            at = eng.value_load(table[0:1, bass.ds((2 * it + s) * PAGES + j, 1)], min_val=0, max_val=N_POOL - 1)
                            eng.dma_start(page[HD * q:HD * q + HD, s, j // 2],
                                          rows[bass.ds(at, 1)].rearrange("g p c -> (g p) c")).then_inc(page_in[k][s][q], 16)
                if q == 0:
                    eng.wait_ge(turned[k], 2 * NB + 2)
                    own = o[("new_cmp_k_p", "new_cmp_v_p")[k]][0, 0].rearrange("(j p a) h d -> p j (a h d)", a=2, p=P)
                    eng.dma_start(page[:, 0], own).then_inc(page_in[k][0][0], 16)

        with nc.Block() as block:
            @block.sync
            def _(sp):
                sp.dma_start(table[:], i["page_table"].rearrange("(o b) j -> o (b j)", o=1)).then_inc(table_in, 16)
                for k in range(2):
                    sp.dma_start(w1[:, k], i["cmp_w1"][0, k].rearrange("(j a) d f -> (a d) j f", a=2)).then_inc(loaded, 16)
                    sp.dma_start(pe_in[:, k], i["cmp_pe"][0, k].rearrange("(j a) d -> (a d) j", a=2)).then_inc(loaded, 16)
                sp.dma_start(w2[:], i["cmp_w2"][0].rearrange("k f d -> f k d")).then_inc(loaded, 16)
                gather(sp, 0)

            @block.gpsimd
            def _(pool):
                gather(pool, 1)

            @block.tensor
            def _(pe):
                def turn(k, s):
                    for a in range(2):
                        for j in range(4):
                            last = pe.transpose(ps[2 * a + s][:, j * P:(j + 1) * P], page[:, s, j, P * a:P * a + P], ident[:])
                        last.then_inc(turned[k], 1)

                for k in range(2):
                    pe.sem_inc(turned[k], 4)
                    with pe.Fori(0, NB // 2) as it:
                        for s in range(2):
                            for q in range(2):
                                pe.wait_ge(page_in[k][s][q], 8 * PAGES * it + 8 * PAGES)
                            pe.wait_ge(kept[k][0], 2 * it + s + 1)
                            pe.wait_ge(kept[k][1], 2 * it + s + 1)
                            turn(k, s)
                    pe.wait_ge(page_in[k][0][0], 8 * PAGES * 4 + 16)
                    pe.wait_ge(kept[k][0], NB + 1)
                    pe.wait_ge(kept[k][1], NB + 1)
                    turn(k, 0)
                    pe.wait_ge(kept[k][0], SRC + 2)
                    pe.wait_ge(kept[k][1], SRC + 2)
                    if k == 0:
                        pe.wait_ge(loaded, 16 * 5)
                        for kk in range(2):
                            for j in range(16):
                                last = pe.matmul(ps[4][:, kk:kk + 1], w1[:, kk, j], pe_in[:, kk, j:j + 1], start=j == 0, stop=j == 15)
                        last.then_inc(bias_sum, 1)
                        pe.wait_ge(bias_kept, 1)
                    for h in range(2):
                        for n, (b0, b1) in enumerate(halves):
                            if k == 1:
                                pe.wait_ge(gelu_done, 2 * h + n + 1)
                            for j in range(16):
                                last = pe.matmul(ps[4 + 2 * h + n][:, 0:(b1 - b0) * CMP], w1[:, k, j],
                                                 pairs[:, h, b0:b1, j:j + 8 * (CMP - 1) + 1:8], start=j == 0, stop=j == 15)
                            last.then_inc(summed, 1)
                    pe.wait_ge(gelu_done, 4 * k + 4)
                    if k == 0:
                        for h in range(2):
                            for n, (b0, b1) in enumerate(halves):
                                last = pe.matmul(ps[n][HD * h:HD * h + HD, 0:(b1 - b0) * CMP], w2[:, 0], hid[:, h, b0 * CMP:b1 * CMP],
                                                 start=True, stop=True, skip_group_check=True)
                        last.then_inc(out_done, 1)
                        pe.wait_ge(rest_kept, 2)
                    else:
                        for b in range(SRC):
                            for h in range(2):
                                at = P * (b % 4) + HD * h
                                last = pe.matmul(ps[b // 4][0:CMP, at:at + HD], hid[:, h, b * CMP:(b + 1) * CMP], w2[:, 1],
                                                 start=True, stop=True, skip_group_check=True)
                        last.then_inc(out_done, 1)

            def keep(eng, h, copy):
                for k in range(2):
                    eng.sem_inc(kept[k][h], 2)
                    with eng.Fori(0, NB // 2) as it:
                        for s in range(2):
                            eng.wait_ge(turned[k], 4 * it + 2 * s + h + 5)
                            for hh in range(2):
                                last = copy(pairs[HD * h:HD * h + HD, hh, bass.ds(2 * it + s, 1), :].rearrange("p a t -> p (a t)"),
                                            ps[2 * h + s][HD * hh:HD * hh + HD, :])
                            last.then_inc(kept[k][h], 1)
                    eng.wait_ge(turned[k], 2 * NB + h + 5)
                    for hh in range(2):
                        last = copy(pairs[HD * h:HD * h + HD, hh, NB, :], ps[2 * h][HD * hh:HD * hh + HD, :])
                    last.then_inc(kept[k][h], 1)
                    if h == 0:
                        if k == 0:
                            eng.wait_ge(bias_kept, 1)
                        for hh in range(2):
                            for n, (b0, b1) in enumerate(halves):
                                eng.wait_ge(summed, 4 * k + 2 * hh + n + 1)
                                if k == 1 and hh == 0 and n == 0:
                                    eng.wait_ge(out_done, 1)
                                eng.activation(hid[:, hh, b0 * CMP:b1 * CMP], ps[4 + 2 * hh + n][:, 0:(b1 - b0) * CMP],
                                               ACT.Gelu_apprx_tanh, bias=pe_sum[:, k:k + 1]).then_inc(gelu_done, 1)
                    elif k == 0:
                        eng.wait_ge(bias_sum, 1)
                        eng.tensor_copy(pe_sum[:], ps[4][:, 0:2]).then_inc(bias_kept, 1)
                        eng.wait_ge(out_done, 1)
                        for n, (b0, b1) in enumerate(halves):
                            eng.tensor_copy(ck[:, b0:b1, :].rearrange("p b n -> p (b n)"), ps[n][:, 0:(b1 - b0) * CMP]).then_inc(rest_kept, 1)

            @block.scalar
            def _(act):
                keep(act, 0, act.copy)

            @block.vector
            def _(dve):
                keep(dve, 1, dve.tensor_copy)
                dve.wait_ge(out_done, 2)
                for n in range(3):
                    b0, b1 = 4 * n, min(4 * n + 4, SRC)
                    dve.tensor_copy(cv[:, b0:b1, :].rearrange("p b c -> p (b c)"), ps[n][0:CMP, 0:(b1 - b0) * P])


def attend_prompt(nc, i, sem, sb, banks, qk, vtok, gates, ck, cv, oT, ident):
    with ExitStack() as ctx:
        diag = sb(ctx, "diag", [P, P])
        far = sb(ctx, "far", [P, P])
        seen = sb(ctx, "seen", [P, NT, CMP])
        hidden = sb(ctx, "hidden", [P, NT, CMP])
        cs = sb(ctx, "cs", [P, 8, CMP])
        probs = sb(ctx, "probs", [P, 2, NP])
        turned = sb(ctx, "turned", [P, 2, 8, P])
        rows = sb(ctx, "rows", [P, 2, 512])
        mx = sb(ctx, "mx", [P, 4])
        cmx = sb(ctx, "cmx", [P, 8])
        total = sb(ctx, "total", [P, 4])
        ctotal = sb(ctx, "ctotal", [P, 8])
        factor = sb(ctx, "factor", [P, 2])
        ps = banks(ctx, 4)
        wide = [ctx.enter_context(nc.psum_tensor(f"scores{k}", [P, 1024], F32)) for k in range(2)]
        loaded = sem("mask_in")
        score, peak, expd, shown, pt, combined = (sem(f"at_{x}") for x in ("score", "peak", "exp", "shown", "pt", "combined"))
        pt_free = [sem(f"at_pt_free{k}") for k in range(2)]
        pv, chain, out_turned, out_kept = sem("at_pv"), sem("at_chain"), sem("at_out_turned"), sem("at_out_kept")
        units = [(t, None, None, "cmp") if n < 0 else (t, n // 4, n // 2 % 2, ("sel", "win")[n % 2])
                 for t in range(NT) for n in range(-1, 16)]

        def blocks(u):
            t, _, _, kind = units[u]
            return 8 if kind == "cmp" else t + 1 if kind == "sel" else min(t + 1, 5)

        first_group, n_groups = [], 0
        out_group = {}
        for u in range(len(units)):
            first_group.append(n_groups)
            n_groups += -(-blocks(u) // 4)
            if units[u][3] == "cmp" and units[u][0] > 0:
                out_group[units[u][0] - 1] = n_groups
                n_groups += 1
        out_group[NT - 1] = n_groups
        cmp_units = [u for u in range(len(units)) if units[u][3] == "cmp"]

        def group_list(u):
            return [(first_group[u] + j, 4 * j, min(4 * j + 4, blocks(u))) for j in range(-(-blocks(u) // 4))]

        with nc.Block() as block:
            @block.sync
            def _(sp):
                for dst, name in ((diag, "c_diag"), (far, "c_far"), (seen, "c_seen"), (hidden, "c_hidden")):
                    sp.dma_start(dst[:], i[name]).then_inc(loaded, 16)

            @block.tensor
            def _(pe):
                def scores(u):
                    t, g, h, kind = units[u]
                    s = wide[u % 2]
                    if u >= 2:
                        pe.wait_ge(expd, u - 1)
                    qt = slice(t * P, t * P + P)
                    if kind == "cmp":
                        for n in range(8):
                            gg, hh = n // 2, n % 2
                            at = slice(HD * hh, HD * hh + HD)
                            to = 512 * hh + gg * CMP
                            last = pe.matmul(s[:, to:to + CMP], qk[at, gg, qt], ck[at, NB, :], start=True, stop=True,
                                             skip_group_check=True)
                    else:
                        at = slice(HD * h, HD * h + HD)
                        tile = 6 if kind == "sel" else 8
                        k0 = 0 if kind == "sel" else max(t - 4, 0) * P
                        n = blocks(u) * P
                        for c in range(0, n, 512):
                            w = min(512, n - c)
                            last = pe.matmul(s[:, c:c + w], qk[at, g, qt], qk[at, tile, k0 + c:k0 + c + w], start=True, stop=True)
                    last.then_inc(score, 1)

                def turn_and_sum(u):
                    t, g, h, kind = units[u]
                    if kind == "cmp":
                        pe.wait_ge(shown, t + 1)
                    else:
                        pe.wait_ge(expd, u + 1)
                    for n, b0, b1 in group_list(u):
                        if n >= 2:
                            pe.wait_ge(pt_free[n % 2], n // 2)
                        for b in range(b0, b1):
                            if kind == "cmp":
                                last = pe.transpose(ps[n % 2][0:CMP, (b - b0) * P:(b - b0 + 1) * P], probs[:, u % 2, b * CMP:(b + 1) * CMP], ident[:])
                            else:
                                last = pe.transpose(ps[n % 2][:, (b - b0) * P:(b - b0 + 1) * P], probs[:, u % 2, b * P:(b + 1) * P], ident[:])
                        last.then_inc(pt, 1)
                    if u >= 2:
                        pe.wait_ge(combined, u - 1)
                    out = ps[2 + u % 2]
                    for n, b0, b1 in group_list(u):
                        pe.wait_ge(pt_free[n % 2], n // 2 + 1)
                        for b in range(b0, b1):
                            if kind == "cmp":
                                gg, hh = b // 2, b % 2
                                last = pe.matmul(out[:, b * HD:(b + 1) * HD], turned[0:CMP, u % 2, b], cv[:, NB, HD * hh:HD * hh + HD],
                                                 start=True, stop=True, skip_group_check=True)
                            else:
                                k0 = 0 if kind == "sel" else max(t - 4, 0)
                                last = pe.matmul(out[:, 0:HD], turned[:, u % 2, b], vtok[:, k0 + b, kind == "win", HD * h:HD * h + HD],
                                                 start=b == 0, stop=b == blocks(u) - 1)
                    last.then_inc(pv, 1)

                def turn_rows(t):
                    n = out_group[t]
                    pe.wait_ge(combined, 17 * t + 17)
                    pe.wait_ge(pt_free[n % 2], n // 2)
                    for g in range(4):
                        last = pe.transpose(ps[n % 2][:, g * P:(g + 1) * P], rows[:, t % 2, g * P:(g + 1) * P], ident[:])
                    last.then_inc(pt, 1)

                pe.wait_ge(loaded, 64)
                scores(0)
                for u in range(len(units)):
                    if u + 1 < len(units):
                        scores(u + 1)
                    turn_and_sum(u)
                    if units[u][3] == "cmp" and units[u][0] > 0:
                        turn_rows(units[u][0] - 1)
                turn_rows(NT - 1)

            def empty(eng, copy, which, u):
                for n, b0, b1 in group_list(u):
                    if n % 2 == which:
                        r = CMP if units[u][3] == "cmp" else P
                        eng.wait_ge(pt, n + 1)
                        copy(turned[0:r, u % 2, b0:b1, :].rearrange("p b c -> p (b c)"), ps[n % 2][0:r, 0:(b1 - b0) * P]).then_inc(pt_free[which], 1)
                if units[u][3] == "cmp" and units[u][0] > 0:
                    empty_rows(eng, copy, which, units[u][0] - 1)

            def empty_rows(eng, copy, which, t):
                n = out_group[t]
                if n % 2 == which:
                    eng.wait_ge(pt, n + 1)
                    copy(oT[:, :, t * P:(t + 1) * P], ps[n % 2][:].rearrange("p (g c) -> p g c", g=4)).then_inc(pt_free[which], 1)

            @block.scalar
            def _(act):
                def exp(u):
                    act.wait_ge(peak, u + 1)
                    if u >= 2:
                        act.wait_ge(pv, u - 1)
                    if units[u][3] == "cmp":
                        act.activation(probs[:, u % 2, 0:8 * CMP], cs[:].rearrange("p h n -> p (h n)"), ACT.Exp).then_inc(expd, 1)
                    else:
                        n = blocks(u) * P
                        act.activation(probs[:, u % 2, 0:n], wide[u % 2][:, 0:n], ACT.Exp, bias=mx[:, u % 4:u % 4 + 1],
                                       accum_out=total[:, u % 4:u % 4 + 1]).then_inc(expd, 1)

                exp(0)
                for u in range(len(units)):
                    empty(act, act.copy, 1, u)
                    if u + 1 < len(units):
                        exp(u + 1)
                empty_rows(act, act.copy, 1, NT - 1)

            @block.vector
            def _(dve):
                ch = Chain(dve, chain)

                def peaks(u):
                    t, _, _, kind = units[u]
                    s = wide[u % 2]
                    dve.wait_ge(score, u + 1)
                    if kind == "cmp":
                        by_head = cs[:].rearrange("p (g h) n -> p h g n", h=2)
                        for h in range(2):
                            last = dve.tensor_tensor(by_head[:, h], s[:, 512 * h:512 * h + 4 * CMP].rearrange("p (g n) -> p g n", g=4),
                                                     hidden[:, t].unsqueeze(1).to_broadcast([P, 4, CMP]), ALU.add)
                        ch(last)
                        ch(dve.tensor_reduce(cmx[:], cs[:], X, ALU.max))
                        dve.tensor_tensor(cs[:], cs[:], cmx[:].unsqueeze(2).to_broadcast([P, 8, CMP]), ALU.subtract).then_inc(peak, 1)
                        return
                    n = blocks(u) * P
                    ch(dve.tensor_tensor(s[:, n - P:n], s[:, n - P:n], diag[:], ALU.add))
                    if kind == "win" and t >= 4:
                        ch(dve.tensor_tensor(s[:, 0:P], s[:, 0:P], far[:], ALU.add))
                    dve.tensor_reduce(mx[:, u % 4:u % 4 + 1], s[:, 0:n], X, ALU.max, negate=True).then_inc(peak, 1)

                def show(u):
                    t = units[u][0]
                    p = probs[:, u % 2, 0:8 * CMP].rearrange("p (h n) -> p h n", h=8)
                    dve.wait_ge(expd, u + 1)
                    dve.tensor_tensor(p, p, seen[:, t].unsqueeze(1).to_broadcast([P, 8, CMP]), ALU.mult).then_inc(shown, 1)
                    dve.wait_ge(shown, t + 1)
                    ch(dve.tensor_reduce(ctotal[:], p, X, ALU.add))
                    ch(dve.tensor_scalar(ctotal[:], ctotal[:], 1e-30, None, ALU.max))
                    ch(dve.reciprocal(ctotal[:], ctotal[:]))
                    gate = gates[:, t, :].rearrange("p (h g j) -> p g h j", h=2, g=4)[:, :, :, 0]
                    ch(dve.tensor_tensor(ctotal[:].rearrange("p (g h) -> p g h", g=4), ctotal[:].rearrange("p (g h) -> p g h", g=4), gate, ALU.mult))

                def combine(u):
                    t, g, h, kind = units[u]
                    out = ps[2 + u % 2]
                    if kind == "cmp":
                        dve.wait_ge(pv, u + 1)
                        if t >= 2:
                            dve.wait_ge(pt, out_group[t - 2] + 1)
                        dve.tensor_tensor(rows[:, t % 2].rearrange("p (h d) -> p h d", h=8), out[:].rearrange("p (h d) -> p h d", h=8),
                                          ctotal[:].unsqueeze(2).to_broadcast([P, 8, HD]), ALU.mult).then_inc(combined, 1)
                        return
                    j = 3 * (4 * h + g) + (1 if kind == "sel" else 2)
                    dve.wait_ge(expd, u + 1)
                    ch(dve.reciprocal(factor[:, 0:1], total[:, u % 4:u % 4 + 1]))
                    ch(dve.tensor_tensor(factor[:, 1:2], factor[:, 0:1], gates[:, t, j:j + 1], ALU.mult))
                    dve.wait_ge(pv, u + 1)
                    dve.wait_ge(combined, u)
                    r = rows[:, t % 2, (2 * g + h) * HD:(2 * g + h + 1) * HD]
                    dve.scalar_tensor_tensor(r, out[:, 0:HD], factor[:, 1:2], r, ALU.mult, ALU.add).then_inc(combined, 1)

                dve.wait_ge(loaded, 64)
                peaks(0)
                for u in range(len(units)):
                    if units[u][3] == "cmp":
                        show(u)
                    empty(dve, dve.tensor_copy, 0, u)
                    if u + 1 < len(units):
                        peaks(u + 1)
                    combine(u)
                empty_rows(dve, dve.tensor_copy, 0, NT - 1)


def attend_sample(nc, i, o, sem, sb, banks, qk, uv, gates, ck, cv, oT, ident):
    SEL, WINC = 0, 1532
    CMPC, ROWG, SC0, SC1 = 0, 64, 96, 112
    PS_, PW, PC = 0, 1028, 1544
    with ExitStack() as ctx:
        ring = uv[:, 4:8, :].rearrange("p a t -> p (a t)")[:, 0:2 * 12 * P].rearrange("p (s j c) -> p s j c", s=2, j=12)
        probs = qk[:, 4:6, :].rearrange("p a t -> p (a t)")
        table = sb(ctx, "table_s", [1, NB * PAGES], I32)
        kT = sb(ctx, "kT", [P, 2, 12 * P])
        pT = sb(ctx, "pT", [P, 16, P])
        q_rows = sb(ctx, "q_rows", [P, NB, 32])
        v_new = sb(ctx, "v_new", [NS, 2, NB, P])
        same = sb(ctx, "same", [P, P])
        shared = sb(ctx, "shared", [CMP, 16])
        new = sb(ctx, "new", [P, NS])
        old = sb(ctx, "old", [P, NS])
        row_of = sb(ctx, "row_of", [TS, 2, P])
        hg = sb(ctx, "hg", [P, 24])
        block_no = sb(ctx, "block_no", [P, 16])
        small = sb(ctx, "small", [P, 8, 24])
        one = sb(ctx, "one", [P, 12])
        wide = ctx.enter_context(nc.psum_tensor("s_wide", [P, 2048], F32))
        tp = banks(ctx, 2)
        out, misc = banks(ctx, 2)
        loaded, table_in, zeroed, q_ready = sem("sa_loaded"), sem("sa_table"), sem("sa_zeroed"), sem("sa_q")
        ring_in = [[sem(f"sa_ring{s}{q}") for q in range(2)] for s in range(2)]
        turned, score, pv = (sem(f"sa_{x}") for x in ("turned", "score", "pv"))
        kept = [sem(f"sa_kept{k}") for k in range(2)]
        chain, ready, expd, cmp_p, probs_ready, summed, small_mm = (sem(f"sa_{x}") for x in ("chain", "ready", "exp", "cmp_p", "probs", "summed", "mm"))
        small_kept = sem("sa_small_kept")
        per = 12 + 1 + 4

        def gather(eng, q):
            eng.wait_ge(table_in, 16)
            for grp in range(2):
                for v, (pool, state) in enumerate((("cache_slc_k", "state_win_k"), ("cache_slc_v", "state_win_v"))):
                    pages = i[pool][0].rearrange("g p h d -> g p (h d)")
                    for bb in range(4):
                        b, s = 4 * grp + bb, bb % 2
                        if bb >= 2 and v == 0:
                            eng.wait_ge(turned, per * grp + 3 * bb - 3)
                        elif bb >= 2:
                            eng.wait_ge(pv, b - 1)
                        elif v == 1:
                            eng.wait_ge(turned, per * grp + 3 * bb + 9)
                        elif grp > 0:
                            eng.wait_ge(pv, b - 1)
                        with eng.Fori(0, PAGES // 2) as j:
                            at = eng.value_load(table[0:1, bass.ds(2 * j + (b * PAGES + q), 1)], min_val=0, max_val=N_POOL - 1)
                            eng.dma_start(ring[:, s, bass.ds(2 * j + q, 1)].rearrange("p j c -> p (j c)"),
                                          pages[bass.ds(at, 1)].rearrange("g p c -> (g p) c")).then_inc(ring_in[s][q], 16)
                        eng.dma_start(ring[:, s, 8 + 2 * q:10 + 2 * q],
                                      i[state][0, b, 2 * P * q:2 * P * q + 2 * P].rearrange("(j p) h d -> p j (h d)", p=P)).then_inc(ring_in[s][q], 16)

        with nc.Block() as block:
            @block.sync
            def _(sp):
                sp.dma_start(table[:], i["page_table"].rearrange("(o b) j -> o (b j)", o=1)).then_inc(table_in, 16)
                for dst, name in ((same, "c_same"), (shared, "c_shared"), (new, "c_new"), (old, "c_old"), (row_of, "c_row_of"),
                                  (hg, "c_hg"), (block_no, "c_block")):
                    src = i[name].rearrange("p x j -> p (x j)") if name == "c_hg" else i[name]
                    sp.dma_start(dst[:], src).then_inc(loaded, 16)
                sp.dma_start(v_new[:, 0], o["new_slc_v_s"][0].rearrange("b s h d -> s b (h d)")).then_inc(loaded, 16)
                sp.dma_start(v_new[:, 1], o["new_win_v_s"][0, :, WIN - NS:WIN].rearrange("b s h d -> s b (h d)")).then_inc(loaded, 16)
                gather(sp, 0)

            @block.gpsimd
            def _(pool):
                pool.memset(q_rows[:], 0.0).then_inc(zeroed, 1)
                gather(pool, 1)

            def arrived(pe, load):
                for q in range(2):
                    pe.wait_ge(ring_in[load % 2][q], 16 * 5 * (load // 2 + 1))

            @block.tensor
            def _(pe):
                pe.wait_ge(loaded, 16 * 9)
                pe.wait_ge(q_ready, 2)

                def room(n):
                    if n >= 2:
                        pe.wait_ge(kept[n % 2], n // 2)

                def turn_keys(b):
                    grp, bb = b // 4, b % 4
                    load = 8 * grp + bb
                    arrived(pe, load)
                    for j in range(3):
                        n = per * grp + 3 * bb + j
                        room(n)
                        for m in range(4):
                            last = pe.transpose(tp[n % 2][:, m * P:(m + 1) * P], ring[:, load % 2, 4 * j + m, :], ident[:])
                        last.then_inc(turned, 1)

                def scores(b):
                    grp, bb = b // 4, b % 4
                    for j in range(3):
                        n = per * grp + 3 * bb + j
                        pe.wait_ge(kept[n % 2], n // 2 + 1)
                    if bb == 0 and grp > 0:
                        pe.wait_ge(expd, 3 * grp)
                    q = q_rows[:, b, :]
                    r = slice(32 * bb, 32 * bb + 32)
                    k, new_k = kT[:, b % 2], slice(NP + NS * b, NP + NS * b + NS)
                    for at, rhs in ((CMPC, ck[:, b, :]), (0, k[:, 0:512]), (512, k[:, 512:1024]), (1024, qk[:, 6, new_k]),
                                    (WINC, qk[:, 8, new_k]), (1536, k[:, 1024:1536])):
                        to = misc if rhs.shape[-1] == CMP else wide
                        last = pe.matmul(to[r, at:at + rhs.shape[-1]], q, rhs, start=True, stop=True, skip_group_check=True,
                                         tile_position=(0, 32 * bb))
                    last.then_inc(score, 1)

                def group(n, blocks):
                    room(n)
                    for m, (at, w) in enumerate(blocks):
                        last = pe.transpose(tp[n % 2][0:w, m * P:(m + 1) * P], probs[:, at:at + w], ident[:])
                    last.then_inc(turned, 1)

                for grp in range(2):
                    b0, n0 = 4 * grp, per * grp
                    pe.matmul(misc[:, ROWG:ROWG + 24], row_of[:, grp], gates[0:TS, NT, :], start=True, stop=True,
                              skip_group_check=True).then_inc(small_mm, 1) if grp == 0 else None
                    turn_keys(b0)
                    for b in range(b0, b0 + 4):
                        if b < b0 + 3:
                            turn_keys(b + 1)
                        scores(b)
                    if grp == 1:
                        pe.matmul(misc[:, ROWG:ROWG + 24], row_of[:, grp], gates[0:TS, NT, :], start=True, stop=True,
                                  skip_group_check=True).then_inc(small_mm, 1)
                    pe.wait_ge(cmp_p, grp + 1)
                    group(n0 + 12, [(PC, CMP)])
                    pe.wait_ge(kept[(n0 + 12) % 2], (n0 + 12) // 2 + 1)
                    pe.matmul(misc[:, SC0:SC0 + 16], pT[0:CMP, 15], shared[:], start=True, stop=True, skip_group_check=True).then_inc(small_mm, 1)
                    pe.wait_ge(small_kept, grp + 1)
                    pe.matmul(misc[:, SC1:SC1 + 16], same[:], small[:, 3, 0:16], start=True, stop=True, skip_group_check=True).then_inc(small_mm, 1)
                    pe.wait_ge(probs_ready, grp + 1)
                    group(n0 + 13, [(PS_ + m * P, P) for m in range(4)])
                    group(n0 + 14, [(PS_ + m * P, P) for m in range(4, 8)])
                    group(n0 + 15, [(PW + NS + m * P, P) for m in range(4)])
                    group(n0 + 16, [(PS_ + NP, NS), (PW, NS), (PC, CMP)])
                    for n in range(n0 + 13, n0 + 17):
                        pe.wait_ge(kept[n % 2], n // 2 + 1)
                    for b in range(b0, b0 + 4):
                        load = 8 * grp + 4 + b % 4
                        arrived(pe, load)
                        r = slice(32 * (b % 4), 32 * (b % 4) + 32)
                        v = ring[:, load % 2]
                        terms = [(v[:, j], pT[:, j, r]) for j in range(12)]
                        terms += [(v_new[:, 0, b], pT[0:NS, 12, r]), (v_new[:, 1, b], pT[0:NS, 13, r]), (cv[:, b], pT[0:CMP, 14, r])]
                        for m, (lhsT, rhs) in enumerate(terms):
                            last = pe.matmul(out[:, 32 * b:32 * b + 32], lhsT, rhs, start=m == 0, stop=m == len(terms) - 1,
                                             skip_group_check=True)
                        last.then_inc(pv, 1)

            def keep(eng, copy, which, grp, ns):
                for n in ns:
                    if n % 2 != which:
                        continue
                    eng.wait_ge(turned, n + 1)
                    m = n - per * grp
                    src = tp[n % 2]
                    if m < 12:
                        b = 4 * grp + m // 3
                        if b >= 2:
                            eng.wait_ge(score, b - 1)
                        copy(kT[:, b % 2, 512 * (m % 3):512 * (m % 3) + 512], src[:]).then_inc(kept[which], 1)
                    elif m == 12:
                        copy(pT[0:CMP, 15], src[0:CMP, 0:P]).then_inc(kept[which], 1)
                    elif m < 16:
                        copy(pT[:, 4 * (m - 13):4 * (m - 13) + 4, :].rearrange("p b c -> p (b c)"), src[:]).then_inc(kept[which], 1)
                    else:
                        copy(pT[0:NS, 12:14].rearrange("p b c -> p (b c)"), src[0:NS, 0:2 * P])
                        copy(pT[0:CMP, 14], src[0:CMP, 2 * P:3 * P]).then_inc(kept[which], 1)

            @block.scalar
            def _(act):
                def exp(src, at, n, col):
                    act.activation(probs[:, at:at + n], (wide if col else misc)[:, src:src + n], ACT.Exp, bias=one[:, col:col + 1],
                                   accum_out=one[:, 5 + col:6 + col]).then_inc(expd, 1)

                for grp in range(2):
                    n0 = per * grp
                    keep(act, act.copy, 1, grp, range(n0, n0 + 12))
                    act.wait_ge(ready, 3 * grp + 1)
                    exp(CMPC, PC, CMP, 0)
                    keep(act, act.copy, 1, grp, [n0 + 12])
                    act.wait_ge(ready, 3 * grp + 3)
                    exp(SEL, PS_, NP + NS, 1)
                    exp(WINC, PW, WIN + NS, 2)
                    keep(act, act.copy, 1, grp, range(n0 + 13, n0 + 17))

            @block.vector
            def _(dve):
                ch = Chain(dve, chain)
                dve.wait_ge(zeroed, 1)
                for h in range(2):
                    r = slice(HD * h, HD * h + HD)
                    dve.tensor_copy(q_rows[r, :, 16 * h:16 * h + 16].rearrange("p b (g s) -> p g b s", g=4),
                                    qk[r, 0:4, NP:T].rearrange("p g (b s) -> p g b s", b=NB)).then_inc(q_ready, 1)
                dve.wait_ge(loaded, 16 * 9)
                for grp in range(2):
                    n0 = per * grp
                    mm = 3 * grp
                    keep(dve, dve.tensor_copy, 0, grp, range(n0, n0 + 12))
                    dve.wait_ge(score, 4 * grp + 4)
                    dve.wait_ge(small_mm, mm + 1)
                    ch(dve.tensor_tensor(small[:, 0], misc[:, ROWG:ROWG + 24], hg[:], ALU.mult))
                    ch(dve.tensor_reduce(small[:, 1, 0:3], small[:, 0].rearrange("p (x j) -> p j x", j=3), X, ALU.add))
                    dve.tensor_reduce(one[:, 0:1], misc[:, CMPC:CMPC + CMP], X, ALU.max, negate=True).then_inc(ready, 1)
                    ch(dve.tensor_tensor(wide[:, NP:NP + NS], wide[:, NP:NP + NS], new[:], ALU.add))
                    ch(dve.tensor_tensor(wide[:, WINC:WINC + NS], wide[:, WINC:WINC + NS], new[:], ALU.add))
                    ch(dve.tensor_tensor(wide[:, 1536:1536 + NS], wide[:, 1536:1536 + NS], old[:], ALU.add))
                    dve.tensor_reduce(one[:, 2:3], wide[:, WINC:2048], X, ALU.max, negate=True).then_inc(ready, 1)
                    dve.wait_ge(expd, 3 * grp + 1)
                    ch(dve.reciprocal(one[:, 10:11], one[:, 5:6]))
                    dve.tensor_scalar(probs[:, PC:PC + CMP], probs[:, PC:PC + CMP], one[:, 10:11], None, ALU.mult).then_inc(cmp_p, 1)
                    keep(dve, dve.tensor_copy, 0, grp, [n0 + 12])
                    dve.wait_ge(small_mm, mm + 2)
                    dve.tensor_copy(small[:, 3, 0:16], misc[:, SC0:SC0 + 16]).then_inc(small_kept, 1)
                    dve.wait_ge(small_mm, mm + 3)
                    ch(dve.tensor_copy(small[:, 4, 0:16], misc[:, SC1:SC1 + 16]))
                    ch(dve.tensor_reduce(one[:, 3:4], small[:, 4, 1:15], X, ALU.min))
                    ch(dve.tensor_scalar(small[:, 5, 1:15], small[:, 4, 1:15], one[:, 3:4], None, ALU.is_equal))
                    ch(dve.tensor_tensor(small[:, 5, 1:15], small[:, 5, 1:15], block_no[:, 1:15], ALU.mult))
                    ch(dve.tensor_reduce(one[:, 4:5], small[:, 5, 1:15], X, ALU.max))
                    ch(dve.tensor_scalar(small[:, 6, 0:16], block_no[:], one[:, 4:5], NEG, ALU.is_equal, ALU.mult))
                    sel = wide[:, 0:NP].rearrange("p (m c) -> p m c", m=16)
                    ch(dve.tensor_tensor(sel, sel, small[:, 6, 0:16].unsqueeze(2).to_broadcast([P, 16, HD]), ALU.add))
                    dve.tensor_reduce(one[:, 1:2], wide[:, 0:NP + NS], X, ALU.max, negate=True).then_inc(ready, 1)
                    dve.tensor_scalar(probs[:, PC:PC + CMP], probs[:, PC:PC + CMP], small[:, 1, 0:1], None, ALU.mult)
                    dve.wait_ge(expd, 3 * grp + 3)
                    ch(dve.reciprocal(one[:, 10:12], one[:, 6:8]))
                    dve.tensor_scalar(probs[:, 0:PW], probs[:, 0:PW], one[:, 10:11], small[:, 1, 1:2], ALU.mult, ALU.mult)
                    dve.tensor_scalar(probs[:, PW:PC], probs[:, PW:PC], one[:, 11:12], small[:, 1, 2:3], ALU.mult, ALU.mult).then_inc(probs_ready, 1)
                    keep(dve, dve.tensor_copy, 0, grp, range(n0 + 13, n0 + 17))
                dve.wait_ge(pv, NB)
                for h in range(2):
                    r = slice(HD * h, HD * h + HD)
                    dve.tensor_copy(oT[r, :, NP:T].rearrange("p g (b s) -> p g b s", b=NB),
                                    out[r, 0:256].rearrange("p (b x) -> p b x", b=NB)[:, :, 16 * h:16 * h + 16].rearrange("p b (g s) -> p g b s", g=4))


def merge(nc, i, sem, sb, banks, hT, oT, uv, qk):
    w = i["w_in"][0].rearrange("(k p) n -> p k n", p=P)
    wa = i["w_branch_a"][0].rearrange("(h g d) n -> h d g n", h=2, g=4)
    wb = i["w_branch_b"][0].rearrange("(k p) n -> p k n", p=P)
    with ExitStack() as ctx:
        slots = sb(ctx, "mg_w", [P, 2, 24, P])
        free = uv[:, 4:8, :].rearrange("p a t -> p (a t)")
        sg = free[:, 0:4 * C].rearrange("p (b m t) -> p b m t", b=2, m=2)
        prod = free[:, 4 * C:8 * C].rearrange("p (b m t) -> p b m t", b=2, m=2)
        ps = banks(ctx, 8)
        st = Stream(sem, "mg", 8, 2, loads=5)
        gated, chain = sem("mg_gated"), sem("mg_chain")
        with nc.Block() as block:
            @block.sync
            def _(sp):
                st.load(sp, lambda n, s: [
                    (slots[:, s, 0:8], w[:, :, bass.ds(GA_COL + n * P, P)]),
                    (slots[:, s, 8:16], w[:, :, bass.ds(GB_COL + n * P, P)]),
                    (slots[0:HD, s, 16:20], wa[0, :, :, bass.ds(n * P, P)]),
                    (slots[HD:P, s, 16:20], wa[1, :, :, bass.ds(n * P, P)]),
                    (slots[:, s, 20:24], wb[:, :, bass.ds(n * P, P)])])

            @block.tensor
            def _(pe):
                st.multiply(pe, lambda b, s, c: [
                    (ps[4 * b][:, 0:C], [(slots[:, s, k], hT[:, k, cols(c)]) for k in range(8)]),
                    (ps[4 * b + 1][:, 0:C], [(slots[:, s, 8 + k], hT[:, k, cols(c)]) for k in range(8)]),
                    (ps[4 * b + 2][:, 0:C], [(slots[:, s, 16 + k], oT[:, k, cols(c)]) for k in range(4)]),
                    (ps[4 * b + 3][:, 0:C], [(slots[:, s, 20 + k], uv[:, k, cols(c)]) for k in range(4)])])

            @block.scalar
            def _(act):
                with act.Fori(0, 4) as it:
                    for j in range(6):
                        act.wait_ge(st.done, 6 * it + j + 7)
                        act.wait_ge(chain, 18 * it + 3 * j + 3)
                        for m in range(2):
                            last = act.activation(sg[:, j % 2, m], ps[4 * (j % 2) + m][:, 0:C], ACT.Sigmoid)
                        last.then_inc(gated, 1)

            @block.vector
            def _(dve):
                dve.sem_inc(st.freed, 2)
                dve.sem_inc(chain, 6)
                with dve.Fori(0, 4) as it:
                    for j in range(6):
                        b = j % 2
                        dve.wait_ge(gated, 6 * it + j + 1)
                        dve.wait_ge(chain, 18 * it + 3 * j + 3)
                        dve.tensor_tensor(prod[:, b, 0], sg[:, b, 0], ps[4 * b + 2][:, 0:C], ALU.mult).then_inc(chain, 1)
                        dve.tensor_tensor(prod[:, b, 1], sg[:, b, 1], ps[4 * b + 3][:, 0:C], ALU.mult).then_inc(chain, 1)
                        dve.wait_ge(chain, 18 * it + 3 * j + 8)
                        dve.sem_inc(st.freed, 1)
                        dve.tensor_tensor(qk[:, bass.ds(2 * it + j // 3, 1), cols(j % 3)].rearrange("p a t -> p (a t)"),
                                          prod[:, b, 0], prod[:, b, 1], ALU.add).then_inc(chain, 1)


def add_product(nc, name, sem, sb, banks, w, src, xT, k_tiles):
    w = w.rearrange("(k p) n -> p k n", p=P)
    with ExitStack() as ctx:
        slots = sb(ctx, f"{name}_w", [P, 2, k_tiles, P])
        ps = banks(ctx, 6)
        st = Stream(sem, name, KD, 6)
        with nc.Block() as block:
            @block.sync
            def _(sp):
                st.load(sp, lambda n, s: [(slots[:, s], w[:, :, bass.ds(n * P, P)])])

            @block.tensor
            def _(pe):
                st.multiply(pe, lambda b, s, c: [(ps[b][:, 0:C], [(slots[:, s, k, :], src[:, k, cols(c)]) for k in range(k_tiles)])])

            @block.vector
            def _(dve):
                def use(n, b, c):
                    x = xT[:, bass.ds(n, 1), cols(c)].rearrange("p a t -> p (a t)")
                    return dve.tensor_tensor(x, x, ps[b][:, 0:C], ALU.add)
                st.take(dve, use)


def plain_product(nc, name, sem, sb, banks, w, src, dst):
    w = w.rearrange("(k p) n -> p k n", p=P)
    with ExitStack() as ctx:
        slots = sb(ctx, f"{name}_w", [P, 2, KD, P])
        ps = banks(ctx, 6)
        st = Stream(sem, name, KD, 6)
        with nc.Block() as block:
            @block.sync
            def _(sp):
                st.load(sp, lambda n, s: [(slots[:, s], w[:, :, bass.ds(n * P, P)])])

            @block.tensor
            def _(pe):
                st.multiply(pe, lambda b, s, c: [(ps[b][:, 0:C], [(slots[:, s, k, :], src[:, k, cols(c)]) for k in range(KD)])])

            @block.scalar
            def _(act):
                st.take(act, lambda n, b, c: act.copy(dst[:, bass.ds(n, 1), cols(c)].rearrange("p a t -> p (a t)"), ps[b][:, 0:C]))


def gate_up(nc, i, sem, sb, banks, hT, aT):
    wg, wu = (i[n][0].rearrange("(k p) n -> p k n", p=P) for n in ("w_gate", "w_up"))
    with ExitStack() as ctx:
        slots = sb(ctx, "gu_w", [P, 2, 2, KD, P])
        sg = sb(ctx, "silu", [P, 3, C])
        ps = banks(ctx, 6)
        st = Stream(sem, "gu", KF, 3, loads=2)
        silu = sem("silu_done")
        with nc.Block() as block:
            @block.sync
            def _(sp):
                st.load(sp, lambda n, s: [(slots[:, s, 0], wg[:, :, bass.ds(n * P, P)]), (slots[:, s, 1], wu[:, :, bass.ds(n * P, P)])])

            @block.tensor
            def _(pe):
                st.multiply(pe, lambda b, s, c: [(ps[2 * b + m][:, 0:C], [(slots[:, s, m, k, :], hT[:, k, cols(c)]) for k in range(KD)])
                                                 for m in range(2)])

            @block.scalar
            def _(act):
                with act.Fori(0, KF // 2) as it:
                    for j in range(6):
                        act.wait_ge(st.done, 6 * it + j + 7)
                        act.wait_ge(st.freed, 6 * it + j + 1)
                        act.activation(sg[:, j % 3], ps[2 * (j % 3)][:, 0:C], ACT.Silu).then_inc(silu, 1)

            @block.vector
            def _(dve):
                dve.sem_inc(st.freed, 3)
                with dve.Fori(0, KF // 2) as it:
                    for j in range(6):
                        dve.wait_ge(silu, 6 * it + j + 1)
                        dve.tensor_tensor(aT[:, bass.ds(2 * it + j // 3, 1), cols(j % 3)].rearrange("p a t -> p (a t)"),
                                          sg[:, j % 3], ps[2 * (j % 3) + 1][:, 0:C], ALU.mult).then_inc(st.freed, 1)


def memory(nc, i, o, sem, sb, banks, mkT, mv, ident, ones, gains, g):
    with ExitStack() as outer:
        memT = sb(outer, "memT", [P, KD, NM])
        hmT = sb(outer, "hmT", [P, KD, NM])
        with ExitStack() as ctx:
            rows = sb(ctx, "mem_rows", [P, 2, D])
            tp = banks(ctx, 4)
            mem_in, turned = sem("mem_in"), sem("mem_turned")
            with nc.Block() as block:
                @block.sync
                def _(sp):
                    sp.dma_start(rows[:], i["mem_prompt"][0].rearrange("(m p) c -> p m c", p=P)).then_inc(mem_in, 16)

                @block.tensor
                def _(pe):
                    pe.wait_ge(mem_in, 16)
                    for m in range(2):
                        for h in range(2):
                            for k in range(4):
                                last = pe.transpose(tp[2 * m + h][:, k * P:(k + 1) * P], rows[:, m, (4 * h + k) * P:(4 * h + k + 1) * P], ident[:])
                            last.then_inc(turned, 1)

                @block.vector
                def _(dve):
                    for m in range(2):
                        for h in range(2):
                            dve.wait_ge(turned, 2 * m + h + 1)
                            dve.tensor_copy(memT[:, 4 * h:4 * h + 4, m * P:(m + 1) * P], tp[2 * m + h][:].rearrange("p (k c) -> p k c", k=4))
        norm(nc, "mem", sem, sb, banks, memT, hmT, NM, 1, gains, g, ones)
        with ExitStack() as ctx:
            slots = sb(ctx, "mem_w", [P, 2, KD, 512])
            rows = memT[:].rearrange("p k m -> p (k m)").rearrange("p (m c) -> p m c", m=2)
            ps = banks(ctx, 4)
            w_in = [sem(f"mem_w{s}") for s in range(2)]
            done, kept, turned, row_kept, stored = (sem(f"mkv_{x}") for x in ("done", "kept", "turned", "rows", "stored"))
            with nc.Block() as block:
                @block.sync
                def _(sp):
                    for n in range(4):
                        if n >= 2:
                            sp.wait_ge(done, (4, 8)[n - 2])
                        w = i[("w_ck", "w_cv")[n // 2]][0].rearrange("(k p) n -> p k n", p=P)
                        sp.dma_start(slots[:, n % 2], w[:, :, (n % 2) * 512:(n % 2) * 512 + 512]).then_inc(w_in[n % 2], 16)
                    for n, (src, name) in enumerate(((rows, "new_mem_k_p"), (mv, "new_mem_v_p"))):
                        sp.wait_ge(row_kept, 4 * n + 4)
                        sp.dma_start(o[name][0, 0].rearrange("(m p) h d -> p m (h d)", p=P), src[:]).then_inc(stored, 16)
                    sp.wait_ge(stored, 32)

                @block.tensor
                def _(pe):
                    for n in range(8):
                        pe.wait_ge(w_in[n // 4], 16)
                        if n >= 2:
                            pe.wait_ge(kept, n - 1)
                        for k in range(KD):
                            last = pe.matmul(ps[n % 2][:, 0:NM], slots[:, n // 4, k, (n % 4) * P:(n % 4 + 1) * P], hmT[:, k, :],
                                             start=k == 0, stop=k == KD - 1)
                        last.then_inc(done, 1)
                    pe.wait_ge(kept, 8)
                    for m in range(2):
                        for h in range(2):
                            u = 2 * m + h
                            if u >= 2:
                                pe.wait_ge(row_kept, u - 1)
                            for k in range(4):
                                last = pe.transpose(ps[2 + u % 2][:, k * P:(k + 1) * P], mkT[:, 4 * h + k, m * P:(m + 1) * P], ident[:])
                            last.then_inc(turned, 1)
                    for h in range(2):
                        for m in range(2):
                            u = 4 + 2 * h + m
                            pe.wait_ge(w_in[h], 32)
                            pe.wait_ge(row_kept, u - 1)
                            for k in range(KD):
                                last = pe.matmul(ps[2 + u % 2][:], hmT[:, k, m * P:(m + 1) * P], slots[:, h, k, :], start=k == 0, stop=k == KD - 1)
                            last.then_inc(turned, 1)

                @block.scalar
                def _(act):
                    for n in range(8):
                        act.wait_ge(done, n + 1)
                        act.copy(mkT[:, n, :], ps[n % 2][:, 0:NM]).then_inc(kept, 1)

                @block.vector
                def _(dve):
                    for u in range(8):
                        dve.wait_ge(turned, u + 1)
                        if u < 4:
                            dst = rows[:, u // 2, 512 * (u % 2):512 * (u % 2) + 512]
                        else:
                            dst = mv[:, u % 2, 512 * (u // 2 - 2):512 * (u // 2 - 2) + 512]
                        dve.tensor_copy(dst, ps[2 + u % 2][:]).then_inc(row_kept, 1)


CSCALE = (D // 4) ** -0.5


def cross_prompt(nc, sem, sb, banks, uv, qk, mkT, mv, ident):
    with ExitStack() as ctx:
        qt = sb(ctx, "qt", [P, 2, KD, P])
        probs = sb(ctx, "cprobs", [P, 2, NM])
        turned = sb(ctx, "cturned", [P, 2, 2, P])
        mx = sb(ctx, "cp_mx", [P, 4])
        total = sb(ctx, "cp_total", [P, 4])
        ps = banks(ctx, 6)
        q_in, score, peak, expd, normed, pt, pt_kept, pv, out_kept, chain = (
            sem(f"cp_{x}") for x in ("q", "score", "peak", "exp", "normed", "pt", "pt_kept", "pv", "out", "chain"))
        with nc.Block() as block:
            @block.gpsimd
            def _(pool):
                with pool.Fori(0, NT // 2) as it:
                    for s in range(2):
                        pool.wait_ge(score, 8 * it + 4 * s + 4)
                        pool.tensor_copy(qt[:, s], uv[:, :, bass.ds((2 * it + s) * P, P)]).then_inc(q_in, 1)

            @block.tensor
            def _(pe):
                pe.sem_inc(score, 8)
                pe.sem_inc(pt, 4)
                pe.sem_inc(pv, 4)
                with pe.Fori(0, NT // 2) as it:
                    for s in range(2):
                        base = 8 * it + 4 * s
                        pe.wait_ge(q_in, 2 * it + s + 1)

                        def scores(h):
                            pe.wait_ge(expd, base + h + 3)
                            for k in range(2):
                                last = pe.matmul(ps[h % 2][:, 0:NM], qt[:, s, 2 * h + k, :], mkT[:, 2 * h + k, :], start=k == 0, stop=k == 1)
                            last.then_inc(score, 1)

                        scores(0)
                        for h in range(4):
                            if h < 3:
                                scores(h + 1)
                            pe.wait_ge(normed, base + h + 1)
                            pe.wait_ge(pt_kept, base + h + 3)
                            for m in range(2):
                                last = pe.transpose(ps[2 + h % 2][:, m * P:(m + 1) * P], probs[:, h % 2, m * P:(m + 1) * P], ident[:])
                            last.then_inc(pt, 1)
                            pe.wait_ge(pt_kept, base + h + 5)
                            pe.wait_ge(out_kept, base + h + 3)
                            for k in range(2):
                                for m in range(2):
                                    last = pe.matmul(ps[4 + h % 2][:, k * P:(k + 1) * P], mv[:, m, (2 * h + k) * P:(2 * h + k + 1) * P],
                                                     turned[:, h % 2, m], start=m == 0, stop=m == 1)
                            last.then_inc(pv, 1)

            @block.scalar
            def _(act):
                act.sem_inc(expd, 4)
                act.sem_inc(pt_kept, 4)
                with act.Fori(0, NT // 2) as it:
                    for j in range(8):
                        h = j % 4
                        base = 8 * it + j
                        act.wait_ge(peak, base + 1)
                        act.wait_ge(pt, base + 3)
                        act.activation(probs[:, j % 2], ps[j % 2][:, 0:NM], ACT.Exp, bias=mx[:, h:h + 1], scale=CSCALE,
                                       accum_out=total[:, h:h + 1]).then_inc(expd, 1)
                        act.wait_ge(pt, base + 5)
                        act.wait_ge(pv, base + 3)
                        act.copy(turned[:, j % 2].rearrange("p m c -> p (m c)"), ps[2 + j % 2][:, 0:NM]).then_inc(pt_kept, 1)

            @block.vector
            def _(dve):
                dve.sem_inc(out_kept, 4)
                with dve.Fori(0, NT // 2) as it:
                    for j in range(8):
                        h = j % 4
                        base = 8 * it + j
                        dve.wait_ge(score, base + 9)
                        dve.tensor_reduce(mx[:, h:h + 1], ps[j % 2][:, 0:NM], X, ALU.max, negate=True).then_inc(chain, 1)
                        dve.wait_ge(chain, 2 * base + 1)
                        dve.tensor_scalar(mx[:, h:h + 1], mx[:, h:h + 1], CSCALE, None, ALU.mult).then_inc(peak, 1)
                        dve.wait_ge(expd, base + 5)
                        dve.reciprocal(total[:, h:h + 1], total[:, h:h + 1]).then_inc(chain, 1)
                        dve.wait_ge(chain, 2 * base + 2)
                        dve.tensor_scalar(probs[:, j % 2], probs[:, j % 2], total[:, h:h + 1], None, ALU.mult).then_inc(normed, 1)
                        dve.wait_ge(pv, base + 5)
                        dve.tensor_copy(qk[:, 2 * h:2 * h + 2, bass.ds((2 * it + j // 4) * P, P)],
                                        ps[4 + j % 2][:, 0:NM].rearrange("p (k c) -> p k c", k=2)).then_inc(out_kept, 1)


def cross_sample(nc, i, sem, sb, banks, uv, qk, ident):
    with ExitStack() as ctx:
        mem = sb(ctx, "mem", [P, 2, 2, D])
        kT = sb(ctx, "mem_kT", [P, KD, NM])
        q_rows = sb(ctx, "cq_rows", [P, KD, NB, 32])
        probs = sb(ctx, "cs_probs", [P, 2, NM])
        turned = sb(ctx, "cs_turned", [P, 2, 2, P])
        one = sb(ctx, "cs_one", [P, 2, 4])
        tp = banks(ctx, 4)
        sc = banks(ctx, 2)
        out = banks(ctx, 1)[0]
        zeroed, q_ready, keys, score, peak, expd, normed, pt, pt_kept, pv, chain = (
            sem(f"cs_{x}") for x in ("zeroed", "q", "keys", "score", "peak", "exp", "normed", "pt", "pt_kept", "pv", "chain"))
        mem_in = [sem(f"cs_mem{s}") for s in range(2)]
        kept = [sem(f"cs_kept{k}") for k in range(2)]
        loads = [(name, 4 * grp + b) for grp in range(2) for name in ("cache_mem_k", "cache_mem_v") for b in range(4)]
        with nc.Block() as block:
            @block.sync
            def _(sp):
                for n, (name, b) in enumerate(loads):
                    if n >= 2:
                        before, bb = loads[n - 2]
                        if before == "cache_mem_k":
                            sp.wait_ge(keys, 4 * bb + 4)
                        else:
                            sp.wait_ge(pv, bb + 1)
                    sp.dma_start(mem[:, n % 2], i[name][0, b].rearrange("(m p) h d -> p m (h d)", p=P)).then_inc(mem_in[n % 2], 16)

            @block.gpsimd
            def _(pool):
                pool.memset(q_rows[:], 0.0).then_inc(zeroed, 1)

            @block.tensor
            def _(pe):
                pe.wait_ge(q_ready, KD)
                for grp in range(2):
                    for bb in range(4):
                        b = 4 * grp + bb
                        n = 8 * grp + bb
                        pe.wait_ge(mem_in[n % 2], 16 * (n // 2 + 1))
                        for x in range(4):
                            if b > 0:
                                pe.wait_ge(kept[x % 2], 2 * b - 1 + x // 2)
                            for k in range(2):
                                for m in range(2):
                                    last = pe.transpose(tp[x][:, k * NM + m * P:k * NM + (m + 1) * P],
                                                        mem[:, n % 2, m, (2 * x + k) * P:(2 * x + k + 1) * P], ident[:])
                            last.then_inc(keys, 1)
                        for x in range(2):
                            pe.wait_ge(kept[x], 2 * b + 2)
                        for k in range(KD):
                            last = pe.matmul(sc[grp][32 * bb:32 * bb + 32, 0:NM], q_rows[:, k, b, :], kT[:, k, :], start=k == 0, stop=k == KD - 1,
                                             tile_position=(0, 32 * bb), skip_group_check=True)
                        last.then_inc(score, 1)
                    pe.wait_ge(normed, grp + 1)
                    for m in range(2):
                        last = pe.transpose(tp[0][:, m * P:(m + 1) * P], probs[:, grp, m * P:(m + 1) * P], ident[:])
                    last.then_inc(pt, 1)
                    pe.wait_ge(pt_kept, grp + 1)
                    for bb in range(4):
                        b = 4 * grp + bb
                        n = 8 * grp + 4 + bb
                        pe.wait_ge(mem_in[n % 2], 16 * (n // 2 + 1))
                        for k in range(KD):
                            r = 32 * bb + NS * (k // 2)
                            at = k * TS + NS * b
                            for m in range(2):
                                last = pe.matmul(out[:, at:at + NS], mem[:, n % 2, m, k * P:(k + 1) * P], turned[:, grp, m, r:r + NS],
                                                 start=m == 0, stop=m == 1, skip_group_check=True)
                        last.then_inc(pv, 1)

            def keep(eng, copy, which):
                for b in range(NB):
                    for x in (which, which + 2):
                        eng.wait_ge(keys, 4 * b + x + 1)
                        if b > 0:
                            eng.wait_ge(score, b)
                        copy(kT[:, 2 * x:2 * x + 2, :].rearrange("p k c -> p (k c)"), tp[x][:]).then_inc(kept[which], 1)
                    if b % 4 == 3:
                        yield b // 4

            @block.scalar
            def _(act):
                for grp in keep(act, act.copy, 1):
                    act.wait_ge(peak, grp + 1)
                    act.activation(probs[:, grp], sc[grp][:, 0:NM], ACT.Exp, bias=one[:, grp, 0:1], scale=CSCALE,
                                   accum_out=one[:, grp, 1:2]).then_inc(expd, 1)

            @block.vector
            def _(dve):
                ch = Chain(dve, chain)
                dve.wait_ge(zeroed, 1)
                for k in range(KD):
                    h = k // 2
                    dve.tensor_copy(q_rows[:, k, :, NS * h:NS * h + NS], uv[:, k, NP:T].rearrange("p (b s) -> p b s", b=NB)).then_inc(q_ready, 1)
                for grp in keep(dve, dve.tensor_copy, 0):
                    dve.wait_ge(score, 4 * grp + 4)
                    ch(dve.tensor_reduce(one[:, grp, 2:3], sc[grp][:, 0:NM], X, ALU.max, negate=True))
                    dve.tensor_scalar(one[:, grp, 0:1], one[:, grp, 2:3], CSCALE, None, ALU.mult).then_inc(peak, 1)
                    dve.wait_ge(expd, grp + 1)
                    ch(dve.reciprocal(one[:, grp, 3:4], one[:, grp, 1:2]))
                    dve.tensor_scalar(probs[:, grp], probs[:, grp], one[:, grp, 3:4], None, ALU.mult).then_inc(normed, 1)
                    dve.wait_ge(pt, grp + 1)
                    dve.tensor_copy(turned[:, grp].rearrange("p m c -> p (m c)"), tp[0][:, 0:NM]).then_inc(pt_kept, 1)
                dve.wait_ge(pv, NB)
                dve.tensor_copy(qk[:, 0:KD, NP:T], out[:, 0:KD * TS].rearrange("p (k t) -> p k t", k=KD))


def store_y(nc, o, sem, sb, banks, hT, ident):
    with ExitStack() as ctx:
        rows = sb(ctx, "y_rows", [P, 2, D])
        tp = banks(ctx, 4)
        turned = sem("y_turned")
        kept = [sem(f"y_kept{h}") for h in range(2)]
        stored = [sem(f"y_stored{s}") for s in range(2)]

        def n_rows(t):
            return P if t < NT else TS

        with nc.Block() as block:
            @block.tensor
            def _(pe):
                for t in range(NT + 1):
                    for h in range(2):
                        if t >= 2:
                            pe.wait_ge(kept[h], t - 1)
                        for k in range(4):
                            last = pe.transpose(tp[2 * h + t % 2][0:n_rows(t), k * P:(k + 1) * P], hT[:, 4 * h + k, t * P:t * P + n_rows(t)], ident[:])
                        last.then_inc(turned, 1)

            def keep(eng, h, copy):
                for t in range(NT + 1):
                    r = n_rows(t)
                    eng.wait_ge(turned, 2 * t + h + 1)
                    if t >= 2:
                        eng.wait_ge(stored[t % 2], 16 * (t // 2))
                    copy(rows[0:r, t % 2, 512 * h:512 * h + 512], tp[2 * h + t % 2][0:r, :]).then_inc(kept[h], 1)

            @block.scalar
            def _(act):
                keep(act, 0, act.copy)

            @block.vector
            def _(dve):
                keep(dve, 1, dve.tensor_copy)

            @block.sync
            def _(sp):
                for t in range(NT + 1):
                    sp.wait_ge(kept[0], t + 1)
                    sp.wait_ge(kept[1], t + 1)
                    dst = o["y_prompt"][0, t * P:(t + 1) * P] if t < NT else o["y_sample"].rearrange("b s c -> (b s) c")
                    sp.dma_start(dst, rows[0:n_rows(t), t % 2]).then_inc(stored[t % 2], 16)
                sp.wait_ge(stored[0], 16 * 5)
                sp.wait_ge(stored[1], 16 * 4)


KV = (2, HD)
OUTS = [("y_prompt", (1, NP, D)), ("y_sample", (NB, NS, D)),
        ("new_cmp_k_p", (1, 1, NP, *KV)), ("new_cmp_v_p", (1, 1, NP, *KV)),
        ("new_slc_k_p", (1, 1, NP, *KV)), ("new_slc_v_p", (1, 1, NP, *KV)),
        ("new_win_k_p", (1, 1, WIN, *KV)), ("new_win_v_p", (1, 1, WIN, *KV)),
        ("new_mem_k_p", (1, 1, NM, 4, 256)), ("new_mem_v_p", (1, 1, NM, 4, 256)),
        ("new_cmp_k_s", (1, NB, NS, *KV)), ("new_cmp_v_s", (1, NB, NS, *KV)),
        ("new_slc_k_s", (1, NB, NS, *KV)), ("new_slc_v_s", (1, NB, NS, *KV)),
        ("new_win_k_s", (1, NB, WIN, *KV)), ("new_win_v_s", (1, NB, WIN, *KV)),
        ("new_gmlp_v_s", (1, NB, NS, 512))]


def kernel(**inputs):
    import concourse.bacc as bacc
    from concourse.bass_utils import run_bass_kernel_spmd

    nc = bacc.Bacc("TRN2", target_bir_lowering=False, num_devices=1)
    arrays = {k: np.ascontiguousarray(v) for k, v in inputs.items()}
    arrays.update(consts())
    ins = {k: nc.dram_tensor(k, v.shape, mybir.dt.from_np(v.dtype), kind="ExternalInput").ap() for k, v in arrays.items()}
    outs = {n: nc.dram_tensor("out_" + n, s, F32, kind="ExternalOutput").ap() for n, s in OUTS}
    build(nc, ins, outs)
    r = run_bass_kernel_spmd(nc, [arrays], core_ids=[0])
    return tuple(r.results[0]["out_" + n] for n, _ in OUTS)
```

```python
from contextlib import ExitStack

import numpy as np

import concourse.bass as bass
from concourse import mybir

ALU = mybir.AluOpType
ACT = mybir.ActivationFunctionType
F32 = mybir.dt.float32
F32R = mybir.dt.float32r
I32 = mybir.dt.int32
X = mybir.AxisListType.X

P = 128
D = 1024
KD = D // P
NP = 1024
NB = 8
NS = 4
TS = NB * NS
T = NP + TS
NT = NP // P
CH = 3
C = T // CH
HD = 64
G = 4
CMP = 63
SRC = NB + 1
PAIRS = 512
PAGES = 8
N_POOL = 80
WIN = 512
NM = 256
FF = 2816
KF = FF // P
EPS = 1e-6
NEG = -1e30
U_COL = 1304
GN_COL = 1280
GA_COL = 2328
GB_COL = 3352


def consts():
    half = HD // 2
    inv = (np.float32(10000.0) ** (-np.arange(half, dtype=np.float32) / np.float32(half))).astype(np.float32)
    pos = np.concatenate([np.arange(NP), np.tile(NP + np.arange(NS), NB)]).astype(np.float32)
    ang = (pos[None, :] * inv[:, None]).astype(np.float32)
    rot = np.zeros((P, P), np.float32)
    for m in range(P):
        if m % HD < half:
            rot[m + half, m] = -1.0
        else:
            rot[m - half, m] = 1.0
    a = np.arange(P)
    cend = 16 * np.arange(CMP) + 31
    seen = (cend[None, None, :] <= (P * np.arange(NT)[None, :, None] + a[:, None, None])).astype(np.float32)
    rb, rh, rg, rs = a // 32, a // 16 % 2, a // 4 % 4, a % 4
    same = (rb[:, None] == rb) & (rh[:, None] == rh) & (rs[:, None] == rs)
    shared = np.zeros((CMP, 16), np.float32)
    for n in range(CMP):
        for m in range(16):
            shared[n, m] = max(min(16 * n + 32, 64 * m + 64) - max(16 * n, 64 * m), 0) / 32
    s4 = np.arange(4)
    row_of = np.zeros((TS, 2, P), np.float32)
    for grp in range(2):
        row_of[(4 * grp + rb) * 4 + rs, grp, a] = 1.0
    hg = np.zeros((P, 8, 3), np.float32)
    hg[a, rh * 4 + rg, :] = 1.0
    lane = np.zeros((TS, 8, TS), np.float32)
    for j in range(TS):
        for k in range(TS):
            if j // 4 == k // 4 and j % 4 <= k % 4:
                lane[j, :, k] = 1.0
    return {
        "c_ident": np.eye(P, dtype=np.float32),
        "c_cos": np.tile(np.cos(ang), (4, 1)).astype(np.float32),
        "c_sin": np.tile(np.sin(ang), (4, 1)).astype(np.float32),
        "c_rot": rot,
        "c_tril": (a[:, None] <= a[None, :]).astype(np.float32),
        "c_lane": lane,
        "c_diag": np.where(a[None, :] <= a[:, None], 0.0, NEG).astype(np.float32),
        "c_far": np.where(a[None, :] > a[:, None], 0.0, NEG).astype(np.float32),
        "c_seen": seen,
        "c_hidden": np.where(seen > 0, 0.0, NEG).astype(np.float32),
        "c_same": same.astype(np.float32),
        "c_shared": shared,
        "c_new": np.where(s4[None, :] <= rs[:, None], 0.0, NEG).astype(np.float32),
        "c_old": np.where(s4[None, :] > rs[:, None], 0.0, NEG).astype(np.float32),
        "c_row_of": row_of,
        "c_hg": hg,
        "c_block": np.tile(np.arange(16, dtype=np.float32), (P, 1)),
    }


class Chain:

    def __init__(self, eng, sem):
        self.eng, self.sem, self.n = eng, sem, 0

    def __call__(self, ins):
        self.n += 1
        ins.then_inc(self.sem, 1)
        self.eng.wait_ge(self.sem, self.n)


class Stream:

    def __init__(self, sem, name, tiles, sets, loads=1):
        self.tiles, self.sets, self.loads = tiles, sets, loads
        self.w_in = [sem(f"{name}_w{s}") for s in range(2)]
        self.done = sem(f"{name}_done")
        self.freed = sem(f"{name}_freed")

    def load(self, sp, copies):
        with sp.Fori(0, self.tiles // 2) as it:
            for s in range(2):
                sp.wait_ge(self.done, 6 * it + 3 * s + 3)
                for dst, src in copies(2 * it + s, s):
                    sp.dma_start(dst, src).then_inc(self.w_in[s], 16)

    def multiply(self, pe, groups):
        pe.sem_inc(self.done, 6)
        with pe.Fori(0, self.tiles // 2) as it:
            for s in range(2):
                pe.wait_ge(self.w_in[s], 16 * self.loads * it + 16 * self.loads)
                for c in range(CH):
                    pe.wait_ge(self.freed, 6 * it + 3 * s + c + 1)
                    for out, terms in groups((3 * s + c) % self.sets, s, c):
                        for j, (lhsT, rhs) in enumerate(terms):
                            last = pe.matmul(out, lhsT, rhs, start=j == 0, stop=j == len(terms) - 1)
                    last.then_inc(self.done, 1)

    def take(self, eng, use):
        eng.sem_inc(self.freed, self.sets)
        with eng.Fori(0, self.tiles // 2) as it:
            for s in range(2):
                for c in range(CH):
                    eng.wait_ge(self.done, 6 * it + 3 * s + c + 7)
                    use(2 * it + s, (3 * s + c) % self.sets, c).then_inc(self.freed, 1)


class SplitStream:

    def __init__(self, sb, sem, ctx, name, depth, sets):
        self.sets = sets
        self.raw = sb(ctx, f"{name}_raw", [P, 2, depth, P])
        self.w_hi = sb(ctx, f"{name}_w_hi", [P, 2, depth, P], F32R)
        self.w_lo = sb(ctx, f"{name}_w_lo", [P, 2, depth, P], F32R)
        self.w_in = [sem(f"{name}_w{s}") for s in range(2)]
        self.rounded, self.split, self.passed, self.done, self.freed = (
            sem(f"{name}_{x}") for x in ("rounded", "split", "passed", "done", "freed"))

    def load(self, sp, first, tiles, copies):
        with sp.Fori(0, tiles // 2) as it:
            for s in range(2):
                sp.wait_ge(self.split, 2 * it + (first + s + 1))
                for dst, src in copies(2 * it + s, self.raw[:, s]):
                    sp.dma_start(dst, src).then_inc(self.w_in[s], 16)

    def start_split(self, pool):
        pool.sem_inc(self.split, 2)

    def split_weights(self, pool, first, tiles, depth):
        with pool.Fori(0, tiles // 2) as it:
            for s in range(2):
                raw, hi, lo = (x[:, s, 0:depth] for x in (self.raw, self.w_hi, self.w_lo))
                pool.wait_ge(self.w_in[s], 32 * it + (16 * first + 32))
                pool.wait_ge(self.done, 6 * it + (3 * first + 3 * s + 3))
                pool.sem_inc(self.passed, 1)
                pool.tensor_copy(hi, raw).then_inc(self.rounded, 1)
                pool.wait_ge(self.rounded, 2 * it + (first + s + 1))
                pool.sem_inc(self.passed, 1)
                pool.tensor_tensor(lo, raw, hi.bitcast(F32), ALU.subtract).then_inc(self.split, 1)

    def start_multiply(self, pe):
        pe.sem_inc(self.done, 6)

    def multiply(self, pe, first, tiles, groups, ready=None):
        with pe.Fori(0, tiles // 2) as it:
            for s in range(2):
                pe.wait_ge(self.split, 2 * it + (first + s + 3))
                for c in range(CH):
                    if ready is not None:
                        pe.wait_ge(ready, c + 1)
                    pe.wait_ge(self.freed, 6 * it + (3 * first + 3 * s + c + 1))
                    for out, k0, terms in groups((3 * s + c) % self.sets, c):
                        for k, (x_hi, x_lo) in enumerate(terms):
                            hi, lo = self.w_hi[:, s, k0 + k, :], self.w_lo[:, s, k0 + k, :]
                            pe.matmul(out, hi, x_hi, start=k == 0, stop=False)
                            pe.matmul(out, hi, x_lo, start=False, stop=False)
                            last = pe.matmul(out, lo, x_hi, start=False, stop=k == len(terms) - 1)
                    last.then_inc(self.done, 1)

    def start_take(self, eng):
        eng.sem_inc(self.freed, self.sets)

    def take(self, eng, first, tiles, use):
        with eng.Fori(0, tiles // 2) as it:
            for s in range(2):
                for c in range(CH):
                    eng.wait_ge(self.done, 6 * it + (3 * first + 3 * s + c + 7))
                    use(2 * it + s, (3 * s + c) % self.sets, c).then_inc(self.freed, 1)


def halves(raw, src, depth):
    h = depth // 2
    return [(raw[:, 0:h], src[:, 0:h]), (raw[:, h:depth], src[:, h:depth])]


def cols(c):
    return slice(c * C, c * C + C)


def build(nc, i, o):
    with ExitStack() as top, nc.allow_non_contiguous_dma(reason="small tables"):
        taken = []

        def sem(name):
            taken.append(nc.alloc_semaphore(name))
            return taken[-1]

        def clear_semaphores():
            nc.clear_and_free_semaphores(taken)
            nc.all_engine_barrier()
            taken.clear()

        def sb(ctx, name, shape, dt=F32):
            return ctx.enter_context(nc.sbuf_tensor(name, shape, dt))

        def banks(ctx, n):
            return [ctx.enter_context(nc.psum_tensor(f"bank{k}_{nc.next_id()}", [P, 512], F32)) for k in range(n)]

        xT = sb(top, "xT", [P, KD, T])
        ident = sb(top, "ident", [P, P])
        ones = sb(top, "ones", [P, P])
        gains = sb(top, "gains", [P, 5, KD])
        G_MIX, G_CROSS, G_MEM, G_FFN, G_FINAL = range(5)

        def halved(ctx, name):
            return sb(ctx, f"{name}_hi", [P, KD, T], F32R), sb(ctx, f"{name}_lo", [P, KD, T], F32R)

        load_x(nc, i, sem, sb, banks, xT, ident, ones, gains)
        with ExitStack() as mid:
            qk = sb(mid, "qk", [P, 10, T])
            with ExitStack() as mix:
                hT = sb(mix, "hT", [P, KD, T])
                norm(nc, "mix", sem, sb, banks, xT, hT, T, CH, gains, G_MIX, ones)
                uv = sb(mix, "uv", [P, 8, T])
                vtok = sb(mix, "vtok", [P, NT, 2, P])
                gates = sb(mix, "gates", [P, NT + 1, 24])
                project(nc, i, sem, sb, banks, hT, qk, uv)
                rope(nc, i, sem, sb, banks, qk)
                rows_and_gmlp(nc, i, o, sem, sb, banks, hT, qk, uv, vtok, gates, ident)
                with ExitStack() as att:
                    ck = sb(att, "ck", [P, SRC, CMP])
                    cv = sb(att, "cv", [CMP, SRC, P])
                    compress(nc, i, o, sem, sb, banks, uv, ck, cv, ident)
                    oT = sb(att, "oT", [P, G, T])
                    attend_prompt(nc, i, sem, sb, banks, qk, vtok, gates, ck, cv, oT, ident)
                    attend_sample(nc, i, o, sem, sb, banks, qk, uv, gates, ck, cv, oT, ident)
                    clear_semaphores()
                    merge(nc, i, sem, sb, banks, hT, oT, uv, qk)
            cqT = sb(mid, "cqT", [P, KD, T])
            with ExitStack() as parts:
                hi, lo = halved(parts, "mix")
                add_product(nc, "out", sem, sb, banks, i["w_out"][0], qk, hi, lo, xT)
                norm_split(nc, "cross", sem, sb, banks, xT, hi, lo, gains, G_CROSS, ones)
                plain_product(nc, "cq", sem, sb, banks, i["w_cq"][0], hi, lo, cqT)
            with ExitStack() as mem:
                mkT = sb(mem, "mkT", [P, KD, NM])
                mv = sb(mem, "mv", [P, 2, D])
                memory(nc, i, o, sem, sb, banks, mkT, mv, ident, ones, gains, G_MEM)
                cross_prompt(nc, sem, sb, banks, cqT, qk, mkT, mv, ident)
            cross_sample(nc, i, sem, sb, banks, cqT, qk, ident)
            with ExitStack() as parts:
                hi, lo = halved(parts, "cross")
                add_product(nc, "co", sem, sb, banks, i["w_co"][0], qk, hi, lo, xT)
        with ExitStack() as ffn:
            hi, lo = halved(ffn, "ffn")
            norm_split(nc, "ffn", sem, sb, banks, xT, hi, lo, gains, G_FFN, ones)
            feed_forward(nc, i, sem, sb, banks, hi, lo, xT)
        yT = sb(top, "yT", [P, KD, T])
        norm(nc, "final", sem, sb, banks, xT, yT, T, CH, gains, G_FINAL, ones)
        store_y(nc, o, sem, sb, banks, yT, ident)


def load_x(nc, i, sem, sb, banks, xT, ident, ones, gains):
    with ExitStack() as ctx:
        xin = sb(ctx, "xin", [P, 3, D])
        tp = banks(ctx, 4)
        const_in, ones_set = sem("const_in"), sem("ones_set")
        x_in = [sem(f"x_in{s}") for s in range(3)]
        turned = [sem(f"x_turned{h}") for h in range(2)]
        taken = [sem(f"x_taken{h}") for h in range(2)]
        with nc.Block() as block:
            @block.sync
            def _(sp):
                sp.dma_start(ident[:], i["c_ident"]).then_inc(const_in, 16)
                sp.dma_start(xin[0:TS, 2, :], i["x_sample"].rearrange("b s d -> (b s) d")).then_inc(x_in[2], 16)
                with sp.Fori(0, NT // 2) as it:
                    for s in range(2):
                        sp.wait_ge(turned[1], 2 * it + s + 1)
                        sp.dma_start(xin[:, s, :], i["x_prompt"][0, bass.ds((2 * it + s) * P, P), :]).then_inc(x_in[s], 16)

            @block.gpsimd
            def _(pool):
                pool.memset(ones[:], 1.0).then_inc(ones_set, 1)

            def turn(pe, h, s, rows, src):
                for k in range(4):
                    last = pe.transpose(tp[2 * h + s][:, k * P:k * P + rows], src[:, (4 * h + k) * P:(4 * h + k + 1) * P],
                                        ident[0:rows, 0:rows])
                last.then_inc(turned[h], 1)

            @block.tensor
            def _(pe):
                pe.wait_ge(const_in, 16 * 6)
                pe.sem_inc(turned[0], 2)
                pe.sem_inc(turned[1], 2)
                with pe.Fori(0, NT // 2) as it:
                    for s in range(2):
                        pe.wait_ge(x_in[s], 16 * it + 16)
                        for h in range(2):
                            pe.wait_ge(taken[h], 2 * it + s + 1)
                            turn(pe, h, s, P, xin[:, s, :])
                pe.wait_ge(x_in[2], 16)
                for h in range(2):
                    pe.wait_ge(taken[h], NT + 1)
                    turn(pe, h, 0, TS, xin[0:TS, 2, :])

            def take(eng, h, copy):
                eng.sem_inc(taken[h], 2)
                with eng.Fori(0, NT // 2) as it:
                    for s in range(2):
                        eng.wait_ge(turned[h], 2 * it + s + 3)
                        copy(xT[:, 4 * h:4 * h + 4, bass.ds((2 * it + s) * P, P)],
                             tp[2 * h + s][:].rearrange("p (k c) -> p k c", k=4)).then_inc(taken[h], 1)
                eng.wait_ge(turned[h], NT + 3)
                copy(xT[:, 4 * h:4 * h + 4, NP:T],
                     tp[2 * h][:].rearrange("p (k c) -> p k c", k=4)[:, :, 0:TS]).then_inc(taken[h], 1)

            @block.scalar
            def _(act):
                for n, name in enumerate(("g_mix", "g_cross", "g_mem", "g_ffn")):
                    act.dma_start(gains[:, n, :], i[name][0].rearrange("(k p) -> p k", p=P)).then_inc(const_in, 16)
                act.dma_start(gains[:, 4, :], i["g_final"].rearrange("(k p) -> p k", p=P)).then_inc(const_in, 16)
                take(act, 0, act.copy)

            @block.vector
            def _(dve):
                take(dve, 1, dve.tensor_copy)


def norm(nc, name, sem, sb, banks, src, dst, width, chunks, gains, g, ones):
    n = width // chunks
    with ExitStack() as ctx:
        sq = sb(ctx, f"{name}_sq", [P, 2, KD, n])
        part = sb(ctx, f"{name}_part", [P, chunks, n])
        std = sb(ctx, f"{name}_std", [P, chunks, n])
        ps = banks(ctx, chunks)
        squared, summed, spread, rooted, chain = (sem(f"{name}_{x}") for x in ("squared", "summed", "spread", "rooted", "chain"))
        with nc.Block() as block:
            @block.scalar
            def _(act):
                for c in range(chunks):
                    if c >= 2:
                        act.wait_ge(summed, c - 1)
                    act.square(sq[:, c % 2], src[:, 0:KD, c * n:(c + 1) * n]).then_inc(squared, 1)
                for c in range(chunks):
                    act.wait_ge(chain, c + 1)
                    act.sqrt(std[:, c], std[:, c]).then_inc(rooted, 1)

            @block.tensor
            def _(pe):
                for c in range(chunks):
                    pe.wait_ge(summed, c + 1)
                    pe.matmul(ps[c][:, 0:n], ones[:], part[:, c], start=True, stop=True).then_inc(spread, 1)

            @block.vector
            def _(dve):
                for c in range(chunks):
                    dve.wait_ge(squared, c + 1)
                    dve.tensor_reduce(part[:, c], sq[:, c % 2].rearrange("p k t -> p t k"), X, ALU.add).then_inc(summed, 1)
                ch = Chain(dve, chain)
                for c in range(chunks):
                    dve.wait_ge(spread, c + 1)
                    ch(dve.tensor_scalar(std[:, c], ps[c][:, 0:n], 1.0 / D, EPS, ALU.mult, ALU.add))
                for c in range(chunks):
                    dve.wait_ge(rooted, c + 1)
                    ch(dve.reciprocal(part[:, c], std[:, c]))
                    for k in range(KD):
                        dve.scalar_tensor_tensor(dst[:, k, c * n:(c + 1) * n], src[:, k, c * n:(c + 1) * n], gains[:, g, k:k + 1],
                                                 part[:, c], ALU.mult, ALU.mult)


def norm_split(nc, name, sem, sb, banks, src, hi, lo, gains, g, ones):
    units = [(c, k) for c in range(CH) for k in range(KD)]
    with ExitStack() as ctx:
        sq = sb(ctx, f"{name}_sq", [P, 2, KD, C])
        part = sb(ctx, f"{name}_part", [P, CH, C])
        h = sb(ctx, f"{name}_h", [P, 4, C])
        ps = banks(ctx, CH)
        squared, summed, spread, rooted, chain, scaled, rounded, split = (
            sem(f"{name}_{x}") for x in ("squared", "summed", "spread", "rooted", "chain", "scaled", "rounded", "split"))
        with nc.Block() as block:
            @block.scalar
            def _(act):
                for c in range(CH):
                    if c >= 2:
                        act.wait_ge(summed, c - 1)
                    act.square(sq[:, c % 2], src[:, 0:KD, cols(c)]).then_inc(squared, 1)
                for c in range(CH):
                    act.wait_ge(chain, c + 1)
                    act.sqrt(part[:, c], part[:, c]).then_inc(rooted, 1)
                for u, (c, k) in enumerate(units):
                    act.wait_ge(scaled, u + 1)
                    act.copy(hi[:, k, cols(c)], h[:, u % 4]).then_inc(rounded, 1)

            @block.tensor
            def _(pe):
                for c in range(CH):
                    pe.wait_ge(summed, c + 1)
                    pe.matmul(ps[c][:, 0:C], ones[:], part[:, c], start=True, stop=True).then_inc(spread, 1)

            @block.gpsimd
            def _(pool):
                for u, (c, k) in enumerate(units):
                    pool.wait_ge(rounded, u + 1)
                    pool.tensor_tensor(lo[:, k, cols(c)], h[:, u % 4], hi[:, k, cols(c)].bitcast(F32), ALU.subtract).then_inc(split, 1)

            @block.vector
            def _(dve):
                for c in range(CH):
                    dve.wait_ge(squared, c + 1)
                    dve.tensor_reduce(part[:, c], sq[:, c % 2].rearrange("p k t -> p t k"), X, ALU.add).then_inc(summed, 1)
                ch = Chain(dve, chain)
                for c in range(CH):
                    dve.wait_ge(spread, c + 1)
                    ch(dve.tensor_scalar(part[:, c], ps[c][:, 0:C], 1.0 / D, EPS, ALU.mult, ALU.add))
                for c in range(CH):
                    dve.wait_ge(rooted, c + 1)
                    ch(dve.reciprocal(part[:, c], part[:, c]))
                    for k in range(KD):
                        u = KD * c + k
                        if u >= 4:
                            dve.wait_ge(split, u - 3)
                        dve.scalar_tensor_tensor(h[:, u % 4], src[:, k, cols(c)], gains[:, g, k:k + 1],
                                                 part[:, c], ALU.mult, ALU.mult).then_inc(scaled, 1)


def project(nc, i, sem, sb, banks, hT, qk, uv):
    w = i["w_in"][0].rearrange("(k p) n -> p k n", p=P)
    with ExitStack() as ctx:
        slots = sb(ctx, "in_w", [P, 4, KD, P])
        ps = banks(ctx, 6)
        parts = [(Stream(sem, "q", 4, 6, loads=2), qk, ACT.Copy, 0), (Stream(sem, "kv", 6, 6), qk[:, 4:10], ACT.Copy, 2),
                 (Stream(sem, "uv", 8, 6), uv, ACT.Gelu_apprx_tanh, 0)]

        def q_load(n, s):
            return [(slots[:, s, :, HD * h:HD * h + HD], w[:, :, bass.ds(n * HD + G * HD * h, HD)]) for h in range(2)]

        with nc.Block() as block:
            @block.sync
            def _(sp):
                parts[0][0].load(sp, q_load)
                parts[1][0].load(sp, lambda n, s: [(slots[:, 2 + s], w[:, :, bass.ds(4 * P + n * P, P)])])
                sp.wait_ge(parts[0][0].done, 6 + 3 * 4)
                parts[2][0].load(sp, lambda n, s: [(slots[:, s], w[:, :, bass.ds(U_COL + n * P, P)])])

            @block.tensor
            def _(pe):
                for n, (st, _, _, slot) in enumerate(parts):
                    if n:
                        before = parts[n - 1][0]
                        pe.wait_ge(before.freed, before.sets + 3 * before.tiles)
                    st.multiply(pe, lambda b, s, c: [(ps[b][:, 0:C], [(slots[:, slot + s, k, :], hT[:, k, cols(c)]) for k in range(KD)])])

            @block.scalar
            def _(act):
                for st, dst, func, _ in parts:
                    st.take(act, lambda n, b, c: act.activation(dst[:, bass.ds(n, 1), cols(c)].rearrange("p a t -> p (a t)"),
                                                                ps[b][:, 0:C], func))


ROPED = (0, 1, 2, 3, 4, 6, 8)


def rope(nc, i, sem, sb, banks, qk):
    with ExitStack() as ctx:
        cos = sb(ctx, "cos", [P, T])
        sin = sb(ctx, "sin", [P, T])
        rot = sb(ctx, "rot", [P, P])
        t = sb(ctx, "rope_t", [P, 2, 2, C])
        ps = banks(ctx, 2)
        table_in, rotated, done, sin_done = sem("table_in"), sem("rotated"), sem("roped"), sem("rope_sin")
        cos_done = sem("rope_cos")
        units = [(tile, c) for tile in ROPED for c in range(CH)]
        with nc.Block() as block:
            @block.sync
            def _(sp):
                for dst, name in ((cos, "c_cos"), (sin, "c_sin"), (rot, "c_rot")):
                    sp.dma_start(dst[:], i[name]).then_inc(table_in, 16)

            @block.tensor
            def _(pe):
                pe.wait_ge(table_in, 48)
                for u, (tile, c) in enumerate(units):
                    if u >= 2:
                        pe.wait_ge(sin_done, u - 1)
                    pe.matmul(ps[u % 2][:, 0:C], rot[:], qk[:, tile, cols(c)], start=True, stop=True).then_inc(rotated, 1)

            @block.gpsimd
            def _(pool):
                pool.wait_ge(table_in, 48)
                for u, (tile, c) in enumerate(units):
                    if u >= 2:
                        pool.wait_ge(done, u - 1)
                    pool.tensor_tensor(t[:, u % 2, 1], qk[:, tile, cols(c)], cos[:, cols(c)], ALU.mult).then_inc(cos_done, 1)

            @block.vector
            def _(dve):
                dve.wait_ge(table_in, 48)
                for u, (tile, c) in enumerate(units):
                    dve.wait_ge(rotated, u + 1)
                    dve.tensor_tensor(t[:, u % 2, 0], ps[u % 2][:, 0:C], sin[:, cols(c)], ALU.mult).then_inc(sin_done, 1)
                    dve.wait_ge(sin_done, u + 1)
                    dve.wait_ge(cos_done, u + 1)
                    dve.tensor_tensor(qk[:, tile, cols(c)], t[:, u % 2, 0], t[:, u % 2, 1], ALU.add).then_inc(done, 1)
                for g in range(4):
                    dve.wait_ge(done, 3 * g + 3)
                    dve.tensor_scalar(qk[:, g, :], qk[:, g, :], HD ** -0.5, None, ALU.mult)


def rows_and_gmlp(nc, i, o, sem, sb, banks, hT, qk, uv, vtok, gates, ident):
    with ExitStack() as ctx:
        w_gn = sb(ctx, "w_gn", [P, KD, 24])
        ws = sb(ctx, "ws", [P, 8, P])
        wsT = sb(ctx, "wsT", [P, 8, P])
        wlane = sb(ctx, "wlane", [TS, 8, TS])
        tril = sb(ctx, "tril", [P, P])
        lane = sb(ctx, "lane", [TS, 8, TS])
        bias = sb(ctx, "bias", [P, 4, P])
        ln_g = sb(ctx, "ln_g", [P, 512])
        ln_b = sb(ctx, "ln_b", [P, 512])
        kv = sb(ctx, "kv", [P, 2, 6, P])
        gv = sb(ctx, "gv", [TS, 512])
        vn = sb(ctx, "vn", [P, 2, 512])
        sp_t = sb(ctx, "sp_t", [P, 2, 4, P])
        stat = sb(ctx, "stat", [P, 2, 6])
        mom = sb(ctx, "mom", [P, 2, 2])
        dev = sb(ctx, "dev", [P, 2, 2])
        ps = banks(ctx, 8)
        loaded, lane0, lane_in, ws_turned, ws_kept = sem("gm_loaded"), sem("lane0"), sem("lane_in"), sem("ws_turned"), sem("ws_kept")
        a_full, b_full, v_full, s_full = (sem(f"rw_{x}_full") for x in "abvs")
        copied, v_kept, v_rooted, var_ready, chain, vn_ready, s_used = (
            sem(f"rw_{x}") for x in ("copied", "v_kept", "rooted", "var", "chain", "vn", "s_used"))
        gates_done, gv_copied, gv_out = sem("gates_done"), sem("gv_copied"), sem("gv_out")
        kv_out = [sem(f"kv_out{s}") for s in range(2)]
        win_out = sem("win_out")
        stored = [0, 0]
        after = []
        for t in range(NT + 1):
            stored[t % 2] += 6 if t >= 4 else 4
            after.append(stored[t % 2])

        def rows(t):
            return P if t < NT else TS

        def at(t):
            return slice(t * P, t * P + rows(t))

        with nc.Block() as block:
            @block.sync
            def _(sp):
                w = i["w_in"][0].rearrange("(k p) n -> p k n", p=P)
                sp.dma_start(ws[:], i["gmlp_ws"][0].rearrange("g i j -> i g j")).then_inc(loaded, 16)
                sp.dma_start(w_gn[:], w[:, :, GN_COL:GN_COL + 24]).then_inc(loaded, 16)
                sp.dma_start(tril[:], i["c_tril"]).then_inc(loaded, 16)
                sp.dma_start(lane[:], i["c_lane"]).then_inc(loaded, 16)
                bs = i["gmlp_bs"][0].rearrange("(t a) i -> a t i", a=2)
                for a in range(2):
                    sp.dma_start(bias[HD * a:HD * a + HD], bs[a].partition_broadcast(HD)).then_inc(loaded, 16)
                sp.dma_start(ln_g[:], i["gmlp_ln_g"][0].partition_broadcast(P)).then_inc(loaded, 16)
                sp.dma_start(ln_b[:], i["gmlp_ln_b"][0].partition_broadcast(P)).then_inc(loaded, 16)
                sp.wait_ge(lane0, 1)
                for b in range(NB):
                    for g in range(8):
                        sp.dma_start(wlane[NS * b:NS * b + NS, g, NS * b:NS * b + NS],
                                     i["gmlp_ws"][0, g, 0:NS, 0:NS].rearrange("i j -> j i")).then_inc(lane_in, 16)

            @block.gpsimd
            def _(pool):
                pool.memset(wlane[:], 0.0).then_inc(lane0, 1)
                for name, state in (("new_win_k_s", "state_win_k"), ("new_win_v_s", "state_win_v")):
                    pool.dma_start(o[name][0, :, 0:WIN - NS].rearrange("b t h d -> b (t h d)"),
                                   i[state][0, :, NS:WIN].rearrange("b t h d -> b (t h d)")).then_inc(win_out, 16)
                for t in range(NT + 1):
                    pool.wait_ge(copied, 2 * t + 2)
                    s = t % 2
                    flat = "t h d -> t (h d)"
                    for n, name in enumerate(("cmp_k", "cmp_v", "slc_k", "slc_v", "win_k", "win_v")):
                        if t < NT:
                            if n >= 4 and t < 4:
                                continue
                            dst = o[f"new_{name}_p"][0, 0].rearrange(flat)
                            r0 = t * P - (WIN if n >= 4 else 0)
                            dst = dst[r0:r0 + P]
                        elif n < 4:
                            dst = o[f"new_{name}_s"][0].rearrange("b s h d -> (b s) (h d)")
                        else:
                            dst = o[f"new_{name}_s"][0, :, WIN - NS:WIN].rearrange("b s h d -> b s (h d)")
                        pool.dma_start(dst, kv[0:rows(t), s, n]).then_inc(kv_out[s], 16)
                pool.wait_ge(gv_copied, 1)
                pool.dma_start(o["new_gmlp_v_s"][0].rearrange("b s c -> (b s) c"), gv[:]).then_inc(gv_out, 16)
                pool.wait_ge(gv_out, 16)
                pool.wait_ge(win_out, 32)
                for s in range(2):
                    pool.wait_ge(kv_out[s], 16 * stored[s])

            @block.tensor
            def _(pe):
                pe.wait_ge(loaded, 16 * 8)
                for h in range(2):
                    for g in range(4):
                        last = pe.transpose(ps[6 + h][:, g * P:(g + 1) * P], ws[:, 4 * h + g, :], ident[:])
                    last.then_inc(ws_turned, 1)

                def turn(t):
                    if t >= 2:
                        pe.wait_ge(copied, 2 * t - 2)
                        pe.wait_ge(v_kept, t - 1)
                        pe.wait_ge(gates_done, t - 1)
                    r = rows(t)
                    a, b, v = ps[t % 2], ps[2 + t % 2], ps[4 + t % 2]
                    for n in range(4):
                        last = pe.transpose(a[0:r, n * P:(n + 1) * P], qk[:, 4 + n, at(t)], ident[:])
                    last.then_inc(a_full, 1)
                    for n in range(2):
                        pe.transpose(b[0:r, n * P:(n + 1) * P], qk[:, 8 + n, at(t)], ident[:])
                    for k in range(KD):
                        last = pe.matmul(b[0:r, 256:280], hT[:, k, at(t)], w_gn[:, k, :], start=k == 0, stop=k == KD - 1)
                    last.then_inc(b_full, 1)
                    for n in range(4):
                        last = pe.transpose(v[0:r, n * P:(n + 1) * P], uv[:, 4 + n, at(t)], ident[:])
                    last.then_inc(v_full, 1)

                turn(0)
                for t in range(NT + 1):
                    if t < NT:
                        turn(t + 1)
                    pe.wait_ge(vn_ready, t + 1)
                    pe.wait_ge(ws_kept, 2)
                    if t >= 2:
                        pe.wait_ge(s_used, t - 1)
                    if t == NT:
                        pe.wait_ge(lane_in, 16 * 64)
                        pe.wait_ge(ws_kept, 3)
                    r = rows(t)
                    for g in range(8):
                        w = wsT[:, g, :] if t < NT else wlane[:, g, :]
                        a = HD * (g % 2)
                        last = pe.matmul(ps[6 + t % 2][a:a + HD, (g // 2) * P:(g // 2) * P + r], vn[0:r, t % 2, g * HD:(g + 1) * HD], w,
                                         start=True, stop=True, skip_group_check=True)
                    last.then_inc(s_full, 1)

            @block.scalar
            def _(act):
                for t in range(NT + 1):
                    r, s = rows(t), t % 2
                    if t >= 2:
                        act.wait_ge(kv_out[s], 16 * after[t - 2])
                    act.wait_ge(a_full, t + 1)
                    act.copy(kv[0:r, s, 0:4].rearrange("p a c -> p (a c)"), ps[s][0:r, :]).then_inc(copied, 1)
                    act.wait_ge(b_full, t + 1)
                    act.copy(kv[0:r, s, 4:6].rearrange("p a c -> p (a c)"), ps[2 + s][0:r, 0:256]).then_inc(copied, 1)
                    act.activation(gates[0:r, t, :], ps[2 + s][0:r, 256:280], ACT.Sigmoid).then_inc(gates_done, 1)
                    act.wait_ge(var_ready, t + 1)
                    act.sqrt(dev[0:r, s, 0:1], dev[0:r, s, 0:1]).then_inc(v_rooted, 1)

            @block.vector
            def _(dve):
                ch = Chain(dve, chain)
                for h in range(2):
                    dve.wait_ge(ws_turned, h + 1)
                    dve.tensor_tensor(wsT[:, 4 * h:4 * h + 4, :], ps[6 + h][:].rearrange("p (g c) -> p g c", g=4),
                                      tril[:].unsqueeze(1).to_broadcast([P, 4, P]), ALU.mult).then_inc(ws_kept, 1)
                dve.wait_ge(lane_in, 16 * 64)
                dve.tensor_tensor(wlane[:], wlane[:], lane[:], ALU.mult).then_inc(ws_kept, 1)

                def layer_norm(t):
                    r, s = rows(t), t % 2
                    v = ps[4 + s][0:r, :]
                    dve.wait_ge(v_full, t + 1)
                    ch(dve.bn_stats(stat[0:r, s], v))
                    ch(dve.bn_aggr(mom[0:r, s], stat[0:r, s]))
                    dve.tensor_scalar(dev[0:r, s, 0:1], mom[0:r, s, 1:2], EPS, None, ALU.add).then_inc(var_ready, 1)
                    if t < NT:
                        dve.wait_ge(copied, 2 * t + 2)
                        dve.tensor_copy(vtok[:, t], kv[:, s, 3:6:2])
                    else:
                        dve.tensor_copy(gv[:], v).then_inc(gv_copied, 1)
                    dve.wait_ge(v_rooted, t + 1)
                    ch(dve.reciprocal(dev[0:r, s, 1:2], dev[0:r, s, 0:1]))
                    if t >= 2:
                        dve.wait_ge(s_full, t - 1)
                    dve.tensor_scalar(vn[0:r, s], v, mom[0:r, s, 0:1], dev[0:r, s, 1:2], ALU.subtract, ALU.mult).then_inc(v_kept, 1)
                    dve.wait_ge(v_kept, t + 1)
                    ch(dve.tensor_tensor(vn[0:r, s], vn[0:r, s], ln_g[0:r], ALU.mult))
                    dve.tensor_tensor(vn[0:r, s], vn[0:r, s], ln_b[0:r], ALU.add).then_inc(vn_ready, 1)

                def spatial(t):
                    r, s = rows(t), t % 2
                    dve.wait_ge(s_full, t + 1)
                    y = ps[6 + s][:].rearrange("p (a c) -> p a c", a=4)
                    if t < NT:
                        dve.tensor_tensor(sp_t[:, s], y, bias[:], ALU.add).then_inc(s_used, 1)
                    else:
                        dve.tensor_tensor(sp_t[:, s, :, 0:TS].rearrange("p a (b i) -> p a b i", b=NB),
                                          y[:, :, 0:TS].rearrange("p a (b i) -> p a b i", b=NB),
                                          bias[:, :, 0:NS].unsqueeze(2).to_broadcast([P, 4, NB, NS]), ALU.add).then_inc(s_used, 1)
                    dve.wait_ge(s_used, t + 1)
                    dve.tensor_tensor(uv[:, 0:4, at(t)], sp_t[:, s, :, 0:r], uv[:, 0:4, at(t)], ALU.mult)

                dve.wait_ge(loaded, 16 * 8)
                layer_norm(0)
                for t in range(NT + 1):
                    if t < NT:
                        layer_norm(t + 1)
                    spatial(t)


def compress(nc, i, o, sem, sb, banks, uv, ck, cv, ident):
    with ExitStack() as ctx:
        w1 = uv[:, 4:8, :].rearrange("p a t -> p (a t)")[:, 0:2 * 16 * P].rearrange("p (k j f) -> p k j f", k=2, j=16)
        w2 = sb(ctx, "w2", [P, 2, HD])
        pe_in = sb(ctx, "pe_in", [P, 2, 16])
        pe_sum = sb(ctx, "pe_sum", [P, 2])
        table = sb(ctx, "table", [1, NB * PAGES], I32)
        page = sb(ctx, "page", [P, 2, 4, 2 * P])
        pairs = sb(ctx, "pairs", [P, 2, SRC, PAIRS])
        hid = sb(ctx, "hid", [P, 2, SRC * CMP])
        ps = banks(ctx, 8)
        loaded, table_in, chain = sem("cmp_loaded"), sem("cmp_table"), sem("cmp_chain")
        page_in = [[[sem(f"page_in{k}{s}{q}") for q in range(2)] for s in range(2)] for k in range(2)]
        turned = [sem(f"pair_turned{k}") for k in range(2)]
        kept = [[sem(f"pair_kept{k}{h}") for h in range(2)] for k in range(2)]
        summed, bias_sum, bias_kept, gelu_done, out_done = (sem(f"cmp_{x}") for x in ("summed", "bsum", "bias", "gelu", "out"))
        rest_kept = sem("cmp_rest")
        halves = [(0, 5), (5, SRC)]
        pools = ("cache_cmp_k", "cache_cmp_v")

        def gather(eng, q):
            eng.wait_ge(table_in, 16)
            for k in range(2):
                rows = i[pools[k]][0].rearrange("g (p a) h d -> g p (a h d)", a=2)
                with eng.Fori(0, NB // 2) as it:
                    for s in range(2):
                        eng.wait_ge(turned[k], 4 * it + 2 * s + 2)
                        if k == 1:
                            eng.wait_ge(turned[0], 4 + 2 * SRC)
                        for j in range(q, PAGES, 2):
                            at = eng.value_load(table[0:1, bass.ds((2 * it + s) * PAGES + j, 1)], min_val=0, max_val=N_POOL - 1)
                            eng.dma_start(page[HD * q:HD * q + HD, s, j // 2],
                                          rows[bass.ds(at, 1)].rearrange("g p c -> (g p) c")).then_inc(page_in[k][s][q], 16)
                if q == 0:
                    eng.wait_ge(turned[k], 2 * NB + 2)
                    own = o[("new_cmp_k_p", "new_cmp_v_p")[k]][0, 0].rearrange("(j p a) h d -> p j (a h d)", a=2, p=P)
                    eng.dma_start(page[:, 0], own).then_inc(page_in[k][0][0], 16)

        with nc.Block() as block:
            @block.sync
            def _(sp):
                sp.dma_start(table[:], i["page_table"].rearrange("(o b) j -> o (b j)", o=1)).then_inc(table_in, 16)
                for k in range(2):
                    sp.dma_start(w1[:, k], i["cmp_w1"][0, k].rearrange("(j a) d f -> (a d) j f", a=2)).then_inc(loaded, 16)
                    sp.dma_start(pe_in[:, k], i["cmp_pe"][0, k].rearrange("(j a) d -> (a d) j", a=2)).then_inc(loaded, 16)
                sp.dma_start(w2[:], i["cmp_w2"][0].rearrange("k f d -> f k d")).then_inc(loaded, 16)
                gather(sp, 0)

            @block.gpsimd
            def _(pool):
                gather(pool, 1)

            @block.tensor
            def _(pe):
                def turn(k, s):
                    for a in range(2):
                        for j in range(4):
                            last = pe.transpose(ps[2 * a + s][:, j * P:(j + 1) * P], page[:, s, j, P * a:P * a + P], ident[:])
                        last.then_inc(turned[k], 1)

                for k in range(2):
                    pe.sem_inc(turned[k], 4)
                    with pe.Fori(0, NB // 2) as it:
                        for s in range(2):
                            for q in range(2):
                                pe.wait_ge(page_in[k][s][q], 8 * PAGES * it + 8 * PAGES)
                            pe.wait_ge(kept[k][0], 2 * it + s + 1)
                            pe.wait_ge(kept[k][1], 2 * it + s + 1)
                            turn(k, s)
                    pe.wait_ge(page_in[k][0][0], 8 * PAGES * 4 + 16)
                    pe.wait_ge(kept[k][0], NB + 1)
                    pe.wait_ge(kept[k][1], NB + 1)
                    turn(k, 0)
                    pe.wait_ge(kept[k][0], SRC + 2)
                    pe.wait_ge(kept[k][1], SRC + 2)
                    if k == 0:
                        pe.wait_ge(loaded, 16 * 5)
                        for kk in range(2):
                            for j in range(16):
                                last = pe.matmul(ps[4][:, kk:kk + 1], w1[:, kk, j], pe_in[:, kk, j:j + 1], start=j == 0, stop=j == 15)
                        last.then_inc(bias_sum, 1)
                        pe.wait_ge(bias_kept, 1)
                    for h in range(2):
                        for n, (b0, b1) in enumerate(halves):
                            if k == 1:
                                pe.wait_ge(gelu_done, 2 * h + n + 1)
                            for j in range(16):
                                last = pe.matmul(ps[4 + 2 * h + n][:, 0:(b1 - b0) * CMP], w1[:, k, j],
                                                 pairs[:, h, b0:b1, j:j + 8 * (CMP - 1) + 1:8], start=j == 0, stop=j == 15)
                            last.then_inc(summed, 1)
                    pe.wait_ge(gelu_done, 4 * k + 4)
                    if k == 0:
                        for h in range(2):
                            for n, (b0, b1) in enumerate(halves):
                                last = pe.matmul(ps[n][HD * h:HD * h + HD, 0:(b1 - b0) * CMP], w2[:, 0], hid[:, h, b0 * CMP:b1 * CMP],
                                                 start=True, stop=True, skip_group_check=True)
                        last.then_inc(out_done, 1)
                        pe.wait_ge(rest_kept, 2)
                    else:
                        for b in range(SRC):
                            for h in range(2):
                                at = P * (b % 4) + HD * h
                                last = pe.matmul(ps[b // 4][0:CMP, at:at + HD], hid[:, h, b * CMP:(b + 1) * CMP], w2[:, 1],
                                                 start=True, stop=True, skip_group_check=True)
                        last.then_inc(out_done, 1)

            def keep(eng, h, copy):
                for k in range(2):
                    eng.sem_inc(kept[k][h], 2)
                    with eng.Fori(0, NB // 2) as it:
                        for s in range(2):
                            eng.wait_ge(turned[k], 4 * it + 2 * s + h + 5)
                            for hh in range(2):
                                last = copy(pairs[HD * h:HD * h + HD, hh, bass.ds(2 * it + s, 1), :].rearrange("p a t -> p (a t)"),
                                            ps[2 * h + s][HD * hh:HD * hh + HD, :])
                            last.then_inc(kept[k][h], 1)
                    eng.wait_ge(turned[k], 2 * NB + h + 5)
                    for hh in range(2):
                        last = copy(pairs[HD * h:HD * h + HD, hh, NB, :], ps[2 * h][HD * hh:HD * hh + HD, :])
                    last.then_inc(kept[k][h], 1)
                    if h == 0:
                        if k == 0:
                            eng.wait_ge(bias_kept, 1)
                        for hh in range(2):
                            for n, (b0, b1) in enumerate(halves):
                                eng.wait_ge(summed, 4 * k + 2 * hh + n + 1)
                                if k == 1 and hh == 0 and n == 0:
                                    eng.wait_ge(out_done, 1)
                                eng.activation(hid[:, hh, b0 * CMP:b1 * CMP], ps[4 + 2 * hh + n][:, 0:(b1 - b0) * CMP],
                                               ACT.Gelu_apprx_tanh, bias=pe_sum[:, k:k + 1]).then_inc(gelu_done, 1)
                    elif k == 0:
                        eng.wait_ge(bias_sum, 1)
                        eng.tensor_copy(pe_sum[:], ps[4][:, 0:2]).then_inc(bias_kept, 1)
                        eng.wait_ge(out_done, 1)
                        for n, (b0, b1) in enumerate(halves):
                            eng.tensor_copy(ck[:, b0:b1, :].rearrange("p b n -> p (b n)"), ps[n][:, 0:(b1 - b0) * CMP]).then_inc(rest_kept, 1)

            @block.scalar
            def _(act):
                keep(act, 0, act.copy)

            @block.vector
            def _(dve):
                keep(dve, 1, dve.tensor_copy)
                dve.wait_ge(out_done, 2)
                for n in range(3):
                    b0, b1 = 4 * n, min(4 * n + 4, SRC)
                    dve.tensor_copy(cv[:, b0:b1, :].rearrange("p b c -> p (b c)"), ps[n][0:CMP, 0:(b1 - b0) * P])


def attend_prompt(nc, i, sem, sb, banks, qk, vtok, gates, ck, cv, oT, ident):
    BOTH = 2 * CMP
    with ExitStack() as ctx:
        diag = sb(ctx, "diag", [P, P])
        far = sb(ctx, "far", [P, P])
        seen = sb(ctx, "seen", [P, NT, CMP])
        hidden = sb(ctx, "hidden", [P, NT, CMP])
        ck_both = sb(ctx, "ck_both", [P, BOTH])
        cv_both = sb(ctx, "cv_both", [BOTH, P])
        cs = sb(ctx, "cs", [P, 8, CMP])
        probs = sb(ctx, "probs", [P, 2, NP])
        turned = sb(ctx, "turned", [P, 2, 8, P])
        c_turned = sb(ctx, "c_turned", [BOTH, 2, G, P])
        scale = sb(ctx, "scale", [P, 2, P])
        factor = sb(ctx, "factor", [P, 4])
        mx = sb(ctx, "mx", [P, 4])
        cmx = sb(ctx, "cmx", [P, 8])
        total = sb(ctx, "total", [P, 4])
        ctotal = sb(ctx, "ctotal", [P, 8])
        ps = banks(ctx, 4)
        wide = [ctx.enter_context(nc.psum_tensor(f"scores{k}", [P, 1024], F32)) for k in range(2)]
        loaded, cleared, both_ready, cv_in = sem("mask_in"), sem("at_cleared"), sem("at_ck_both"), sem("at_cv_both")
        score, peak, expd, shown, pt, pv = (sem(f"at_{x}") for x in ("score", "peak", "exp", "shown", "pt", "pv"))
        pt_free = [sem(f"at_pt_free{k}") for k in range(2)]
        chain, divided, scaled, out_kept = sem("at_chain"), sem("at_divided"), sem("at_scaled"), sem("at_out_kept")
        units = [(t, None, None, "cmp") if n < 0 else (t, n // 4, n // 2 % 2, ("sel", "win")[n % 2])
                 for t in range(NT) for n in range(-1, 16)]

        def blocks(u):
            t, _, _, kind = units[u]
            return G if kind == "cmp" else t + 1 if kind == "sel" else min(t + 1, 5)

        def heads_done(u):
            return u + 1 - (u // 17 + 1)

        def last_of_group(u):
            _, _, h, kind = units[u]
            return kind == "win" and h == 1

        first_group = [0]
        for u in range(len(units)):
            first_group.append(first_group[u] + -(-blocks(u) // 4))

        def group_list(u):
            return [(n, 4 * j, min(4 * j + 4, blocks(u))) for j, n in enumerate(range(first_group[u], first_group[u + 1]))]

        with nc.Block() as block:
            @block.sync
            def _(sp):
                for dst, name in ((diag, "c_diag"), (far, "c_far"), (seen, "c_seen"), (hidden, "c_hidden")):
                    sp.dma_start(dst[:], i[name]).then_inc(loaded, 16)
                sp.wait_ge(cleared, 2)
                for h in range(2):
                    sp.dma_start(cv_both[CMP * h:CMP * h + CMP, HD * h:HD * h + HD], cv[:, NB, HD * h:HD * h + HD]).then_inc(cv_in, 16)

            @block.gpsimd
            def _(pool):
                pool.memset(ck_both[:], 0.0).then_inc(cleared, 1)
                pool.memset(cv_both[:], 0.0).then_inc(cleared, 1)
                pool.wait_ge(cleared, 2)
                for h in range(2):
                    pool.tensor_copy(ck_both[HD * h:HD * h + HD, CMP * h:CMP * h + CMP], ck[HD * h:HD * h + HD, NB, :]).then_inc(both_ready, 1)
                for u, (t, g, h, kind) in enumerate(units):
                    if kind == "cmp":
                        continue
                    j = 3 * (4 * h + g) + (1 if kind == "sel" else 2)
                    pool.wait_ge(divided, heads_done(u))
                    if u >= 2:
                        pool.wait_ge(pt, first_group[u - 1])
                    pool.tensor_scalar(scale[:, u % 2], ident[:], factor[:, u % 4:u % 4 + 1], gates[:, t, j:j + 1], ALU.mult, ALU.mult).then_inc(scaled, 1)

            @block.tensor
            def _(pe):
                def scores(u):
                    t, g, h, kind = units[u]
                    s = wide[u % 2]
                    if u >= 2:
                        pe.wait_ge(expd, u - 1)
                    qt = slice(t * P, t * P + P)
                    if kind == "cmp":
                        for gg in range(G):
                            last = pe.matmul(s[:, gg * BOTH:(gg + 1) * BOTH], qk[:, gg, qt], ck_both[:], start=True, stop=True)
                    else:
                        at = slice(HD * h, HD * h + HD)
                        tile = 6 if kind == "sel" else 8
                        k0 = 0 if kind == "sel" else max(t - 4, 0) * P
                        n = blocks(u) * P
                        for c in range(0, n, 512):
                            w = min(512, n - c)
                            last = pe.matmul(s[:, c:c + w], qk[at, g, qt], qk[at, tile, k0 + c:k0 + c + w], start=True, stop=True)
                    last.then_inc(score, 1)

                def turn(u):
                    t, _, _, kind = units[u]
                    if kind == "cmp":
                        pe.wait_ge(shown, t + 1)
                    else:
                        pe.wait_ge(scaled, heads_done(u))
                    for n, b0, b1 in group_list(u):
                        if n >= 2:
                            pe.wait_ge(pt_free[n % 2], n // 2)
                        for b in range(b0, b1):
                            at = slice((b - b0) * P, (b - b0 + 1) * P)
                            if kind == "cmp":
                                last = pe.transpose(ps[n % 2][0:BOTH, at], probs[:, u % 2, b * BOTH:(b + 1) * BOTH], ident[:])
                            else:
                                last = pe.matmul(ps[n % 2][:, at], probs[:, u % 2, b * P:(b + 1) * P], scale[:, u % 2], start=True, stop=True)
                        last.then_inc(pt, 1)

                def values(u):
                    t, g, h, kind = units[u]
                    if kind == "cmp":
                        return
                    out = ps[2 + g % 2]
                    if kind == "sel" and h == 0:
                        if t or g >= 2:
                            pe.wait_ge(out_kept, G * t + g - 1)
                        if g == 0:
                            n = first_group[17 * t]
                            pe.wait_ge(pt_free[n % 2], n // 2 + 1)
                        pe.matmul(out[:, 0:P], cv_both[:], c_turned[:, t % 2, g], start=True, stop=False, skip_group_check=True)
                    k0 = 0 if kind == "sel" else max(t - 4, 0)
                    for n, b0, b1 in group_list(u):
                        pe.wait_ge(pt_free[n % 2], n // 2 + 1)
                        for b in range(b0, b1):
                            last = pe.matmul(out[HD * h:HD * h + HD, 0:P], vtok[:, k0 + b, int(kind == "win"), HD * h:HD * h + HD], turned[:, u % 2, b],
                                             start=False, stop=last_of_group(u) and b == blocks(u) - 1, tile_position=(0, HD * h),
                                             skip_group_check=True)
                    last.then_inc(pv, 1)

                pe.wait_ge(loaded, 64)
                pe.wait_ge(both_ready, 2)
                scores(0)
                pe.wait_ge(cv_in, 32)
                for u in range(len(units)):
                    if u + 1 < len(units):
                        scores(u + 1)
                    turn(u)
                    if u > 0:
                        values(u - 1)
                values(len(units) - 1)

            def empty(eng, copy, which, u):
                for n, b0, b1 in group_list(u):
                    if n % 2 == which:
                        eng.wait_ge(pt, n + 1)
                        if u >= 3:
                            eng.wait_ge(pv, heads_done(u - 2))
                        if units[u][3] == "cmp":
                            dst, r = c_turned[:, units[u][0] % 2], BOTH
                        else:
                            dst, r = turned[:, u % 2, b0:b1, :], P
                        copy(dst.rearrange("p b c -> p (b c)"), ps[n % 2][0:r, 0:(b1 - b0) * P]).then_inc(pt_free[which], 1)

            @block.scalar
            def _(act):
                def exp(u):
                    act.wait_ge(peak, u + 1)
                    if u >= 2:
                        act.wait_ge(pt, first_group[u - 1])
                    if units[u][3] == "cmp":
                        act.activation(probs[:, u % 2, 0:8 * CMP], cs[:].rearrange("p h n -> p (h n)"), ACT.Exp).then_inc(expd, 1)
                    else:
                        n = blocks(u) * P
                        act.activation(probs[:, u % 2, 0:n], wide[u % 2][:, 0:n], ACT.Exp, bias=mx[:, u % 4:u % 4 + 1],
                                       accum_out=total[:, u % 4:u % 4 + 1]).then_inc(expd, 1)

                def keep(u):
                    t, g, _, _ = units[u]
                    act.wait_ge(pv, heads_done(u))
                    act.copy(oT[:, g, t * P:(t + 1) * P], ps[2 + g % 2][:, 0:P]).then_inc(out_kept, 1)

                exp(0)
                for u in range(len(units)):
                    empty(act, act.copy, 1, u)
                    if u + 1 < len(units):
                        exp(u + 1)
                    if u > 0 and last_of_group(u - 1):
                        keep(u - 1)
                keep(len(units) - 1)

            @block.vector
            def _(dve):
                ch = Chain(dve, chain)

                def peaks(u):
                    t, _, _, kind = units[u]
                    s = wide[u % 2]
                    dve.wait_ge(score, u + 1)
                    if kind == "cmp":
                        ch(dve.tensor_tensor(cs[:], s[:, 0:8 * CMP].rearrange("p (h n) -> p h n", h=8),
                                             hidden[:, t].unsqueeze(1).to_broadcast([P, 8, CMP]), ALU.add))
                        ch(dve.tensor_reduce(cmx[:], cs[:], X, ALU.max))
                        dve.tensor_tensor(cs[:], cs[:], cmx[:].unsqueeze(2).to_broadcast([P, 8, CMP]), ALU.subtract).then_inc(peak, 1)
                        return
                    n = blocks(u) * P
                    ch(dve.tensor_tensor(s[:, n - P:n], s[:, n - P:n], diag[:], ALU.add))
                    if kind == "win" and t >= 4:
                        ch(dve.tensor_tensor(s[:, 0:P], s[:, 0:P], far[:], ALU.add))
                    dve.tensor_reduce(mx[:, u % 4:u % 4 + 1], s[:, 0:n], X, ALU.max, negate=True).then_inc(peak, 1)

                def show(u):
                    t = units[u][0]
                    p = probs[:, u % 2, 0:8 * CMP].rearrange("p (h n) -> p h n", h=8)
                    dve.wait_ge(expd, u + 1)
                    ch(dve.tensor_tensor(p, p, seen[:, t].unsqueeze(1).to_broadcast([P, 8, CMP]), ALU.mult))
                    ch(dve.tensor_reduce(ctotal[:], p, X, ALU.add))
                    ch(dve.tensor_scalar(ctotal[:], ctotal[:], 1e-30, None, ALU.max))
                    ch(dve.reciprocal(ctotal[:], ctotal[:]))
                    gate = gates[:, t, :].rearrange("p (h g j) -> p g h j", h=2, g=4)[:, :, :, 0]
                    ch(dve.tensor_tensor(ctotal[:].rearrange("p (g h) -> p g h", g=4), ctotal[:].rearrange("p (g h) -> p g h", g=4), gate, ALU.mult))
                    dve.tensor_tensor(p, p, ctotal[:].unsqueeze(2).to_broadcast([P, 8, CMP]), ALU.mult).then_inc(shown, 1)

                dve.wait_ge(loaded, 64)
                peaks(0)
                for u in range(len(units)):
                    if units[u][3] == "cmp":
                        show(u)
                    else:
                        dve.wait_ge(expd, u + 1)
                        dve.reciprocal(factor[:, u % 4:u % 4 + 1], total[:, u % 4:u % 4 + 1]).then_inc(divided, 1)
                    if u + 1 < len(units):
                        peaks(u + 1)
                    empty(dve, dve.tensor_copy, 0, u)


def attend_sample(nc, i, o, sem, sb, banks, qk, uv, gates, ck, cv, oT, ident):
    SEL, WINC = 0, 1532
    CMPC, ROWG, SC0, SC1 = 0, 64, 96, 112
    PS_, PW, PC = 0, 1028, 1544
    with ExitStack() as ctx:
        ring = uv[:, 4:8, :].rearrange("p a t -> p (a t)")[:, 0:2 * 12 * P].rearrange("p (s j c) -> p s j c", s=2, j=12)
        probs = qk[:, 4:6, :].rearrange("p a t -> p (a t)")
        table = sb(ctx, "table_s", [1, NB * PAGES], I32)
        kT = sb(ctx, "kT", [P, 2, 12 * P])
        pT = sb(ctx, "pT", [P, 16, P])
        q_rows = sb(ctx, "q_rows", [P, NB, 32])
        v_new = sb(ctx, "v_new", [NS, 2, NB, P])
        same = sb(ctx, "same", [P, P])
        shared = sb(ctx, "shared", [CMP, 16])
        new = sb(ctx, "new", [P, NS])
        old = sb(ctx, "old", [P, NS])
        row_of = sb(ctx, "row_of", [TS, 2, P])
        hg = sb(ctx, "hg", [P, 24])
        block_no = sb(ctx, "block_no", [P, 16])
        small = sb(ctx, "small", [P, 8, 24])
        one = sb(ctx, "one", [P, 12])
        wide = ctx.enter_context(nc.psum_tensor("s_wide", [P, 2048], F32))
        tp = banks(ctx, 2)
        out, misc = banks(ctx, 2)
        loaded, table_in, zeroed, q_ready = sem("sa_loaded"), sem("sa_table"), sem("sa_zeroed"), sem("sa_q")
        ring_in = [[sem(f"sa_ring{s}{q}") for q in range(2)] for s in range(2)]
        turned, score, pv = (sem(f"sa_{x}") for x in ("turned", "score", "pv"))
        kept = [sem(f"sa_kept{k}") for k in range(2)]
        chain, ready, expd, cmp_p, probs_ready, summed, small_mm = (sem(f"sa_{x}") for x in ("chain", "ready", "exp", "cmp_p", "probs", "summed", "mm"))
        small_kept = sem("sa_small_kept")
        per = 12 + 1 + 4

        def gather(eng, q):
            eng.wait_ge(table_in, 16)
            for grp in range(2):
                for v, (pool, state) in enumerate((("cache_slc_k", "state_win_k"), ("cache_slc_v", "state_win_v"))):
                    pages = i[pool][0].rearrange("g p h d -> g p (h d)")
                    for bb in range(4):
                        b, s = 4 * grp + bb, bb % 2
                        if bb >= 2 and v == 0:
                            eng.wait_ge(turned, per * grp + 3 * bb - 3)
                        elif bb >= 2:
                            eng.wait_ge(pv, b - 1)
                        elif v == 1:
                            eng.wait_ge(turned, per * grp + 3 * bb + 9)
                        elif grp > 0:
                            eng.wait_ge(pv, b - 1)
                        with eng.Fori(0, PAGES // 2) as j:
                            at = eng.value_load(table[0:1, bass.ds(2 * j + (b * PAGES + q), 1)], min_val=0, max_val=N_POOL - 1)
                            eng.dma_start(ring[:, s, bass.ds(2 * j + q, 1)].rearrange("p j c -> p (j c)"),
                                          pages[bass.ds(at, 1)].rearrange("g p c -> (g p) c")).then_inc(ring_in[s][q], 16)
                        eng.dma_start(ring[:, s, 8 + 2 * q:10 + 2 * q],
                                      i[state][0, b, 2 * P * q:2 * P * q + 2 * P].rearrange("(j p) h d -> p j (h d)", p=P)).then_inc(ring_in[s][q], 16)

        with nc.Block() as block:
            @block.sync
            def _(sp):
                sp.dma_start(table[:], i["page_table"].rearrange("(o b) j -> o (b j)", o=1)).then_inc(table_in, 16)
                for dst, name in ((same, "c_same"), (shared, "c_shared"), (new, "c_new"), (old, "c_old"), (row_of, "c_row_of"),
                                  (hg, "c_hg"), (block_no, "c_block")):
                    src = i[name].rearrange("p x j -> p (x j)") if name == "c_hg" else i[name]
                    sp.dma_start(dst[:], src).then_inc(loaded, 16)
                sp.dma_start(v_new[:, 0], o["new_slc_v_s"][0].rearrange("b s h d -> s b (h d)")).then_inc(loaded, 16)
                sp.dma_start(v_new[:, 1], o["new_win_v_s"][0, :, WIN - NS:WIN].rearrange("b s h d -> s b (h d)")).then_inc(loaded, 16)
                gather(sp, 0)

            @block.gpsimd
            def _(pool):
                pool.memset(q_rows[:], 0.0).then_inc(zeroed, 1)
                gather(pool, 1)

            def arrived(pe, load):
                for q in range(2):
                    pe.wait_ge(ring_in[load % 2][q], 16 * 5 * (load // 2 + 1))

            @block.tensor
            def _(pe):
                pe.wait_ge(loaded, 16 * 9)
                pe.wait_ge(q_ready, 2)

                def room(n):
                    if n >= 2:
                        pe.wait_ge(kept[n % 2], n // 2)

                def turn_keys(b):
                    grp, bb = b // 4, b % 4
                    load = 8 * grp + bb
                    arrived(pe, load)
                    for j in range(3):
                        n = per * grp + 3 * bb + j
                        room(n)
                        for m in range(4):
                            last = pe.transpose(tp[n % 2][:, m * P:(m + 1) * P], ring[:, load % 2, 4 * j + m, :], ident[:])
                        last.then_inc(turned, 1)

                def scores(b):
                    grp, bb = b // 4, b % 4
                    for j in range(3):
                        n = per * grp + 3 * bb + j
                        pe.wait_ge(kept[n % 2], n // 2 + 1)
                    if bb == 0 and grp > 0:
                        pe.wait_ge(expd, 3 * grp)
                    q = q_rows[:, b, :]
                    r = slice(32 * bb, 32 * bb + 32)
                    k, new_k = kT[:, b % 2], slice(NP + NS * b, NP + NS * b + NS)
                    for at, rhs in ((CMPC, ck[:, b, :]), (0, k[:, 0:512]), (512, k[:, 512:1024]), (1024, qk[:, 6, new_k]),
                                    (WINC, qk[:, 8, new_k]), (1536, k[:, 1024:1536])):
                        to = misc if rhs.shape[-1] == CMP else wide
                        last = pe.matmul(to[r, at:at + rhs.shape[-1]], q, rhs, start=True, stop=True, skip_group_check=True,
                                         tile_position=(0, 32 * bb))
                    last.then_inc(score, 1)

                def group(n, blocks):
                    room(n)
                    for m, (at, w) in enumerate(blocks):
                        last = pe.transpose(tp[n % 2][0:w, m * P:(m + 1) * P], probs[:, at:at + w], ident[:])
                    last.then_inc(turned, 1)

                for grp in range(2):
                    b0, n0 = 4 * grp, per * grp
                    pe.matmul(misc[:, ROWG:ROWG + 24], row_of[:, grp], gates[0:TS, NT, :], start=True, stop=True,
                              skip_group_check=True).then_inc(small_mm, 1) if grp == 0 else None
                    turn_keys(b0)
                    for b in range(b0, b0 + 4):
                        if b < b0 + 3:
                            turn_keys(b + 1)
                        scores(b)
                    if grp == 1:
                        pe.matmul(misc[:, ROWG:ROWG + 24], row_of[:, grp], gates[0:TS, NT, :], start=True, stop=True,
                                  skip_group_check=True).then_inc(small_mm, 1)
                    pe.wait_ge(cmp_p, grp + 1)
                    group(n0 + 12, [(PC, CMP)])
                    pe.wait_ge(kept[(n0 + 12) % 2], (n0 + 12) // 2 + 1)
                    pe.matmul(misc[:, SC0:SC0 + 16], pT[0:CMP, 15], shared[:], start=True, stop=True, skip_group_check=True).then_inc(small_mm, 1)
                    pe.wait_ge(small_kept, grp + 1)
                    pe.matmul(misc[:, SC1:SC1 + 16], same[:], small[:, 3, 0:16], start=True, stop=True, skip_group_check=True).then_inc(small_mm, 1)
                    pe.wait_ge(probs_ready, grp + 1)
                    group(n0 + 13, [(PS_ + m * P, P) for m in range(4)])
                    group(n0 + 14, [(PS_ + m * P, P) for m in range(4, 8)])
                    group(n0 + 15, [(PW + NS + m * P, P) for m in range(4)])
                    group(n0 + 16, [(PS_ + NP, NS), (PW, NS), (PC, CMP)])
                    for n in range(n0 + 13, n0 + 17):
                        pe.wait_ge(kept[n % 2], n // 2 + 1)
                    for b in range(b0, b0 + 4):
                        load = 8 * grp + 4 + b % 4
                        arrived(pe, load)
                        r = slice(32 * (b % 4), 32 * (b % 4) + 32)
                        v = ring[:, load % 2]
                        terms = [(v[:, j], pT[:, j, r]) for j in range(12)]
                        terms += [(v_new[:, 0, b], pT[0:NS, 12, r]), (v_new[:, 1, b], pT[0:NS, 13, r]), (cv[:, b], pT[0:CMP, 14, r])]
                        for m, (lhsT, rhs) in enumerate(terms):
                            last = pe.matmul(out[:, 32 * b:32 * b + 32], lhsT, rhs, start=m == 0, stop=m == len(terms) - 1,
                                             skip_group_check=True)
                        last.then_inc(pv, 1)

            def keep(eng, copy, which, grp, ns):
                for n in ns:
                    if n % 2 != which:
                        continue
                    eng.wait_ge(turned, n + 1)
                    m = n - per * grp
                    src = tp[n % 2]
                    if m < 12:
                        b = 4 * grp + m // 3
                        if b >= 2:
                            eng.wait_ge(score, b - 1)
                        copy(kT[:, b % 2, 512 * (m % 3):512 * (m % 3) + 512], src[:]).then_inc(kept[which], 1)
                    elif m == 12:
                        copy(pT[0:CMP, 15], src[0:CMP, 0:P]).then_inc(kept[which], 1)
                    elif m < 16:
                        copy(pT[:, 4 * (m - 13):4 * (m - 13) + 4, :].rearrange("p b c -> p (b c)"), src[:]).then_inc(kept[which], 1)
                    else:
                        copy(pT[0:NS, 12:14].rearrange("p b c -> p (b c)"), src[0:NS, 0:2 * P])
                        copy(pT[0:CMP, 14], src[0:CMP, 2 * P:3 * P]).then_inc(kept[which], 1)

            @block.scalar
            def _(act):
                def exp(src, at, n, col):
                    act.activation(probs[:, at:at + n], (wide if col else misc)[:, src:src + n], ACT.Exp, bias=one[:, col:col + 1],
                                   accum_out=one[:, 5 + col:6 + col]).then_inc(expd, 1)

                for grp in range(2):
                    n0 = per * grp
                    keep(act, act.copy, 1, grp, range(n0, n0 + 12))
                    act.wait_ge(ready, 3 * grp + 1)
                    exp(CMPC, PC, CMP, 0)
                    keep(act, act.copy, 1, grp, [n0 + 12])
                    act.wait_ge(ready, 3 * grp + 3)
                    exp(SEL, PS_, NP + NS, 1)
                    exp(WINC, PW, WIN + NS, 2)
                    keep(act, act.copy, 1, grp, range(n0 + 13, n0 + 17))

            @block.vector
            def _(dve):
                ch = Chain(dve, chain)
                dve.wait_ge(zeroed, 1)
                for h in range(2):
                    r = slice(HD * h, HD * h + HD)
                    dve.tensor_copy(q_rows[r, :, 16 * h:16 * h + 16].rearrange("p b (g s) -> p g b s", g=4),
                                    qk[r, 0:4, NP:T].rearrange("p g (b s) -> p g b s", b=NB)).then_inc(q_ready, 1)
                dve.wait_ge(loaded, 16 * 9)
                for grp in range(2):
                    n0 = per * grp
                    mm = 3 * grp
                    keep(dve, dve.tensor_copy, 0, grp, range(n0, n0 + 12))
                    dve.wait_ge(score, 4 * grp + 4)
                    dve.wait_ge(small_mm, mm + 1)
                    ch(dve.tensor_tensor(small[:, 0], misc[:, ROWG:ROWG + 24], hg[:], ALU.mult))
                    ch(dve.tensor_reduce(small[:, 1, 0:3], small[:, 0].rearrange("p (x j) -> p j x", j=3), X, ALU.add))
                    dve.tensor_reduce(one[:, 0:1], misc[:, CMPC:CMPC + CMP], X, ALU.max, negate=True).then_inc(ready, 1)
                    ch(dve.tensor_tensor(wide[:, NP:NP + NS], wide[:, NP:NP + NS], new[:], ALU.add))
                    ch(dve.tensor_tensor(wide[:, WINC:WINC + NS], wide[:, WINC:WINC + NS], new[:], ALU.add))
                    ch(dve.tensor_tensor(wide[:, 1536:1536 + NS], wide[:, 1536:1536 + NS], old[:], ALU.add))
                    dve.tensor_reduce(one[:, 2:3], wide[:, WINC:2048], X, ALU.max, negate=True).then_inc(ready, 1)
                    dve.wait_ge(expd, 3 * grp + 1)
                    ch(dve.reciprocal(one[:, 10:11], one[:, 5:6]))
                    dve.tensor_scalar(probs[:, PC:PC + CMP], probs[:, PC:PC + CMP], one[:, 10:11], None, ALU.mult).then_inc(cmp_p, 1)
                    keep(dve, dve.tensor_copy, 0, grp, [n0 + 12])
                    dve.wait_ge(small_mm, mm + 2)
                    dve.tensor_copy(small[:, 3, 0:16], misc[:, SC0:SC0 + 16]).then_inc(small_kept, 1)
                    dve.wait_ge(small_mm, mm + 3)
                    ch(dve.tensor_copy(small[:, 4, 0:16], misc[:, SC1:SC1 + 16]))
                    ch(dve.tensor_reduce(one[:, 3:4], small[:, 4, 1:15], X, ALU.min))
                    ch(dve.tensor_scalar(small[:, 5, 1:15], small[:, 4, 1:15], one[:, 3:4], None, ALU.is_equal))
                    ch(dve.tensor_tensor(small[:, 5, 1:15], small[:, 5, 1:15], block_no[:, 1:15], ALU.mult))
                    ch(dve.tensor_reduce(one[:, 4:5], small[:, 5, 1:15], X, ALU.max))
                    ch(dve.tensor_scalar(small[:, 6, 0:16], block_no[:], one[:, 4:5], NEG, ALU.is_equal, ALU.mult))
                    sel = wide[:, 0:NP].rearrange("p (m c) -> p m c", m=16)
                    ch(dve.tensor_tensor(sel, sel, small[:, 6, 0:16].unsqueeze(2).to_broadcast([P, 16, HD]), ALU.add))
                    dve.tensor_reduce(one[:, 1:2], wide[:, 0:NP + NS], X, ALU.max, negate=True).then_inc(ready, 1)
                    dve.tensor_scalar(probs[:, PC:PC + CMP], probs[:, PC:PC + CMP], small[:, 1, 0:1], None, ALU.mult)
                    dve.wait_ge(expd, 3 * grp + 3)
                    ch(dve.reciprocal(one[:, 10:12], one[:, 6:8]))
                    dve.tensor_scalar(probs[:, 0:PW], probs[:, 0:PW], one[:, 10:11], small[:, 1, 1:2], ALU.mult, ALU.mult)
                    dve.tensor_scalar(probs[:, PW:PC], probs[:, PW:PC], one[:, 11:12], small[:, 1, 2:3], ALU.mult, ALU.mult).then_inc(probs_ready, 1)
                    keep(dve, dve.tensor_copy, 0, grp, range(n0 + 13, n0 + 17))
                dve.wait_ge(pv, NB)
                for h in range(2):
                    r = slice(HD * h, HD * h + HD)
                    dve.tensor_copy(oT[r, :, NP:T].rearrange("p g (b s) -> p g b s", b=NB),
                                    out[r, 0:256].rearrange("p (b x) -> p b x", b=NB)[:, :, 16 * h:16 * h + 16].rearrange("p b (g s) -> p g b s", g=4))


def merge(nc, i, sem, sb, banks, hT, oT, uv, qk):
    w = i["w_in"][0].rearrange("(k p) n -> p k n", p=P)
    wa = i["w_branch_a"][0].rearrange("(h g d) n -> h d g n", h=2, g=4)
    wb = i["w_branch_b"][0].rearrange("(k p) n -> p k n", p=P)
    with ExitStack() as ctx:
        slots = sb(ctx, "mg_w", [P, 2, 24, P])
        free = uv[:, 4:8, :].rearrange("p a t -> p (a t)")
        sg = free[:, 0:4 * C].rearrange("p (b m t) -> p b m t", b=2, m=2)
        prod = free[:, 4 * C:8 * C].rearrange("p (b m t) -> p b m t", b=2, m=2)
        ps = banks(ctx, 8)
        st = Stream(sem, "mg", 8, 2, loads=5)
        gated, chain = sem("mg_gated"), sem("mg_chain")
        with nc.Block() as block:
            @block.sync
            def _(sp):
                st.load(sp, lambda n, s: [
                    (slots[:, s, 0:8], w[:, :, bass.ds(GA_COL + n * P, P)]),
                    (slots[:, s, 8:16], w[:, :, bass.ds(GB_COL + n * P, P)]),
                    (slots[0:HD, s, 16:20], wa[0, :, :, bass.ds(n * P, P)]),
                    (slots[HD:P, s, 16:20], wa[1, :, :, bass.ds(n * P, P)]),
                    (slots[:, s, 20:24], wb[:, :, bass.ds(n * P, P)])])

            @block.tensor
            def _(pe):
                st.multiply(pe, lambda b, s, c: [
                    (ps[4 * b][:, 0:C], [(slots[:, s, k], hT[:, k, cols(c)]) for k in range(8)]),
                    (ps[4 * b + 1][:, 0:C], [(slots[:, s, 8 + k], hT[:, k, cols(c)]) for k in range(8)]),
                    (ps[4 * b + 2][:, 0:C], [(slots[:, s, 16 + k], oT[:, k, cols(c)]) for k in range(4)]),
                    (ps[4 * b + 3][:, 0:C], [(slots[:, s, 20 + k], uv[:, k, cols(c)]) for k in range(4)])])

            @block.scalar
            def _(act):
                with act.Fori(0, 4) as it:
                    for j in range(6):
                        act.wait_ge(st.done, 6 * it + j + 7)
                        act.wait_ge(chain, 18 * it + 3 * j + 3)
                        for m in range(2):
                            last = act.activation(sg[:, j % 2, m], ps[4 * (j % 2) + m][:, 0:C], ACT.Sigmoid)
                        last.then_inc(gated, 1)

            @block.vector
            def _(dve):
                dve.sem_inc(st.freed, 2)
                dve.sem_inc(chain, 6)
                with dve.Fori(0, 4) as it:
                    for j in range(6):
                        b = j % 2
                        dve.wait_ge(gated, 6 * it + j + 1)
                        dve.wait_ge(chain, 18 * it + 3 * j + 3)
                        dve.tensor_tensor(prod[:, b, 0], sg[:, b, 0], ps[4 * b + 2][:, 0:C], ALU.mult).then_inc(chain, 1)
                        dve.tensor_tensor(prod[:, b, 1], sg[:, b, 1], ps[4 * b + 3][:, 0:C], ALU.mult).then_inc(chain, 1)
                        dve.wait_ge(chain, 18 * it + 3 * j + 8)
                        dve.sem_inc(st.freed, 1)
                        dve.tensor_tensor(qk[:, bass.ds(2 * it + j // 3, 1), cols(j % 3)].rearrange("p a t -> p (a t)"),
                                          prod[:, b, 0], prod[:, b, 1], ALU.add).then_inc(chain, 1)


def add_product(nc, name, sem, sb, banks, w, src, hi, lo, xT):
    w = w.rearrange("(k p) n -> p k n", p=P)
    with ExitStack() as ctx:
        ps = banks(ctx, 6)
        st = SplitStream(sb, sem, ctx, name, KD, 6)
        rounded, split = sem(f"{name}_x_rounded"), sem(f"{name}_x_split")
        with nc.Block() as block:
            @block.sync
            def _(sp):
                st.load(sp, 0, KD, lambda n, raw: halves(raw, w[:, :, bass.ds(n * P, P)], KD))

            @block.gpsimd
            def _(pool):
                st.start_split(pool)
                st.split_weights(pool, 0, KD, KD)

            @block.tensor
            def _(pe):
                st.start_multiply(pe)
                st.multiply(pe, 0, KD, lambda b, c: [(ps[b][:, 0:C], 0, [(hi[:, k, cols(c)], lo[:, k, cols(c)]) for k in range(KD)])],
                            ready=split)

            @block.scalar
            def _(act):
                for c in range(CH):
                    act.copy(hi[:, :, cols(c)], src[:, 0:KD, cols(c)]).then_inc(rounded, 1)

            @block.vector
            def _(dve):
                for c in range(CH):
                    dve.wait_ge(rounded, c + 1)
                    dve.tensor_tensor(lo[:, :, cols(c)], src[:, 0:KD, cols(c)], hi[:, :, cols(c)].bitcast(F32), ALU.subtract).then_inc(split, 1)

                def use(n, b, c):
                    x = xT[:, bass.ds(n, 1), cols(c)].rearrange("p a t -> p (a t)")
                    return dve.tensor_tensor(x, x, ps[b][:, 0:C], ALU.add)
                st.start_take(dve)
                st.take(dve, 0, KD, use)


def plain_product(nc, name, sem, sb, banks, w, hi, lo, dst):
    w = w.rearrange("(k p) n -> p k n", p=P)
    with ExitStack() as ctx:
        ps = banks(ctx, 6)
        st = SplitStream(sb, sem, ctx, name, KD, 6)
        with nc.Block() as block:
            @block.sync
            def _(sp):
                st.load(sp, 0, KD, lambda n, raw: halves(raw, w[:, :, bass.ds(n * P, P)], KD))

            @block.gpsimd
            def _(pool):
                st.start_split(pool)
                st.split_weights(pool, 0, KD, KD)

            @block.tensor
            def _(pe):
                st.start_multiply(pe)
                st.multiply(pe, 0, KD, lambda b, c: [(ps[b][:, 0:C], 0, [(hi[:, k, cols(c)], lo[:, k, cols(c)]) for k in range(KD)])])

            @block.scalar
            def _(act):
                st.start_take(act)
                st.take(act, 0, KD, lambda n, b, c: act.copy(dst[:, bass.ds(n, 1), cols(c)].rearrange("p a t -> p (a t)"), ps[b][:, 0:C]))


def feed_forward(nc, i, sem, sb, banks, hi, lo, xT):
    DEPTH = 6
    GROUPS = [(f, min(DEPTH, KF - f)) for f in range(0, KF, DEPTH)]
    wg, wu, wd = (i[n][0].rearrange("(k p) n -> p k n", p=P) for n in ("w_gate", "w_up", "w_down"))
    with ExitStack() as ctx:
        a_hi = sb(ctx, "a_hi", [P, DEPTH, T], F32R)
        a_lo = sb(ctx, "a_lo", [P, DEPTH, T], F32R)
        sg = sb(ctx, "silu", [P, 2, C])
        act_t = sb(ctx, "ff_act", [P, 2, C])
        ps = banks(ctx, 6)
        st = SplitStream(sb, sem, ctx, "ff", 2 * KD, 3)
        silu, chain = sem("ff_silu"), sem("ff_chain")
        plan, at = [], 0
        for f, size in GROUPS:
            plan.append((at, at + size, f, size))
            at += size + KD
        with nc.Block() as block:
            @block.sync
            def _(sp):
                for up_at, down_at, f, size in plan:
                    st.load(sp, up_at, size, lambda n, raw: [(raw[:, 0:KD], wg[:, :, bass.ds(n * P + f * P, P)]),
                                                            (raw[:, KD:2 * KD], wu[:, :, bass.ds(n * P + f * P, P)])])
                    st.load(sp, down_at, KD, lambda n, raw: halves(raw, wd[:, f:f + size, bass.ds(n * P, P)], size))

            @block.gpsimd
            def _(pool):
                st.start_split(pool)
                for up_at, down_at, f, size in plan:
                    st.split_weights(pool, up_at, size, 2 * KD)
                    st.split_weights(pool, down_at, KD, size)

            @block.tensor
            def _(pe):
                st.start_multiply(pe)
                for up_at, down_at, f, size in plan:
                    st.multiply(pe, up_at, size, lambda b, c: [
                        (ps[2 * b + m][:, 0:C], m * KD, [(hi[:, k, cols(c)], lo[:, k, cols(c)]) for k in range(KD)]) for m in range(2)])
                    pe.wait_ge(chain, 6 + 3 * CH * (f + size))
                    st.multiply(pe, down_at, KD, lambda b, c: [
                        (ps[2 * b][:, 0:C], 0, [(a_hi[:, k, cols(c)], a_lo[:, k, cols(c)]) for k in range(size)])])

            @block.scalar
            def _(act):
                for up_at, _, f, size in plan:
                    with act.Fori(0, size // 2) as it:
                        for j in range(6):
                            act.wait_ge(st.done, 6 * it + (CH * up_at + j + 7))
                            act.wait_ge(chain, 18 * it + (3 * (CH * f + j) + 1))
                            act.activation(sg[:, j % 2], ps[2 * (j % 3)][:, 0:C], ACT.Silu).then_inc(silu, 1)

            @block.vector
            def _(dve):
                dve.sem_inc(chain, 6)
                st.start_take(dve)
                for up_at, down_at, f, size in plan:
                    with dve.Fori(0, size // 2) as it:
                        for j in range(6):
                            u = CH * f + j
                            a = act_t[:, j % 2]
                            to_hi, to_lo = (x[:, bass.ds(2 * it + j // 3, 1), cols(j % 3)].rearrange("p a t -> p (a t)") for x in (a_hi, a_lo))
                            dve.wait_ge(silu, 6 * it + (u + 1))
                            dve.tensor_tensor(a, sg[:, j % 2], ps[2 * (j % 3) + 1][:, 0:C], ALU.mult).then_inc(chain, 1)
                            dve.wait_ge(chain, 18 * it + (3 * u + 7))
                            dve.sem_inc(st.freed, 1)
                            dve.tensor_copy(to_hi, a).then_inc(chain, 1)
                            dve.wait_ge(chain, 18 * it + (3 * u + 8))
                            dve.tensor_tensor(to_lo, a, to_hi.bitcast(F32), ALU.subtract).then_inc(chain, 1)

                    def use(n, b, c):
                        x = xT[:, bass.ds(n, 1), cols(c)].rearrange("p a t -> p (a t)")
                        return dve.tensor_tensor(x, x, ps[2 * b][:, 0:C], ALU.add)
                    st.take(dve, down_at, KD, use)


def memory(nc, i, o, sem, sb, banks, mkT, mv, ident, ones, gains, g):
    with ExitStack() as outer:
        memT = sb(outer, "memT", [P, KD, NM])
        hmT = sb(outer, "hmT", [P, KD, NM])
        with ExitStack() as ctx:
            rows = sb(ctx, "mem_rows", [P, 2, D])
            tp = banks(ctx, 4)
            mem_in, turned = sem("mem_in"), sem("mem_turned")
            with nc.Block() as block:
                @block.sync
                def _(sp):
                    sp.dma_start(rows[:], i["mem_prompt"][0].rearrange("(m p) c -> p m c", p=P)).then_inc(mem_in, 16)

                @block.tensor
                def _(pe):
                    pe.wait_ge(mem_in, 16)
                    for m in range(2):
                        for h in range(2):
                            for k in range(4):
                                last = pe.transpose(tp[2 * m + h][:, k * P:(k + 1) * P], rows[:, m, (4 * h + k) * P:(4 * h + k + 1) * P], ident[:])
                            last.then_inc(turned, 1)

                @block.vector
                def _(dve):
                    for m in range(2):
                        for h in range(2):
                            dve.wait_ge(turned, 2 * m + h + 1)
                            dve.tensor_copy(memT[:, 4 * h:4 * h + 4, m * P:(m + 1) * P], tp[2 * m + h][:].rearrange("p (k c) -> p k c", k=4))
        norm(nc, "mem", sem, sb, banks, memT, hmT, NM, 1, gains, g, ones)
        with ExitStack() as ctx:
            slots = sb(ctx, "mem_w", [P, 2, KD, 512])
            rows = memT[:].rearrange("p k m -> p (k m)").rearrange("p (m c) -> p m c", m=2)
            ps = banks(ctx, 4)
            w_in = [sem(f"mem_w{s}") for s in range(2)]
            done, kept, turned, row_kept, stored = (sem(f"mkv_{x}") for x in ("done", "kept", "turned", "rows", "stored"))
            with nc.Block() as block:
                @block.sync
                def _(sp):
                    for n in range(4):
                        if n >= 2:
                            sp.wait_ge(done, (4, 8)[n - 2])
                        w = i[("w_ck", "w_cv")[n // 2]][0].rearrange("(k p) n -> p k n", p=P)
                        sp.dma_start(slots[:, n % 2], w[:, :, (n % 2) * 512:(n % 2) * 512 + 512]).then_inc(w_in[n % 2], 16)
                    for n, (src, name) in enumerate(((rows, "new_mem_k_p"), (mv, "new_mem_v_p"))):
                        sp.wait_ge(row_kept, 4 * n + 4)
                        sp.dma_start(o[name][0, 0].rearrange("(m p) h d -> p m (h d)", p=P), src[:]).then_inc(stored, 16)
                    sp.wait_ge(stored, 32)

                @block.tensor
                def _(pe):
                    for n in range(8):
                        pe.wait_ge(w_in[n // 4], 16)
                        if n >= 2:
                            pe.wait_ge(kept, n - 1)
                        for k in range(KD):
                            last = pe.matmul(ps[n % 2][:, 0:NM], slots[:, n // 4, k, (n % 4) * P:(n % 4 + 1) * P], hmT[:, k, :],
                                             start=k == 0, stop=k == KD - 1)
                        last.then_inc(done, 1)
                    pe.wait_ge(kept, 8)
                    for m in range(2):
                        for h in range(2):
                            u = 2 * m + h
                            if u >= 2:
                                pe.wait_ge(row_kept, u - 1)
                            for k in range(4):
                                last = pe.transpose(ps[2 + u % 2][:, k * P:(k + 1) * P], mkT[:, 4 * h + k, m * P:(m + 1) * P], ident[:])
                            last.then_inc(turned, 1)
                    for h in range(2):
                        for m in range(2):
                            u = 4 + 2 * h + m
                            pe.wait_ge(w_in[h], 32)
                            pe.wait_ge(row_kept, u - 1)
                            for k in range(KD):
                                last = pe.matmul(ps[2 + u % 2][:], hmT[:, k, m * P:(m + 1) * P], slots[:, h, k, :], start=k == 0, stop=k == KD - 1)
                            last.then_inc(turned, 1)

                @block.scalar
                def _(act):
                    for n in range(8):
                        act.wait_ge(done, n + 1)
                        act.copy(mkT[:, n, :], ps[n % 2][:, 0:NM]).then_inc(kept, 1)

                @block.vector
                def _(dve):
                    for u in range(8):
                        dve.wait_ge(turned, u + 1)
                        if u < 4:
                            dst = rows[:, u // 2, 512 * (u % 2):512 * (u % 2) + 512]
                        else:
                            dst = mv[:, u % 2, 512 * (u // 2 - 2):512 * (u // 2 - 2) + 512]
                        dve.tensor_copy(dst, ps[2 + u % 2][:]).then_inc(row_kept, 1)


CSCALE = (D // 4) ** -0.5


def cross_prompt(nc, sem, sb, banks, uv, qk, mkT, mv, ident):
    with ExitStack() as ctx:
        qt = sb(ctx, "qt", [P, 2, KD, P])
        probs = sb(ctx, "cprobs", [P, 2, NM])
        turned = sb(ctx, "cturned", [P, 2, 2, P])
        mx = sb(ctx, "cp_mx", [P, 4])
        total = sb(ctx, "cp_total", [P, 4])
        ps = banks(ctx, 6)
        q_in, score, peak, expd, normed, pt, pt_kept, pv, out_kept, chain = (
            sem(f"cp_{x}") for x in ("q", "score", "peak", "exp", "normed", "pt", "pt_kept", "pv", "out", "chain"))
        with nc.Block() as block:
            @block.gpsimd
            def _(pool):
                with pool.Fori(0, NT // 2) as it:
                    for s in range(2):
                        pool.wait_ge(score, 8 * it + 4 * s + 4)
                        pool.tensor_copy(qt[:, s], uv[:, :, bass.ds((2 * it + s) * P, P)]).then_inc(q_in, 1)

            @block.tensor
            def _(pe):
                pe.sem_inc(score, 8)
                pe.sem_inc(pt, 4)
                pe.sem_inc(pv, 4)
                with pe.Fori(0, NT // 2) as it:
                    for s in range(2):
                        base = 8 * it + 4 * s
                        pe.wait_ge(q_in, 2 * it + s + 1)

                        def scores(h):
                            pe.wait_ge(expd, base + h + 3)
                            for k in range(2):
                                last = pe.matmul(ps[h % 2][:, 0:NM], qt[:, s, 2 * h + k, :], mkT[:, 2 * h + k, :], start=k == 0, stop=k == 1)
                            last.then_inc(score, 1)

                        scores(0)
                        for h in range(4):
                            if h < 3:
                                scores(h + 1)
                            pe.wait_ge(normed, base + h + 1)
                            pe.wait_ge(pt_kept, base + h + 3)
                            for m in range(2):
                                last = pe.transpose(ps[2 + h % 2][:, m * P:(m + 1) * P], probs[:, h % 2, m * P:(m + 1) * P], ident[:])
                            last.then_inc(pt, 1)
                            pe.wait_ge(pt_kept, base + h + 5)
                            pe.wait_ge(out_kept, base + h + 3)
                            for k in range(2):
                                for m in range(2):
                                    last = pe.matmul(ps[4 + h % 2][:, k * P:(k + 1) * P], mv[:, m, (2 * h + k) * P:(2 * h + k + 1) * P],
                                                     turned[:, h % 2, m], start=m == 0, stop=m == 1)
                            last.then_inc(pv, 1)

            @block.scalar
            def _(act):
                act.sem_inc(expd, 4)
                act.sem_inc(pt_kept, 4)
                with act.Fori(0, NT // 2) as it:
                    for j in range(8):
                        h = j % 4
                        base = 8 * it + j
                        act.wait_ge(peak, base + 1)
                        act.wait_ge(pt, base + 3)
                        act.activation(probs[:, j % 2], ps[j % 2][:, 0:NM], ACT.Exp, bias=mx[:, h:h + 1], scale=CSCALE,
                                       accum_out=total[:, h:h + 1]).then_inc(expd, 1)
                        act.wait_ge(pt, base + 5)
                        act.wait_ge(pv, base + 3)
                        act.copy(turned[:, j % 2].rearrange("p m c -> p (m c)"), ps[2 + j % 2][:, 0:NM]).then_inc(pt_kept, 1)

            @block.vector
            def _(dve):
                dve.sem_inc(out_kept, 4)
                with dve.Fori(0, NT // 2) as it:
                    for j in range(8):
                        h = j % 4
                        base = 8 * it + j
                        dve.wait_ge(score, base + 9)
                        dve.tensor_reduce(mx[:, h:h + 1], ps[j % 2][:, 0:NM], X, ALU.max, negate=True).then_inc(chain, 1)
                        dve.wait_ge(chain, 2 * base + 1)
                        dve.tensor_scalar(mx[:, h:h + 1], mx[:, h:h + 1], CSCALE, None, ALU.mult).then_inc(peak, 1)
                        dve.wait_ge(expd, base + 5)
                        dve.reciprocal(total[:, h:h + 1], total[:, h:h + 1]).then_inc(chain, 1)
                        dve.wait_ge(chain, 2 * base + 2)
                        dve.tensor_scalar(probs[:, j % 2], probs[:, j % 2], total[:, h:h + 1], None, ALU.mult).then_inc(normed, 1)
                        dve.wait_ge(pv, base + 5)
                        dve.tensor_copy(qk[:, 2 * h:2 * h + 2, bass.ds((2 * it + j // 4) * P, P)],
                                        ps[4 + j % 2][:, 0:NM].rearrange("p (k c) -> p k c", k=2)).then_inc(out_kept, 1)


def cross_sample(nc, i, sem, sb, banks, uv, qk, ident):
    with ExitStack() as ctx:
        mem = sb(ctx, "mem", [P, 2, 2, D])
        kT = sb(ctx, "mem_kT", [P, KD, NM])
        q_rows = sb(ctx, "cq_rows", [P, KD, NB, 32])
        probs = sb(ctx, "cs_probs", [P, 2, NM])
        turned = sb(ctx, "cs_turned", [P, 2, 2, P])
        one = sb(ctx, "cs_one", [P, 2, 4])
        tp = banks(ctx, 4)
        sc = banks(ctx, 2)
        out = banks(ctx, 1)[0]
        zeroed, q_ready, keys, score, peak, expd, normed, pt, pt_kept, pv, chain = (
            sem(f"cs_{x}") for x in ("zeroed", "q", "keys", "score", "peak", "exp", "normed", "pt", "pt_kept", "pv", "chain"))
        mem_in = [sem(f"cs_mem{s}") for s in range(2)]
        kept = [sem(f"cs_kept{k}") for k in range(2)]
        loads = [(name, 4 * grp + b) for grp in range(2) for name in ("cache_mem_k", "cache_mem_v") for b in range(4)]
        with nc.Block() as block:
            @block.sync
            def _(sp):
                for n, (name, b) in enumerate(loads):
                    if n >= 2:
                        before, bb = loads[n - 2]
                        if before == "cache_mem_k":
                            sp.wait_ge(keys, 4 * bb + 4)
                        else:
                            sp.wait_ge(pv, bb + 1)
                    sp.dma_start(mem[:, n % 2], i[name][0, b].rearrange("(m p) h d -> p m (h d)", p=P)).then_inc(mem_in[n % 2], 16)

            @block.gpsimd
            def _(pool):
                pool.memset(q_rows[:], 0.0).then_inc(zeroed, 1)

            @block.tensor
            def _(pe):
                pe.wait_ge(q_ready, KD)
                for grp in range(2):
                    for bb in range(4):
                        b = 4 * grp + bb
                        n = 8 * grp + bb
                        pe.wait_ge(mem_in[n % 2], 16 * (n // 2 + 1))
                        for x in range(4):
                            if b > 0:
                                pe.wait_ge(kept[x % 2], 2 * b - 1 + x // 2)
                            for k in range(2):
                                for m in range(2):
                                    last = pe.transpose(tp[x][:, k * NM + m * P:k * NM + (m + 1) * P],
                                                        mem[:, n % 2, m, (2 * x + k) * P:(2 * x + k + 1) * P], ident[:])
                            last.then_inc(keys, 1)
                        for x in range(2):
                            pe.wait_ge(kept[x], 2 * b + 2)
                        for k in range(KD):
                            last = pe.matmul(sc[grp][32 * bb:32 * bb + 32, 0:NM], q_rows[:, k, b, :], kT[:, k, :], start=k == 0, stop=k == KD - 1,
                                             tile_position=(0, 32 * bb), skip_group_check=True)
                        last.then_inc(score, 1)
                    pe.wait_ge(normed, grp + 1)
                    for m in range(2):
                        last = pe.transpose(tp[0][:, m * P:(m + 1) * P], probs[:, grp, m * P:(m + 1) * P], ident[:])
                    last.then_inc(pt, 1)
                    pe.wait_ge(pt_kept, grp + 1)
                    for bb in range(4):
                        b = 4 * grp + bb
                        n = 8 * grp + 4 + bb
                        pe.wait_ge(mem_in[n % 2], 16 * (n // 2 + 1))
                        for k in range(KD):
                            r = 32 * bb + NS * (k // 2)
                            at = k * TS + NS * b
                            for m in range(2):
                                last = pe.matmul(out[:, at:at + NS], mem[:, n % 2, m, k * P:(k + 1) * P], turned[:, grp, m, r:r + NS],
                                                 start=m == 0, stop=m == 1, skip_group_check=True)
                        last.then_inc(pv, 1)

            def keep(eng, copy, which):
                for b in range(NB):
                    for x in (which, which + 2):
                        eng.wait_ge(keys, 4 * b + x + 1)
                        if b > 0:
                            eng.wait_ge(score, b)
                        copy(kT[:, 2 * x:2 * x + 2, :].rearrange("p k c -> p (k c)"), tp[x][:]).then_inc(kept[which], 1)
                    if b % 4 == 3:
                        yield b // 4

            @block.scalar
            def _(act):
                for grp in keep(act, act.copy, 1):
                    act.wait_ge(peak, grp + 1)
                    act.activation(probs[:, grp], sc[grp][:, 0:NM], ACT.Exp, bias=one[:, grp, 0:1], scale=CSCALE,
                                   accum_out=one[:, grp, 1:2]).then_inc(expd, 1)

            @block.vector
            def _(dve):
                ch = Chain(dve, chain)
                dve.wait_ge(zeroed, 1)
                for k in range(KD):
                    h = k // 2
                    dve.tensor_copy(q_rows[:, k, :, NS * h:NS * h + NS], uv[:, k, NP:T].rearrange("p (b s) -> p b s", b=NB)).then_inc(q_ready, 1)
                for grp in keep(dve, dve.tensor_copy, 0):
                    dve.wait_ge(score, 4 * grp + 4)
                    ch(dve.tensor_reduce(one[:, grp, 2:3], sc[grp][:, 0:NM], X, ALU.max, negate=True))
                    dve.tensor_scalar(one[:, grp, 0:1], one[:, grp, 2:3], CSCALE, None, ALU.mult).then_inc(peak, 1)
                    dve.wait_ge(expd, grp + 1)
                    ch(dve.reciprocal(one[:, grp, 3:4], one[:, grp, 1:2]))
                    dve.tensor_scalar(probs[:, grp], probs[:, grp], one[:, grp, 3:4], None, ALU.mult).then_inc(normed, 1)
                    dve.wait_ge(pt, grp + 1)
                    dve.tensor_copy(turned[:, grp].rearrange("p m c -> p (m c)"), tp[0][:, 0:NM]).then_inc(pt_kept, 1)
                dve.wait_ge(pv, NB)
                dve.tensor_copy(qk[:, 0:KD, NP:T], out[:, 0:KD * TS].rearrange("p (k t) -> p k t", k=KD))


def store_y(nc, o, sem, sb, banks, hT, ident):
    with ExitStack() as ctx:
        rows = sb(ctx, "y_rows", [P, 2, D])
        tp = banks(ctx, 4)
        turned = sem("y_turned")
        kept = [sem(f"y_kept{h}") for h in range(2)]
        stored = [sem(f"y_stored{s}") for s in range(2)]

        def n_rows(t):
            return P if t < NT else TS

        with nc.Block() as block:
            @block.tensor
            def _(pe):
                for t in range(NT + 1):
                    for h in range(2):
                        if t >= 2:
                            pe.wait_ge(kept[h], t - 1)
                        for k in range(4):
                            last = pe.transpose(tp[2 * h + t % 2][0:n_rows(t), k * P:(k + 1) * P], hT[:, 4 * h + k, t * P:t * P + n_rows(t)], ident[:])
                        last.then_inc(turned, 1)

            def keep(eng, h, copy):
                for t in range(NT + 1):
                    r = n_rows(t)
                    eng.wait_ge(turned, 2 * t + h + 1)
                    if t >= 2:
                        eng.wait_ge(stored[t % 2], 16 * (t // 2))
                    copy(rows[0:r, t % 2, 512 * h:512 * h + 512], tp[2 * h + t % 2][0:r, :]).then_inc(kept[h], 1)

            @block.scalar
            def _(act):
                keep(act, 0, act.copy)

            @block.vector
            def _(dve):
                keep(dve, 1, dve.tensor_copy)

            @block.sync
            def _(sp):
                for t in range(NT + 1):
                    sp.wait_ge(kept[0], t + 1)
                    sp.wait_ge(kept[1], t + 1)
                    dst = o["y_prompt"][0, t * P:(t + 1) * P] if t < NT else o["y_sample"].rearrange("b s c -> (b s) c")
                    sp.dma_start(dst, rows[0:n_rows(t), t % 2]).then_inc(stored[t % 2], 16)
                sp.wait_ge(stored[0], 16 * 5)
                sp.wait_ge(stored[1], 16 * 4)


KV = (2, HD)
OUTS = [("y_prompt", (1, NP, D)), ("y_sample", (NB, NS, D)),
        ("new_cmp_k_p", (1, 1, NP, *KV)), ("new_cmp_v_p", (1, 1, NP, *KV)),
        ("new_slc_k_p", (1, 1, NP, *KV)), ("new_slc_v_p", (1, 1, NP, *KV)),
        ("new_win_k_p", (1, 1, WIN, *KV)), ("new_win_v_p", (1, 1, WIN, *KV)),
        ("new_mem_k_p", (1, 1, NM, 4, 256)), ("new_mem_v_p", (1, 1, NM, 4, 256)),
        ("new_cmp_k_s", (1, NB, NS, *KV)), ("new_cmp_v_s", (1, NB, NS, *KV)),
        ("new_slc_k_s", (1, NB, NS, *KV)), ("new_slc_v_s", (1, NB, NS, *KV)),
        ("new_win_k_s", (1, NB, WIN, *KV)), ("new_win_v_s", (1, NB, WIN, *KV)),
        ("new_gmlp_v_s", (1, NB, NS, 512))]


def kernel(**inputs):
    import concourse.bacc as bacc
    from concourse.bass_utils import run_bass_kernel_spmd

    nc = bacc.Bacc("TRN2", target_bir_lowering=False, num_devices=1)
    arrays = {k: np.ascontiguousarray(v) for k, v in inputs.items()}
    arrays.update(consts())
    ins = {k: nc.dram_tensor(k, v.shape, mybir.dt.from_np(v.dtype), kind="ExternalInput").ap() for k, v in arrays.items()}
    outs = {n: nc.dram_tensor("out_" + n, s, F32, kind="ExternalOutput").ap() for n, s in OUTS}
    build(nc, ins, outs)
    r = run_bass_kernel_spmd(nc, [arrays], core_ids=[0])
    return tuple(r.results[0]["out_" + n] for n, _ in OUTS)
```

```python
from contextlib import ExitStack, nullcontext

import numpy as np

import concourse.bass as bass
from concourse import mybir

ALU = mybir.AluOpType
ACT = mybir.ActivationFunctionType
F32 = mybir.dt.float32
F32R = mybir.dt.float32r
I32 = mybir.dt.int32
X = mybir.AxisListType.X

P = 128
D = 1024
KD = D // P
NP = 1024
NB = 8
NS = 4
TS = NB * NS
T = NP + TS
NT = NP // P
CH = 3
C = T // CH
HD = 64
G = 4
CMP = 63
SRC = NB + 1
PAIRS = 512
PAGES = 8
N_POOL = 80
WIN = 512
NM = 256
FF = 2816
KF = FF // P
EPS = 1e-6
NEG = -1e30
U_COL = 1304
GN_COL = 1280
GA_COL = 2328
GB_COL = 3352


def consts():
    half = HD // 2
    inv = (np.float32(10000.0) ** (-np.arange(half, dtype=np.float32) / np.float32(half))).astype(np.float32)
    pos = np.concatenate([np.arange(NP), np.tile(NP + np.arange(NS), NB)]).astype(np.float32)
    ang = (pos[None, :] * inv[:, None]).astype(np.float32)
    rot = np.zeros((P, P), np.float32)
    for m in range(P):
        if m % HD < half:
            rot[m + half, m] = -1.0
        else:
            rot[m - half, m] = 1.0
    a = np.arange(P)
    cend = 16 * np.arange(CMP) + 31
    seen = (cend[None, None, :] <= (P * np.arange(NT)[None, :, None] + a[:, None, None])).astype(np.float32)
    rb, rh, rg, rs = a // 32, a // 16 % 2, a // 4 % 4, a % 4
    same = (rb[:, None] == rb) & (rh[:, None] == rh) & (rs[:, None] == rs)
    shared = np.zeros((CMP, 16), np.float32)
    for n in range(CMP):
        for m in range(16):
            shared[n, m] = max(min(16 * n + 32, 64 * m + 64) - max(16 * n, 64 * m), 0) / 32
    s4 = np.arange(4)
    row_of = np.zeros((TS, 2, P), np.float32)
    for grp in range(2):
        row_of[(4 * grp + rb) * 4 + rs, grp, a] = 1.0
    hg = np.zeros((P, 8, 3), np.float32)
    hg[a, rh * 4 + rg, :] = 1.0
    lane = np.zeros((TS, 8, TS), np.float32)
    for j in range(TS):
        for k in range(TS):
            if j // 4 == k // 4 and j % 4 <= k % 4:
                lane[j, :, k] = 1.0
    return {
        "c_ident": np.eye(P, dtype=np.float32),
        "c_cos": np.tile(np.cos(ang), (4, 1)).astype(np.float32),
        "c_sin": np.tile(np.sin(ang), (4, 1)).astype(np.float32),
        "c_rot": rot,
        "c_tril": (a[:, None] <= a[None, :]).astype(np.float32),
        "c_lane": lane,
        "c_diag": np.where(a[None, :] <= a[:, None], 0.0, NEG).astype(np.float32),
        "c_far": np.where(a[None, :] > a[:, None], 0.0, NEG).astype(np.float32),
        "c_seen": seen,
        "c_hidden": np.where(seen > 0, 0.0, NEG).astype(np.float32),
        "c_same": same.astype(np.float32),
        "c_shared": shared,
        "c_new": np.where(s4[None, :] <= rs[:, None], 0.0, NEG).astype(np.float32),
        "c_old": np.where(s4[None, :] > rs[:, None], 0.0, NEG).astype(np.float32),
        "c_row_of": row_of,
        "c_hg": hg,
        "c_block": np.tile(np.arange(16, dtype=np.float32), (P, 1)),
    }


class Chain:

    def __init__(self, eng, sem):
        self.eng, self.sem, self.n = eng, sem, 0

    def __call__(self, ins):
        self.n += 1
        ins.then_inc(self.sem, 1)
        self.eng.wait_ge(self.sem, self.n)


class SplitStream:

    def __init__(self, sb, sem, ctx, name, depth, sets, rounds_on_act=False):
        self.sets, self.rounds_on_act = sets, rounds_on_act
        self.raw = sb(ctx, f"{name}_raw", [P, 2, depth, P])
        self.w_hi = sb(ctx, f"{name}_w_hi", [P, 2, depth, P], F32R)
        self.w_lo = sb(ctx, f"{name}_w_lo", [P, 2, depth, P], F32R)
        self.w_in = [sem(f"{name}_w{s}") for s in range(2)]
        self.rounded, self.split, self.passed, self.done, self.freed = (
            sem(f"{name}_{x}") for x in ("rounded", "split", "passed", "done", "freed"))

    def load_tile(self, sp, it, step, m, copies):
        sp.wait_ge(self.split, step * it + (m + 1))
        for dst, src in copies:
            sp.dma_start(dst, src).then_inc(self.w_in[m % 2], 16)

    def load(self, sp, first, tiles, copies):
        with sp.Fori(0, tiles // 2) as it:
            for s in range(2):
                self.load_tile(sp, it, 2, first + s, copies(2 * it + s, self.raw[:, s]))

    def round_tile(self, eng, it, step, m, depth):
        eng.wait_ge(self.w_in[m % 2], 16 * step * it + (16 * (m - m % 2) + 32))
        eng.wait_ge(self.done, 3 * step * it + (3 * m + 3))
        if self.rounds_on_act:
            eng.copy(self.w_hi[:, m % 2, 0:depth], self.raw[:, m % 2, 0:depth]).then_inc(self.rounded, 1)
        else:
            eng.sem_inc(self.passed, 1)
            eng.tensor_copy(self.w_hi[:, m % 2, 0:depth], self.raw[:, m % 2, 0:depth]).then_inc(self.rounded, 1)

    def split_tile(self, pool, it, step, m, depth):
        raw, hi, lo = (x[:, m % 2, 0:depth] for x in (self.raw, self.w_hi, self.w_lo))
        if not self.rounds_on_act:
            self.round_tile(pool, it, step, m, depth)
        pool.wait_ge(self.rounded, step * it + (m + 1))
        pool.sem_inc(self.passed, 1)
        pool.tensor_tensor(lo, raw, hi.bitcast(F32), ALU.subtract).then_inc(self.split, 1)

    def start_split(self, pool):
        pool.sem_inc(self.split, 2)

    def split_weights(self, pool, first, tiles, depth):
        with pool.Fori(0, tiles // 2) as it:
            for s in range(2):
                self.split_tile(pool, it, 2, first + s, depth)

    def each_tile(self, eng, first, tiles, depth, next_depth, use):
        with eng.Fori(0, tiles // 2 - 1) if tiles > 2 else nullcontext(0) as it:
            if tiles > 2:
                for s in range(2):
                    self.round_tile(eng, it, 2, first + s + 1, depth)
                    use(it, first + s, 2 * it + s)
        last = first + tiles - 2
        self.round_tile(eng, 0, 0, last + 1, depth)
        use(0, last, tiles - 2)
        if next_depth is not None:
            self.round_tile(eng, 0, 0, last + 2, next_depth)
        use(0, last + 1, tiles - 1)

    def start_multiply(self, pe):
        pe.sem_inc(self.done, 6)

    def multiply_tile(self, pe, it, step, m, groups, ready=None):
        s = m % 2
        pe.wait_ge(self.split, step * it + (m + 3))
        for c in range(CH):
            if ready is not None:
                pe.wait_ge(ready[0], ready[1] * (c + 1) + (ready[2] if len(ready) > 2 else 0))
            pe.wait_ge(self.freed, 3 * step * it + (3 * m + c + 1))
            for out, k0, terms in groups((3 * m + c) % self.sets, c):
                for k, (x_hi, x_lo) in enumerate(terms):
                    hi, lo = self.w_hi[:, s, k0 + k, :], self.w_lo[:, s, k0 + k, :]
                    pe.matmul(out, hi, x_hi, start=k == 0, stop=False)
                    pe.matmul(out, hi, x_lo, start=False, stop=False)
                    last = pe.matmul(out, lo, x_hi, start=False, stop=k == len(terms) - 1)
            last.then_inc(self.done, 1)

    def multiply(self, pe, first, tiles, groups, ready=None):
        with pe.Fori(0, tiles // 2) as it:
            for s in range(2):
                self.multiply_tile(pe, it, 2, first + s, groups, ready)

    def start_take(self, eng):
        eng.sem_inc(self.freed, self.sets)

    def take_tile(self, eng, it, step, m, use, n=0):
        for c in range(CH):
            eng.wait_ge(self.done, 3 * step * it + (3 * m + c + 7))
            use(n, (3 * m + c) % self.sets, c).then_inc(self.freed, 1)

    def take(self, eng, first, tiles, use):
        with eng.Fori(0, tiles // 2) as it:
            for s in range(2):
                self.take_tile(eng, it, 2, first + s, use, 2 * it + s)


def halves(raw, src, depth):
    h = depth // 2
    return [(raw[:, 0:h], src[:, 0:h]), (raw[:, h:depth], src[:, h:depth])]


def products(ps, hi, lo, depth=KD):
    return lambda b, c: [(ps[b][:, 0:C], 0, [(hi[:, k, cols(c)], lo[:, k, cols(c)]) for k in range(depth)])]


def flat(x):
    return x.rearrange("p a t -> p (a t)")


def cols(c):
    return slice(c * C, c * C + C)


def build(nc, i, o):
    with ExitStack() as top, nc.allow_non_contiguous_dma(reason="small tables"):
        taken = []

        def sem(name):
            taken.append(nc.alloc_semaphore(name))
            return taken[-1]

        def clear_semaphores():
            nc.clear_and_free_semaphores(taken)
            nc.all_engine_barrier()
            taken.clear()

        def sb(ctx, name, shape, dt=F32):
            return ctx.enter_context(nc.sbuf_tensor(name, shape, dt))

        def banks(ctx, n):
            return [ctx.enter_context(nc.psum_tensor(f"bank{k}_{nc.next_id()}", [P, 512], F32)) for k in range(n)]

        ident = sb(top, "ident", [P, P])
        ones = sb(top, "ones", [P, P])
        gains = sb(top, "gains", [P, 4, KD])
        G_MIX, G_CROSS, G_MEM, G_FFN = range(4)
        x_kept = nc.dram_tensor("x_kept", [P, KD * T], F32).ap()

        def halved(ctx, name):
            return sb(ctx, f"{name}_hi", [P, KD, T], F32R), sb(ctx, f"{name}_lo", [P, KD, T], F32R)

        with ExitStack() as mid:
            qk = sb(mid, "qk", [P, 10, T])
            with ExitStack() as mix:
                hi, lo = halved(mix, "mix")
                uv = sb(mix, "uv", [P, 8, T])
                with ExitStack() as early:
                    gT = early.enter_context(nc.sbuf_tensor("gT", [24, T], F32, side="right"))
                    with ExitStack() as first:
                        xT = first.enter_context(nc.sbuf_tensor("x_first", [P, KD, T], F32, side="right"))
                        load_x(nc, i, sem, sb, banks, xT, ident, ones, gains)
                        project(nc, i, sem, sb, banks, xT, x_kept, hi, lo, qk, uv, gT, gains, G_MIX, ones)
                    vtok = sb(mix, "vtok", [P, NT, 2, P])
                    gates = sb(mix, "gates", [P, NT + 1, 24])
                    rope(nc, i, sem, sb, banks, qk)
                    rows_and_gmlp(nc, i, o, sem, sb, banks, gT, qk, uv, vtok, gates, ident)
                with ExitStack() as att:
                    ck = sb(att, "ck", [P, SRC, CMP])
                    cv = sb(att, "cv", [CMP, SRC, P])
                    compress(nc, i, o, sem, sb, banks, uv, ck, cv, ident)
                    oT = sb(att, "oT", [P, G, T])
                    attend_prompt(nc, i, sem, sb, banks, qk, vtok, gates, ck, cv, oT, ident)
                    attend_sample(nc, i, o, sem, sb, banks, qk, uv, vtok, gates, ck, cv, oT, ident)
                    clear_semaphores()
                    merge(nc, i, sem, sb, banks, hi, lo, oT, uv, qk)
            xT = top.enter_context(nc.sbuf_tensor("xT", [P, KD, T], F32, side="right"))
            cqT = sb(mid, "cqT", [P, KD, T])
            with ExitStack() as parts:
                hi, lo = halved(parts, "out")
                add_product(nc, "out", sem, sb, banks, i["w_out"][0], qk, hi, lo, xT, x_kept)
                normed_product(nc, "cq", sem, sb, banks, i["w_cq"][0], xT, flat(qk[:]), hi, lo, cqT, gains, G_CROSS, ones)
            with ExitStack() as mem:
                mkT = sb(mem, "mkT", [P, KD, NM])
                mv = sb(mem, "mv", [P, 2, D])
                memory(nc, i, o, sem, sb, banks, mkT, mv, ident, ones, gains, G_MEM)
                ring = sb(mem, "mem_ring", [P, MEM_SLOTS, 2, D])
                ring_in = [sem(f"mem_ring{s}") for s in range(MEM_SLOTS)]
                cross_prompt(nc, i, sem, sb, banks, cqT, qk, mkT, mv, ident, ring, ring_in)
                cross_sample(nc, i, sem, sb, banks, cqT, qk, ident, ring, ring_in)
            with ExitStack() as parts:
                hi, lo = halved(parts, "cross")
                add_product(nc, "co", sem, sb, banks, i["w_co"][0], qk, hi, lo, xT)
        with ExitStack() as ffn:
            hi, lo = halved(ffn, "ffn")
            feed_forward(nc, i, sem, sb, banks, hi, lo, xT, gains, G_FFN, ones)
        finish(nc, i, o, sem, sb, banks, xT, ident)


def load_x(nc, i, sem, sb, banks, xT, ident, ones, gains):
    with ExitStack() as ctx:
        xin = sb(ctx, "xin", [P, 3, D])
        tp = banks(ctx, 4)
        const_in, ones_set = sem("const_in"), sem("ones_set")
        x_in = [sem(f"x_in{s}") for s in range(3)]
        turned = [sem(f"x_turned{h}") for h in range(2)]
        taken = [sem(f"x_taken{h}") for h in range(2)]
        with nc.Block() as block:
            @block.sync
            def _(sp):
                sp.dma_start(ident[:], i["c_ident"]).then_inc(const_in, 16)
                sp.dma_start(xin[0:TS, 2, :], i["x_sample"].rearrange("b s d -> (b s) d")).then_inc(x_in[2], 16)
                with sp.Fori(0, NT // 2) as it:
                    for s in range(2):
                        sp.wait_ge(turned[1], 2 * it + s + 1)
                        sp.dma_start(xin[:, s, :], i["x_prompt"][0, bass.ds((2 * it + s) * P, P), :]).then_inc(x_in[s], 16)

            @block.gpsimd
            def _(pool):
                pool.memset(ones[:], 1.0).then_inc(ones_set, 1)

            def turn(pe, h, s, rows, src):
                for k in range(4):
                    last = pe.transpose(tp[2 * h + s][:, k * P:k * P + rows], src[:, (4 * h + k) * P:(4 * h + k + 1) * P],
                                        ident[0:rows, 0:rows])
                last.then_inc(turned[h], 1)

            @block.tensor
            def _(pe):
                pe.wait_ge(const_in, 16 * 5)
                pe.sem_inc(turned[0], 2)
                pe.sem_inc(turned[1], 2)
                with pe.Fori(0, NT // 2) as it:
                    for s in range(2):
                        pe.wait_ge(x_in[s], 16 * it + 16)
                        for h in range(2):
                            pe.wait_ge(taken[h], 2 * it + s + 1)
                            turn(pe, h, s, P, xin[:, s, :])
                pe.wait_ge(x_in[2], 16)
                for h in range(2):
                    pe.wait_ge(taken[h], NT + 1)
                    turn(pe, h, 0, TS, xin[0:TS, 2, :])

            def take(eng, h, copy):
                eng.sem_inc(taken[h], 2)
                with eng.Fori(0, NT // 2) as it:
                    for s in range(2):
                        eng.wait_ge(turned[h], 2 * it + s + 3)
                        copy(xT[:, 4 * h:4 * h + 4, bass.ds((2 * it + s) * P, P)],
                             tp[2 * h + s][:].rearrange("p (k c) -> p k c", k=4)).then_inc(taken[h], 1)
                eng.wait_ge(turned[h], NT + 3)
                copy(xT[:, 4 * h:4 * h + 4, NP:T],
                     tp[2 * h][:].rearrange("p (k c) -> p k c", k=4)[:, :, 0:TS]).then_inc(taken[h], 1)

            @block.scalar
            def _(act):
                for n, name in enumerate(("g_mix", "g_cross", "g_mem", "g_ffn")):
                    act.dma_start(gains[:, n, :], i[name][0].rearrange("(k p) -> p k", p=P)).then_inc(const_in, 16)
                take(act, 0, act.copy)

            @block.vector
            def _(dve):
                take(dve, 1, dve.tensor_copy)


def norm(nc, name, sem, sb, banks, src, dst, width, chunks, gains, g, ones):
    n = width // chunks
    with ExitStack() as ctx:
        sq = sb(ctx, f"{name}_sq", [P, 2, KD, n])
        part = sb(ctx, f"{name}_part", [P, chunks, n])
        std = sb(ctx, f"{name}_std", [P, chunks, n])
        ps = banks(ctx, chunks)
        squared, summed, spread, rooted, chain = (sem(f"{name}_{x}") for x in ("squared", "summed", "spread", "rooted", "chain"))
        with nc.Block() as block:
            @block.scalar
            def _(act):
                for c in range(chunks):
                    if c >= 2:
                        act.wait_ge(summed, c - 1)
                    act.square(sq[:, c % 2], src[:, 0:KD, c * n:(c + 1) * n]).then_inc(squared, 1)
                for c in range(chunks):
                    act.wait_ge(chain, c + 1)
                    act.sqrt(std[:, c], std[:, c]).then_inc(rooted, 1)

            @block.tensor
            def _(pe):
                for c in range(chunks):
                    pe.wait_ge(summed, c + 1)
                    pe.matmul(ps[c][:, 0:n], ones[:], part[:, c], start=True, stop=True).then_inc(spread, 1)

            @block.vector
            def _(dve):
                for c in range(chunks):
                    dve.wait_ge(squared, c + 1)
                    dve.tensor_reduce(part[:, c], sq[:, c % 2].rearrange("p k t -> p t k"), X, ALU.add).then_inc(summed, 1)
                ch = Chain(dve, chain)
                for c in range(chunks):
                    dve.wait_ge(spread, c + 1)
                    ch(dve.tensor_scalar(std[:, c], ps[c][:, 0:n], 1.0 / D, EPS, ALU.mult, ALU.add))
                for c in range(chunks):
                    dve.wait_ge(rooted, c + 1)
                    ch(dve.reciprocal(part[:, c], std[:, c]))
                    for k in range(KD):
                        dve.scalar_tensor_tensor(dst[:, k, c * n:(c + 1) * n], src[:, k, c * n:(c + 1) * n], gains[:, g, k:k + 1],
                                                 part[:, c], ALU.mult, ALU.mult)


class SplitNorm:
    SCRATCH = (KD + CH + 4) * C

    def __init__(self, sem, name, src, hi, lo, gain, ones, ps, scratch):
        self.src, self.hi, self.lo, self.gain, self.ones, self.ps = src, hi, lo, gain, ones, ps
        self.sq, self.part, self.h = (
            scratch[:, C * a:C * b].rearrange("p (k t) -> p k t", t=C) for a, b in ((0, KD), (KD, KD + CH), (KD + CH, KD + CH + 4)))
        self.squared, self.summed, self.spread, self.rooted, self.chain, self.scaled, self.rounded, self.split = (
            sem(f"{name}_h_{x}") for x in ("squared", "summed", "spread", "rooted", "chain", "scaled", "rounded", "split"))
        self.ready = (self.split, KD)

    def scalar(self, act, between=None):
        def square(c):
            if c > 0:
                act.wait_ge(self.summed, c)
            act.square(self.sq, self.src[:, 0:KD, cols(c)]).then_inc(self.squared, 1)

        square(0)
        for c in range(CH):
            if c == 0:
                square(1)
            act.wait_ge(self.chain, 2 * c + 1)
            act.sqrt(self.part[:, c], self.part[:, c]).then_inc(self.rooted, 1)
            if c == 0:
                square(2)
                if between is not None:
                    between()
            for k in range(KD):
                u = KD * c + k
                act.wait_ge(self.scaled, u + 1)
                act.copy(self.hi[:, k, cols(c)], self.h[:, u % 4]).then_inc(self.rounded, 1)

    def tensor(self, pe):
        for c in range(CH):
            pe.wait_ge(self.summed, c + 1)
            pe.matmul(self.ps[c][:, 0:C], self.ones[:], self.part[:, c], start=True, stop=True).then_inc(self.spread, 1)

    def gpsimd(self, pool):
        for c in range(CH):
            for k in range(KD):
                u = KD * c + k
                pool.wait_ge(self.rounded, u + 1)
                pool.tensor_tensor(self.lo[:, k, cols(c)], self.h[:, u % 4], self.hi[:, k, cols(c)].bitcast(F32), ALU.subtract).then_inc(self.split, 1)

    def vector(self, dve):
        ch = Chain(dve, self.chain)

        def add_up(c):
            dve.wait_ge(self.squared, c + 1)
            dve.tensor_reduce(self.part[:, c], self.sq.rearrange("p k t -> p t k"), X, ALU.add).then_inc(self.summed, 1)

        add_up(0)
        for c in range(CH):
            dve.wait_ge(self.spread, c + 1)
            ch(dve.tensor_scalar(self.part[:, c], self.ps[c][:, 0:C], 1.0 / D, EPS, ALU.mult, ALU.add))
            if c == 0:
                add_up(1)
            dve.wait_ge(self.rooted, c + 1)
            ch(dve.reciprocal(self.part[:, c], self.part[:, c]))
            if c == 0:
                add_up(2)
            for k in range(KD):
                u = KD * c + k
                if u >= 4:
                    dve.wait_ge(self.split, u - 3)
                dve.scalar_tensor_tensor(self.h[:, u % 4], self.src[:, k, cols(c)], self.gain[:, k:k + 1],
                                         self.part[:, c], ALU.mult, ALU.mult).then_inc(self.scaled, 1)


def project(nc, i, sem, sb, banks, xT, x_kept, hi, lo, qk, uv, gT, gains, g, ones):
    w = i["w_in"][0].rearrange("(k p) n -> p k n", p=P)
    KV, UV, GN = G, G + 6, G + 6 + 8
    with ExitStack() as ctx:
        ps = banks(ctx, 6)
        st = SplitStream(sb, sem, ctx, "in", KD, 6)
        norm_x = SplitNorm(sem, "mix", xT, hi, lo, gains[:, g], ones, ps, flat(uv[:]))
        x_stored = sem("x_stored")

        def columns(first):
            return lambda n, raw: halves(raw, w[:, :, bass.ds(n * P + first, P)], KD)

        with nc.Block() as block:
            @block.sync
            def _(sp):
                st.load(sp, 0, G, lambda n, raw: [(raw[:, :, HD * h:HD * h + HD], w[:, :, bass.ds(n * HD + G * HD * h, HD)]) for h in range(2)])
                st.load(sp, KV, 6, columns(G * P))
                st.load(sp, UV, 8, columns(U_COL))
                st.load_tile(sp, 0, 0, GN, columns(GN_COL)(0, st.raw[:, GN % 2]))
                sp.wait_ge(x_stored, 16)

            @block.gpsimd
            def _(pool):
                st.start_split(pool)
                st.split_tile(pool, 0, 0, 0, KD)
                norm_x.gpsimd(pool)
                st.split_tile(pool, 0, 0, 1, KD)
                st.split_weights(pool, 2, GN - 2, KD)
                st.split_tile(pool, 0, 0, GN, KD)

            @block.tensor
            def _(pe):
                st.start_multiply(pe)
                norm_x.tensor(pe)
                st.multiply(pe, 0, GN, products(ps, hi, lo), norm_x.ready)
                st.multiply_tile(pe, 0, 0, GN, products(ps, hi, lo))

            @block.scalar
            def _(act):
                act.dma_start(x_kept, flat(xT[:])).then_inc(x_stored, 16)
                st.start_take(act)
                norm_x.scalar(act)
                for first, tiles, dst, func in ((0, G, qk, ACT.Copy), (KV, 6, qk[:, 4:10], ACT.Copy), (UV, 8, uv, ACT.Gelu_apprx_tanh)):
                    st.take(act, first, tiles, lambda n, b, c: act.activation(flat(dst[:, bass.ds(n, 1), cols(c)]), ps[b][:, 0:C], func))
                st.take_tile(act, 0, 0, GN, lambda n, b, c: act.copy(gT[:, cols(c)], ps[b][0:24, 0:C]))

            @block.vector
            def _(dve):
                norm_x.vector(dve)


ROPED = (0, 1, 2, 3, 4, 6, 8)


def rope(nc, i, sem, sb, banks, qk):
    with ExitStack() as ctx:
        cos = sb(ctx, "cos", [P, T])
        sin = sb(ctx, "sin", [P, T])
        rot = sb(ctx, "rot", [P, P])
        t = sb(ctx, "rope_t", [P, 2, 2, C])
        ps = banks(ctx, 2)
        table_in, rotated, done, sin_done = sem("table_in"), sem("rotated"), sem("roped"), sem("rope_sin")
        cos_done = sem("rope_cos")
        units = [(tile, c) for tile in ROPED for c in range(CH)]
        with nc.Block() as block:
            @block.sync
            def _(sp):
                for dst, name in ((cos, "c_cos"), (sin, "c_sin"), (rot, "c_rot")):
                    sp.dma_start(dst[:], i[name]).then_inc(table_in, 16)

            @block.tensor
            def _(pe):
                pe.wait_ge(table_in, 48)
                for u, (tile, c) in enumerate(units):
                    if u >= 2:
                        pe.wait_ge(sin_done, u - 1)
                    pe.matmul(ps[u % 2][:, 0:C], rot[:], qk[:, tile, cols(c)], start=True, stop=True).then_inc(rotated, 1)

            @block.gpsimd
            def _(pool):
                pool.wait_ge(table_in, 48)
                for u, (tile, c) in enumerate(units):
                    if u >= 2:
                        pool.wait_ge(done, u - 1)
                    pool.tensor_tensor(t[:, u % 2, 1], qk[:, tile, cols(c)], cos[:, cols(c)], ALU.mult).then_inc(cos_done, 1)

            @block.vector
            def _(dve):
                dve.wait_ge(table_in, 48)
                for u, (tile, c) in enumerate(units):
                    dve.wait_ge(rotated, u + 1)
                    dve.tensor_tensor(t[:, u % 2, 0], ps[u % 2][:, 0:C], sin[:, cols(c)], ALU.mult).then_inc(sin_done, 1)
                    dve.wait_ge(sin_done, u + 1)
                    dve.wait_ge(cos_done, u + 1)
                    dve.tensor_tensor(qk[:, tile, cols(c)], t[:, u % 2, 0], t[:, u % 2, 1], ALU.add).then_inc(done, 1)
                for g in range(4):
                    dve.wait_ge(done, 3 * g + 3)
                    dve.tensor_scalar(qk[:, g, :], qk[:, g, :], HD ** -0.5, None, ALU.mult)


def rows_and_gmlp(nc, i, o, sem, sb, banks, gT, qk, uv, vtok, gates, ident):
    with ExitStack() as ctx:
        ws = sb(ctx, "ws", [P, 8, P])
        wsT = sb(ctx, "wsT", [P, 8, P])
        wlane = sb(ctx, "wlane", [TS, 8, TS])
        tril = sb(ctx, "tril", [P, P])
        lane = sb(ctx, "lane", [TS, 8, TS])
        bias = sb(ctx, "bias", [P, 4, P])
        ln_g = sb(ctx, "ln_g", [P, 512])
        ln_b = sb(ctx, "ln_b", [P, 512])
        kv = sb(ctx, "kv", [P, 2, 6, P])
        gv = sb(ctx, "gv", [TS, 512])
        vn = sb(ctx, "vn", [P, 2, 512])
        sp_t = sb(ctx, "sp_t", [P, 2, 4, P])
        stat = sb(ctx, "stat", [P, 2, 6])
        mom = sb(ctx, "mom", [P, 2, 2])
        dev = sb(ctx, "dev", [P, 2, 2])
        ps = banks(ctx, 8)
        loaded, lane0, lane_in, ws_turned, ws_kept = sem("gm_loaded"), sem("lane0"), sem("lane_in"), sem("ws_turned"), sem("ws_kept")
        a_full, b_full, v_full, s_full = (sem(f"rw_{x}_full") for x in "abvs")
        copied, v_kept, v_rooted, var_ready, chain, vn_ready, s_used = (
            sem(f"rw_{x}") for x in ("copied", "v_kept", "rooted", "var", "chain", "vn", "s_used"))
        gates_done, gv_copied, gv_out = sem("gates_done"), sem("gv_copied"), sem("gv_out")
        kv_out = [sem(f"kv_out{s}") for s in range(2)]
        win_out, ws_in = sem("win_out"), sem("gm_ws_in")
        stored = [0, 0]
        after = []
        for t in range(NT + 1):
            stored[t % 2] += 6 if t >= 4 else 4
            after.append(stored[t % 2])

        def rows(t):
            return P if t < NT else TS

        def at(t):
            return slice(t * P, t * P + rows(t))

        with nc.Block() as block:
            @block.sync
            def _(sp):
                sp.dma_start(ws[:], i["gmlp_ws"][0].rearrange("g i j -> i g j")).then_inc(ws_in, 16)
                sp.dma_start(tril[:], i["c_tril"]).then_inc(ws_in, 16)
                sp.dma_start(lane[:], i["c_lane"]).then_inc(loaded, 16)
                bs = i["gmlp_bs"][0].rearrange("(t a) i -> a t i", a=2)
                for a in range(2):
                    sp.dma_start(bias[HD * a:HD * a + HD], bs[a].partition_broadcast(HD)).then_inc(loaded, 16)
                sp.dma_start(ln_g[:], i["gmlp_ln_g"][0].partition_broadcast(P)).then_inc(loaded, 16)
                sp.dma_start(ln_b[:], i["gmlp_ln_b"][0].partition_broadcast(P)).then_inc(loaded, 16)
                sp.wait_ge(lane0, 1)
                for b in range(NB):
                    for g in range(8):
                        sp.dma_start(wlane[NS * b:NS * b + NS, g, NS * b:NS * b + NS],
                                     i["gmlp_ws"][0, g, 0:NS, 0:NS].rearrange("i j -> j i")).then_inc(lane_in, 16)

            @block.gpsimd
            def _(pool):
                pool.memset(wlane[:], 0.0).then_inc(lane0, 1)
                for name, state in (("new_win_k_s", "state_win_k"), ("new_win_v_s", "state_win_v")):
                    pool.dma_start(o[name][0, :, 0:WIN - NS].rearrange("b t h d -> b (t h d)"),
                                   i[state][0, :, NS:WIN].rearrange("b t h d -> b (t h d)")).then_inc(win_out, 16)
                for t in range(NT + 1):
                    pool.wait_ge(copied, 2 * t + 2)
                    s = t % 2
                    flat = "t h d -> t (h d)"
                    for n, name in enumerate(("cmp_k", "cmp_v", "slc_k", "slc_v", "win_k", "win_v")):
                        if t < NT:
                            if n >= 4 and t < 4:
                                continue
                            dst = o[f"new_{name}_p"][0, 0].rearrange(flat)
                            r0 = t * P - (WIN if n >= 4 else 0)
                            dst = dst[r0:r0 + P]
                        elif n < 4:
                            dst = o[f"new_{name}_s"][0].rearrange("b s h d -> (b s) (h d)")
                        else:
                            dst = o[f"new_{name}_s"][0, :, WIN - NS:WIN].rearrange("b s h d -> b s (h d)")
                        pool.dma_start(dst, kv[0:rows(t), s, n]).then_inc(kv_out[s], 16)
                pool.wait_ge(gv_copied, 1)
                pool.dma_start(o["new_gmlp_v_s"][0].rearrange("b s c -> (b s) c"), gv[:]).then_inc(gv_out, 16)
                pool.wait_ge(gv_out, 16)
                pool.wait_ge(win_out, 32)
                for s in range(2):
                    pool.wait_ge(kv_out[s], 16 * stored[s])

            @block.tensor
            def _(pe):
                def turn(t):
                    if t >= 2:
                        pe.wait_ge(copied, 2 * t - 2)
                        pe.wait_ge(v_kept, t - 1)
                        pe.wait_ge(gates_done, t - 1)
                    r = rows(t)
                    a, b, v = ps[t % 2], ps[2 + t % 2], ps[4 + t % 2]
                    for n in range(4):
                        last = pe.transpose(a[0:r, n * P:(n + 1) * P], qk[:, 4 + n, at(t)], ident[:])
                    last.then_inc(a_full, 1)
                    for n in range(2):
                        pe.transpose(b[0:r, n * P:(n + 1) * P], qk[:, 8 + n, at(t)], ident[:])
                    pe.transpose(b[0:r, 256:280], gT[:, at(t)], ident[0:24, 0:24]).then_inc(b_full, 1)
                    for n in range(4):
                        last = pe.transpose(v[0:r, n * P:(n + 1) * P], uv[:, 4 + n, at(t)], ident[:])
                    last.then_inc(v_full, 1)

                turn(0)
                pe.wait_ge(ws_in, 32)
                for h in range(2):
                    for g in range(4):
                        last = pe.transpose(ps[6 + h][:, g * P:(g + 1) * P], ws[:, 4 * h + g, :], ident[:])
                    last.then_inc(ws_turned, 1)
                for t in range(NT + 1):
                    if t < NT:
                        turn(t + 1)
                    pe.wait_ge(vn_ready, t + 1)
                    pe.wait_ge(ws_kept, 2)
                    if t >= 2:
                        pe.wait_ge(s_used, t - 1)
                    if t == NT:
                        pe.wait_ge(lane_in, 16 * 64)
                        pe.wait_ge(ws_kept, 3)
                    r = rows(t)
                    for g in range(8):
                        w = wsT[:, g, :] if t < NT else wlane[:, g, :]
                        a = HD * (g % 2)
                        last = pe.matmul(ps[6 + t % 2][a:a + HD, (g // 2) * P:(g // 2) * P + r], vn[0:r, t % 2, g * HD:(g + 1) * HD], w,
                                         start=True, stop=True, skip_group_check=True)
                    last.then_inc(s_full, 1)

            @block.scalar
            def _(act):
                for t in range(NT + 1):
                    r, s = rows(t), t % 2
                    if t >= 2:
                        act.wait_ge(kv_out[s], 16 * after[t - 2])
                    act.wait_ge(a_full, t + 1)
                    act.copy(kv[0:r, s, 0:4].rearrange("p a c -> p (a c)"), ps[s][0:r, :]).then_inc(copied, 1)
                    act.wait_ge(b_full, t + 1)
                    act.copy(kv[0:r, s, 4:6].rearrange("p a c -> p (a c)"), ps[2 + s][0:r, 0:256]).then_inc(copied, 1)
                    act.activation(gates[0:r, t, :], ps[2 + s][0:r, 256:280], ACT.Sigmoid).then_inc(gates_done, 1)
                    act.wait_ge(var_ready, t + 1)
                    act.sqrt(dev[0:r, s, 0:1], dev[0:r, s, 0:1]).then_inc(v_rooted, 1)

            @block.vector
            def _(dve):
                ch = Chain(dve, chain)
                dve.wait_ge(ws_in, 32)
                for h in range(2):
                    dve.wait_ge(ws_turned, h + 1)
                    dve.tensor_tensor(wsT[:, 4 * h:4 * h + 4, :], ps[6 + h][:].rearrange("p (g c) -> p g c", g=4),
                                      tril[:].unsqueeze(1).to_broadcast([P, 4, P]), ALU.mult).then_inc(ws_kept, 1)

                def layer_norm(t):
                    r, s = rows(t), t % 2
                    v = ps[4 + s][0:r, :]
                    dve.wait_ge(v_full, t + 1)
                    ch(dve.bn_stats(stat[0:r, s], v))
                    ch(dve.bn_aggr(mom[0:r, s], stat[0:r, s]))
                    dve.tensor_scalar(dev[0:r, s, 0:1], mom[0:r, s, 1:2], EPS, None, ALU.add).then_inc(var_ready, 1)
                    if t < NT:
                        dve.wait_ge(copied, 2 * t + 2)
                        dve.tensor_copy(vtok[:, t], kv[:, s, 3:6:2])
                    else:
                        dve.tensor_copy(gv[:], v).then_inc(gv_copied, 1)
                    dve.wait_ge(v_rooted, t + 1)
                    ch(dve.reciprocal(dev[0:r, s, 1:2], dev[0:r, s, 0:1]))
                    if t >= 2:
                        dve.wait_ge(s_full, t - 1)
                    dve.tensor_scalar(vn[0:r, s], v, mom[0:r, s, 0:1], dev[0:r, s, 1:2], ALU.subtract, ALU.mult).then_inc(v_kept, 1)
                    dve.wait_ge(v_kept, t + 1)
                    ch(dve.tensor_tensor(vn[0:r, s], vn[0:r, s], ln_g[0:r], ALU.mult))
                    dve.tensor_tensor(vn[0:r, s], vn[0:r, s], ln_b[0:r], ALU.add).then_inc(vn_ready, 1)

                def spatial(t):
                    r, s = rows(t), t % 2
                    dve.wait_ge(s_full, t + 1)
                    y = ps[6 + s][:].rearrange("p (a c) -> p a c", a=4)
                    if t < NT:
                        dve.tensor_tensor(sp_t[:, s], y, bias[:], ALU.add).then_inc(s_used, 1)
                    else:
                        dve.tensor_tensor(sp_t[:, s, :, 0:TS].rearrange("p a (b i) -> p a b i", b=NB),
                                          y[:, :, 0:TS].rearrange("p a (b i) -> p a b i", b=NB),
                                          bias[:, :, 0:NS].unsqueeze(2).to_broadcast([P, 4, NB, NS]), ALU.add).then_inc(s_used, 1)
                    dve.wait_ge(s_used, t + 1)
                    dve.tensor_tensor(uv[:, 0:4, at(t)], sp_t[:, s, :, 0:r], uv[:, 0:4, at(t)], ALU.mult)

                dve.wait_ge(loaded, 16 * 5)
                layer_norm(0)
                for t in range(NT + 1):
                    if t == NT - 2:
                        dve.wait_ge(lane_in, 16 * 64)
                        dve.tensor_tensor(wlane[:], wlane[:], lane[:], ALU.mult).then_inc(ws_kept, 1)
                    if t < NT:
                        layer_norm(t + 1)
                    spatial(t)


def compress(nc, i, o, sem, sb, banks, uv, ck, cv, ident):
    with ExitStack() as ctx:
        w1 = uv[:, 4:8, :].rearrange("p a t -> p (a t)")[:, 0:2 * 16 * P].rearrange("p (k j f) -> p k j f", k=2, j=16)
        w2 = sb(ctx, "w2", [P, 2, HD])
        pe_in = sb(ctx, "pe_in", [P, 2, 16])
        pe_sum = sb(ctx, "pe_sum", [P, 2])
        table = sb(ctx, "table", [1, NB * PAGES], I32)
        page = sb(ctx, "page", [P, 2, 4, 2 * P])
        pairs = sb(ctx, "pairs", [P, 2, SRC, PAIRS])
        hid = sb(ctx, "hid", [P, 2, SRC * CMP])
        ps = banks(ctx, 8)
        loaded, table_in, chain = sem("cmp_loaded"), sem("cmp_table"), sem("cmp_chain")
        page_in = [[[sem(f"page_in{k}{s}{q}") for q in range(2)] for s in range(2)] for k in range(2)]
        turned = [sem(f"pair_turned{k}") for k in range(2)]
        kept = [[sem(f"pair_kept{k}{h}") for h in range(2)] for k in range(2)]
        summed, bias_sum, bias_kept, gelu_done, out_done = (sem(f"cmp_{x}") for x in ("summed", "bsum", "bias", "gelu", "out"))
        rest_kept = sem("cmp_rest")
        halves = [(0, 5), (5, SRC)]
        pools = ("cache_cmp_k", "cache_cmp_v")

        def gather(eng, q):
            eng.wait_ge(table_in, 16)
            for k in range(2):
                rows = i[pools[k]][0].rearrange("g (p a) h d -> g p (a h d)", a=2)
                with eng.Fori(0, NB // 2) as it:
                    for s in range(2):
                        eng.wait_ge(turned[k], 4 * it + 2 * s + 2)
                        if k == 1:
                            eng.wait_ge(turned[0], 4 + 2 * SRC)
                        for j in range(q, PAGES, 2):
                            at = eng.value_load(table[0:1, bass.ds((2 * it + s) * PAGES + j, 1)], min_val=0, max_val=N_POOL - 1)
                            eng.dma_start(page[HD * q:HD * q + HD, s, j // 2],
                                          rows[bass.ds(at, 1)].rearrange("g p c -> (g p) c")).then_inc(page_in[k][s][q], 16)
                if q == 0:
                    eng.wait_ge(turned[k], 2 * NB + 2)
                    own = o[("new_cmp_k_p", "new_cmp_v_p")[k]][0, 0].rearrange("(j p a) h d -> p j (a h d)", a=2, p=P)
                    eng.dma_start(page[:, 0], own).then_inc(page_in[k][0][0], 16)

        with nc.Block() as block:
            @block.sync
            def _(sp):
                sp.dma_start(table[:], i["page_table"].rearrange("(o b) j -> o (b j)", o=1)).then_inc(table_in, 16)
                for k in range(2):
                    sp.dma_start(w1[:, k], i["cmp_w1"][0, k].rearrange("(j a) d f -> (a d) j f", a=2)).then_inc(loaded, 16)
                    sp.dma_start(pe_in[:, k], i["cmp_pe"][0, k].rearrange("(j a) d -> (a d) j", a=2)).then_inc(loaded, 16)
                sp.dma_start(w2[:], i["cmp_w2"][0].rearrange("k f d -> f k d")).then_inc(loaded, 16)
                gather(sp, 0)

            @block.gpsimd
            def _(pool):
                gather(pool, 1)

            @block.tensor
            def _(pe):
                def turn(k, s):
                    for a in range(2):
                        for j in range(4):
                            last = pe.transpose(ps[2 * a + s][:, j * P:(j + 1) * P], page[:, s, j, P * a:P * a + P], ident[:])
                        last.then_inc(turned[k], 1)

                for k in range(2):
                    pe.sem_inc(turned[k], 4)
                    with pe.Fori(0, NB // 2) as it:
                        for s in range(2):
                            for q in range(2):
                                pe.wait_ge(page_in[k][s][q], 8 * PAGES * it + 8 * PAGES)
                            pe.wait_ge(kept[k][0], 2 * it + s + 1)
                            pe.wait_ge(kept[k][1], 2 * it + s + 1)
                            turn(k, s)
                    pe.wait_ge(page_in[k][0][0], 8 * PAGES * 4 + 16)
                    pe.wait_ge(kept[k][0], NB + 1)
                    pe.wait_ge(kept[k][1], NB + 1)
                    turn(k, 0)
                    pe.wait_ge(kept[k][0], SRC + 2)
                    pe.wait_ge(kept[k][1], SRC + 2)
                    if k == 0:
                        pe.wait_ge(loaded, 16 * 5)
                        for kk in range(2):
                            for j in range(16):
                                last = pe.matmul(ps[4][:, kk:kk + 1], w1[:, kk, j], pe_in[:, kk, j:j + 1], start=j == 0, stop=j == 15)
                        last.then_inc(bias_sum, 1)
                        pe.wait_ge(bias_kept, 1)
                    for h in range(2):
                        for n, (b0, b1) in enumerate(halves):
                            if k == 1:
                                pe.wait_ge(gelu_done, 2 * h + n + 1)
                            for j in range(16):
                                last = pe.matmul(ps[4 + 2 * h + n][:, 0:(b1 - b0) * CMP], w1[:, k, j],
                                                 pairs[:, h, b0:b1, j:j + 8 * (CMP - 1) + 1:8], start=j == 0, stop=j == 15)
                            last.then_inc(summed, 1)
                    pe.wait_ge(gelu_done, 4 * k + 4)
                    if k == 0:
                        for h in range(2):
                            for n, (b0, b1) in enumerate(halves):
                                last = pe.matmul(ps[n][HD * h:HD * h + HD, 0:(b1 - b0) * CMP], w2[:, 0], hid[:, h, b0 * CMP:b1 * CMP],
                                                 start=True, stop=True, skip_group_check=True)
                        last.then_inc(out_done, 1)
                        pe.wait_ge(rest_kept, 2)
                    else:
                        for b in range(SRC):
                            for h in range(2):
                                at = P * (b % 4) + HD * h
                                last = pe.matmul(ps[b // 4][0:CMP, at:at + HD], hid[:, h, b * CMP:(b + 1) * CMP], w2[:, 1],
                                                 start=True, stop=True, skip_group_check=True)
                        last.then_inc(out_done, 1)

            def keep(eng, h, copy):
                for k in range(2):
                    eng.sem_inc(kept[k][h], 2)
                    with eng.Fori(0, NB // 2) as it:
                        for s in range(2):
                            eng.wait_ge(turned[k], 4 * it + 2 * s + h + 5)
                            for hh in range(2):
                                last = copy(pairs[HD * h:HD * h + HD, hh, bass.ds(2 * it + s, 1), :].rearrange("p a t -> p (a t)"),
                                            ps[2 * h + s][HD * hh:HD * hh + HD, :])
                            last.then_inc(kept[k][h], 1)
                    eng.wait_ge(turned[k], 2 * NB + h + 5)
                    for hh in range(2):
                        last = copy(pairs[HD * h:HD * h + HD, hh, NB, :], ps[2 * h][HD * hh:HD * hh + HD, :])
                    last.then_inc(kept[k][h], 1)
                    if h == 0:
                        if k == 0:
                            eng.wait_ge(bias_kept, 1)
                        for hh in range(2):
                            for n, (b0, b1) in enumerate(halves):
                                eng.wait_ge(summed, 4 * k + 2 * hh + n + 1)
                                if k == 1 and hh == 0 and n == 0:
                                    eng.wait_ge(out_done, 1)
                                eng.activation(hid[:, hh, b0 * CMP:b1 * CMP], ps[4 + 2 * hh + n][:, 0:(b1 - b0) * CMP],
                                               ACT.Gelu_apprx_tanh, bias=pe_sum[:, k:k + 1]).then_inc(gelu_done, 1)
                    elif k == 0:
                        eng.wait_ge(bias_sum, 1)
                        eng.tensor_copy(pe_sum[:], ps[4][:, 0:2]).then_inc(bias_kept, 1)
                        eng.wait_ge(out_done, 1)
                        for n, (b0, b1) in enumerate(halves):
                            eng.tensor_copy(ck[:, b0:b1, :].rearrange("p b n -> p (b n)"), ps[n][:, 0:(b1 - b0) * CMP]).then_inc(rest_kept, 1)

            @block.scalar
            def _(act):
                keep(act, 0, act.copy)

            @block.vector
            def _(dve):
                keep(dve, 1, dve.tensor_copy)
                dve.wait_ge(out_done, 2)
                for n in range(3):
                    b0, b1 = 4 * n, min(4 * n + 4, SRC)
                    dve.tensor_copy(cv[:, b0:b1, :].rearrange("p b c -> p (b c)"), ps[n][0:CMP, 0:(b1 - b0) * P])


def attend_prompt(nc, i, sem, sb, banks, qk, vtok, gates, ck, cv, oT, ident):
    BOTH = 2 * CMP
    with ExitStack() as ctx:
        diag = sb(ctx, "diag", [P, P])
        far = sb(ctx, "far", [P, P])
        seen = sb(ctx, "seen", [P, NT, CMP])
        hidden = sb(ctx, "hidden", [P, NT, CMP])
        ck_both = sb(ctx, "ck_both", [P, BOTH])
        cv_both = sb(ctx, "cv_both", [BOTH, P])
        cs = sb(ctx, "cs", [P, 8, CMP])
        probs = sb(ctx, "probs", [P, 2, NP])
        turned = sb(ctx, "turned", [P, 2, 8, P])
        c_turned = sb(ctx, "c_turned", [BOTH, 2, G, P])
        scale = sb(ctx, "scale", [P, 2, P])
        factor = sb(ctx, "factor", [P, 4])
        mx = sb(ctx, "mx", [P, 4])
        cmx = sb(ctx, "cmx", [P, 8])
        total = sb(ctx, "total", [P, 4])
        ctotal = sb(ctx, "ctotal", [P, 8])
        ps = banks(ctx, 4)
        wide = [ctx.enter_context(nc.psum_tensor(f"scores{k}", [P, 1024], F32)) for k in range(2)]
        loaded, cleared, both_ready, cv_in = sem("mask_in"), sem("at_cleared"), sem("at_ck_both"), sem("at_cv_both")
        score, peak, expd, shown, pt, pv = (sem(f"at_{x}") for x in ("score", "peak", "exp", "shown", "pt", "pv"))
        pt_free = [sem(f"at_pt_free{k}") for k in range(2)]
        chain, divided, scaled, out_kept = sem("at_chain"), sem("at_divided"), sem("at_scaled"), sem("at_out_kept")
        units = [(t, None, None, "cmp") if n < 0 else (t, n // 4, n // 2 % 2, ("sel", "win")[n % 2])
                 for t in range(NT) for n in range(-1, 16)]

        def blocks(u):
            t, _, _, kind = units[u]
            return G if kind == "cmp" else t + 1 if kind == "sel" else min(t + 1, 5)

        def heads_done(u):
            return u + 1 - (u // 17 + 1)

        def last_of_group(u):
            _, _, h, kind = units[u]
            return kind == "win" and h == 1

        first_group = [0]
        for u in range(len(units)):
            first_group.append(first_group[u] + -(-blocks(u) // 4))

        def group_list(u):
            return [(n, 4 * j, min(4 * j + 4, blocks(u))) for j, n in enumerate(range(first_group[u], first_group[u + 1]))]

        with nc.Block() as block:
            @block.sync
            def _(sp):
                for dst, name in ((diag, "c_diag"), (far, "c_far"), (seen, "c_seen"), (hidden, "c_hidden")):
                    sp.dma_start(dst[:], i[name]).then_inc(loaded, 16)
                sp.wait_ge(cleared, 2)
                for h in range(2):
                    sp.dma_start(cv_both[CMP * h:CMP * h + CMP, HD * h:HD * h + HD], cv[:, NB, HD * h:HD * h + HD]).then_inc(cv_in, 16)

            @block.gpsimd
            def _(pool):
                pool.memset(ck_both[:], 0.0).then_inc(cleared, 1)
                pool.memset(cv_both[:], 0.0).then_inc(cleared, 1)
                pool.wait_ge(cleared, 2)
                for h in range(2):
                    pool.tensor_copy(ck_both[HD * h:HD * h + HD, CMP * h:CMP * h + CMP], ck[HD * h:HD * h + HD, NB, :]).then_inc(both_ready, 1)
                for u, (t, g, h, kind) in enumerate(units):
                    if kind == "cmp":
                        continue
                    j = 3 * (4 * h + g) + (1 if kind == "sel" else 2)
                    pool.wait_ge(divided, heads_done(u))
                    if u >= 2:
                        pool.wait_ge(pt, first_group[u - 1])
                    pool.tensor_scalar(scale[:, u % 2], ident[:], factor[:, u % 4:u % 4 + 1], gates[:, t, j:j + 1], ALU.mult, ALU.mult).then_inc(scaled, 1)

            @block.tensor
            def _(pe):
                def scores(u):
                    t, g, h, kind = units[u]
                    s = wide[u % 2]
                    if u >= 2:
                        pe.wait_ge(expd, u - 1)
                    qt = slice(t * P, t * P + P)
                    if kind == "cmp":
                        for gg in range(G):
                            last = pe.matmul(s[:, gg * BOTH:(gg + 1) * BOTH], qk[:, gg, qt], ck_both[:], start=True, stop=True)
                    else:
                        at = slice(HD * h, HD * h + HD)
                        tile = 6 if kind == "sel" else 8
                        k0 = 0 if kind == "sel" else max(t - 4, 0) * P
                        n = blocks(u) * P
                        for c in range(0, n, 512):
                            w = min(512, n - c)
                            last = pe.matmul(s[:, c:c + w], qk[at, g, qt], qk[at, tile, k0 + c:k0 + c + w], start=True, stop=True)
                    last.then_inc(score, 1)

                def turn(u):
                    t, _, _, kind = units[u]
                    if kind == "cmp":
                        pe.wait_ge(shown, t + 1)
                    else:
                        pe.wait_ge(scaled, heads_done(u))
                    for n, b0, b1 in group_list(u):
                        if n >= 2:
                            pe.wait_ge(pt_free[n % 2], n // 2)
                        for b in range(b0, b1):
                            at = slice((b - b0) * P, (b - b0 + 1) * P)
                            if kind == "cmp":
                                last = pe.transpose(ps[n % 2][0:BOTH, at], probs[:, u % 2, b * BOTH:(b + 1) * BOTH], ident[:])
                            else:
                                last = pe.matmul(ps[n % 2][:, at], probs[:, u % 2, b * P:(b + 1) * P], scale[:, u % 2], start=True, stop=True)
                        last.then_inc(pt, 1)

                def values(u):
                    t, g, h, kind = units[u]
                    if kind == "cmp":
                        return
                    out = ps[2 + g % 2]
                    if kind == "sel" and h == 0:
                        if t or g >= 2:
                            pe.wait_ge(out_kept, G * t + g - 1)
                        if g == 0:
                            n = first_group[17 * t]
                            pe.wait_ge(pt_free[n % 2], n // 2 + 1)
                        pe.matmul(out[:, 0:P], cv_both[:], c_turned[:, t % 2, g], start=True, stop=False, skip_group_check=True)
                    k0 = 0 if kind == "sel" else max(t - 4, 0)
                    for n, b0, b1 in group_list(u):
                        pe.wait_ge(pt_free[n % 2], n // 2 + 1)
                        for b in range(b0, b1):
                            last = pe.matmul(out[HD * h:HD * h + HD, 0:P], vtok[:, k0 + b, int(kind == "win"), HD * h:HD * h + HD], turned[:, u % 2, b],
                                             start=False, stop=last_of_group(u) and b == blocks(u) - 1, tile_position=(0, HD * h),
                                             skip_group_check=True)
                    last.then_inc(pv, 1)

                pe.wait_ge(loaded, 64)
                pe.wait_ge(both_ready, 2)
                scores(0)
                pe.wait_ge(cv_in, 32)
                for u in range(len(units)):
                    if u + 1 < len(units):
                        scores(u + 1)
                    if u > 0:
                        values(u - 1)
                    turn(u)
                values(len(units) - 1)

            def empty(eng, copy, which, u):
                for n, b0, b1 in group_list(u):
                    if n % 2 == which:
                        eng.wait_ge(pt, n + 1)
                        if u >= 3:
                            eng.wait_ge(pv, heads_done(u - 2))
                        if units[u][3] == "cmp":
                            dst, r = c_turned[:, units[u][0] % 2], BOTH
                        else:
                            dst, r = turned[:, u % 2, b0:b1, :], P
                        copy(dst.rearrange("p b c -> p (b c)"), ps[n % 2][0:r, 0:(b1 - b0) * P]).then_inc(pt_free[which], 1)

            @block.scalar
            def _(act):
                def exp(u):
                    act.wait_ge(peak, u + 1)
                    if u >= 2:
                        act.wait_ge(pt, first_group[u - 1])
                    if units[u][3] == "cmp":
                        act.activation(probs[:, u % 2, 0:8 * CMP], cs[:].rearrange("p h n -> p (h n)"), ACT.Exp).then_inc(expd, 1)
                    else:
                        n = blocks(u) * P
                        act.activation(probs[:, u % 2, 0:n], wide[u % 2][:, 0:n], ACT.Exp, bias=mx[:, u % 4:u % 4 + 1],
                                       accum_out=total[:, u % 4:u % 4 + 1]).then_inc(expd, 1)

                def keep(u):
                    t, g, _, _ = units[u]
                    act.wait_ge(pv, heads_done(u))
                    act.copy(oT[:, g, t * P:(t + 1) * P], ps[2 + g % 2][:, 0:P]).then_inc(out_kept, 1)

                exp(0)
                for u in range(len(units)):
                    if u + 1 < len(units):
                        exp(u + 1)
                    empty(act, act.copy, 1, u)
                    if u > 0 and last_of_group(u - 1):
                        keep(u - 1)
                keep(len(units) - 1)

            @block.vector
            def _(dve):
                ch = Chain(dve, chain)

                def peaks(u):
                    t, _, _, kind = units[u]
                    s = wide[u % 2]
                    dve.wait_ge(score, u + 1)
                    if kind == "cmp":
                        ch(dve.tensor_tensor(cs[:], s[:, 0:8 * CMP].rearrange("p (h n) -> p h n", h=8),
                                             hidden[:, t].unsqueeze(1).to_broadcast([P, 8, CMP]), ALU.add))
                        ch(dve.tensor_reduce(cmx[:], cs[:], X, ALU.max))
                        dve.tensor_tensor(cs[:], cs[:], cmx[:].unsqueeze(2).to_broadcast([P, 8, CMP]), ALU.subtract).then_inc(peak, 1)
                        return
                    n = blocks(u) * P
                    ch(dve.tensor_tensor(s[:, n - P:n], s[:, n - P:n], diag[:], ALU.add))
                    if kind == "win" and t >= 4:
                        ch(dve.tensor_tensor(s[:, 0:P], s[:, 0:P], far[:], ALU.add))
                    dve.tensor_reduce(mx[:, u % 4:u % 4 + 1], s[:, 0:n], X, ALU.max, negate=True).then_inc(peak, 1)

                def show(u):
                    t = units[u][0]
                    p = probs[:, u % 2, 0:8 * CMP].rearrange("p (h n) -> p h n", h=8)
                    dve.wait_ge(expd, u + 1)
                    ch(dve.tensor_tensor(p, p, seen[:, t].unsqueeze(1).to_broadcast([P, 8, CMP]), ALU.mult))
                    ch(dve.tensor_reduce(ctotal[:], p, X, ALU.add))
                    ch(dve.tensor_scalar(ctotal[:], ctotal[:], 1e-30, None, ALU.max))
                    ch(dve.reciprocal(ctotal[:], ctotal[:]))
                    gate = gates[:, t, :].rearrange("p (h g j) -> p g h j", h=2, g=4)[:, :, :, 0]
                    ch(dve.tensor_tensor(ctotal[:].rearrange("p (g h) -> p g h", g=4), ctotal[:].rearrange("p (g h) -> p g h", g=4), gate, ALU.mult))
                    dve.tensor_tensor(p, p, ctotal[:].unsqueeze(2).to_broadcast([P, 8, CMP]), ALU.mult).then_inc(shown, 1)

                dve.wait_ge(loaded, 64)
                peaks(0)
                for u in range(len(units)):
                    if units[u][3] == "cmp":
                        show(u)
                    else:
                        dve.wait_ge(expd, u + 1)
                        dve.reciprocal(factor[:, u % 4:u % 4 + 1], total[:, u % 4:u % 4 + 1]).then_inc(divided, 1)
                    if u + 1 < len(units):
                        peaks(u + 1)
                    empty(dve, dve.tensor_copy, 0, u)


def attend_sample(nc, i, o, sem, sb, banks, qk, uv, vtok, gates, ck, cv, oT, ident):
    SEL, WINC = 0, 1532
    CMPC, ROWG, SC0, SC1 = 0, 64, 96, 112
    PS_, PW, PC = 0, 1028, 1544
    with ExitStack() as ctx:
        spare = flat(uv[:, 4:8, :])
        ring = [x.rearrange("p (j c) -> p j c", j=12) for x in (
            spare[:, 0:12 * P], spare[:, 12 * P:24 * P], vtok[:].rearrange("p t s c -> p (t s c)")[:, 0:12 * P])]
        probs = qk[:, 4:6, :].rearrange("p a t -> p (a t)")
        table = sb(ctx, "table_s", [1, NB * PAGES], I32)
        kT = sb(ctx, "kT", [P, 2, 12 * P])
        pT = sb(ctx, "pT", [P, 16, P])
        q_rows = sb(ctx, "q_rows", [P, NB, 32])
        v_new = sb(ctx, "v_new", [NS, 2, NB, P])
        same = sb(ctx, "same", [P, P])
        shared = sb(ctx, "shared", [CMP, 16])
        new = sb(ctx, "new", [P, NS])
        old = sb(ctx, "old", [P, NS])
        row_of = sb(ctx, "row_of", [TS, 2, P])
        hg = sb(ctx, "hg", [P, 24])
        block_no = sb(ctx, "block_no", [P, 16])
        small = sb(ctx, "small", [P, 8, 24])
        one = sb(ctx, "one", [P, 12])
        wide = ctx.enter_context(nc.psum_tensor("s_wide", [P, 2048], F32))
        tp = banks(ctx, 2)
        out, misc = banks(ctx, 2)
        loaded, table_in, zeroed, q_ready = sem("sa_loaded"), sem("sa_table"), sem("sa_zeroed"), sem("sa_q")
        ring_in = [[sem(f"sa_ring{s}{q}") for q in range(2)] for s in range(3)]
        turned, score, pv = (sem(f"sa_{x}") for x in ("turned", "score", "pv"))
        kept = [sem(f"sa_kept{k}") for k in range(2)]
        chain, ready, expd, cmp_p, probs_ready, summed, small_mm = (sem(f"sa_{x}") for x in ("chain", "ready", "exp", "cmp_p", "probs", "summed", "mm"))
        small_kept = sem("sa_small_kept")
        per = 12 + 1 + 4

        def gather(eng, q):
            eng.wait_ge(table_in, 16)
            for grp in range(2):
                for v, (pool, state) in enumerate((("cache_slc_k", "state_win_k"), ("cache_slc_v", "state_win_v"))):
                    pages = i[pool][0].rearrange("g p h d -> g p (h d)")
                    for bb in range(4):
                        b, load = 4 * grp + bb, 8 * grp + 4 * v + bb
                        s = load % 3
                        if load >= 3:
                            g0, v0, bb0 = (load - 3) // 8, (load - 3) // 4 % 2, (load - 3) % 4
                            if v0 == 0:
                                eng.wait_ge(turned, per * g0 + 3 * bb0 + 3)
                            else:
                                eng.wait_ge(pv, 4 * g0 + bb0 + 1)
                        with eng.Fori(0, PAGES // 2) as j:
                            at = eng.value_load(table[0:1, bass.ds(2 * j + (b * PAGES + q), 1)], min_val=0, max_val=N_POOL - 1)
                            eng.dma_start(ring[s][:, bass.ds(2 * j + q, 1)].rearrange("p j c -> p (j c)"),
                                          pages[bass.ds(at, 1)].rearrange("g p c -> (g p) c")).then_inc(ring_in[s][q], 16)
                        eng.dma_start(ring[s][:, 8 + 2 * q:10 + 2 * q],
                                      i[state][0, b, 2 * P * q:2 * P * q + 2 * P].rearrange("(j p) h d -> p j (h d)", p=P)).then_inc(ring_in[s][q], 16)

        with nc.Block() as block:
            @block.sync
            def _(sp):
                sp.dma_start(table[:], i["page_table"].rearrange("(o b) j -> o (b j)", o=1)).then_inc(table_in, 16)
                for dst, name in ((same, "c_same"), (shared, "c_shared"), (new, "c_new"), (old, "c_old"), (row_of, "c_row_of"),
                                  (hg, "c_hg"), (block_no, "c_block")):
                    src = i[name].rearrange("p x j -> p (x j)") if name == "c_hg" else i[name]
                    sp.dma_start(dst[:], src).then_inc(loaded, 16)
                sp.dma_start(v_new[:, 0], o["new_slc_v_s"][0].rearrange("b s h d -> s b (h d)")).then_inc(loaded, 16)
                sp.dma_start(v_new[:, 1], o["new_win_v_s"][0, :, WIN - NS:WIN].rearrange("b s h d -> s b (h d)")).then_inc(loaded, 16)
                gather(sp, 0)

            @block.gpsimd
            def _(pool):
                pool.memset(q_rows[:], 0.0).then_inc(zeroed, 1)
                gather(pool, 1)

            def arrived(pe, load):
                for q in range(2):
                    pe.wait_ge(ring_in[load % 3][q], 16 * 5 * (load // 3 + 1))

            @block.tensor
            def _(pe):
                pe.wait_ge(loaded, 16 * 9)
                pe.wait_ge(q_ready, 2)

                def room(n):
                    if n >= 2:
                        pe.wait_ge(kept[n % 2], n // 2)

                def turn_keys(b):
                    grp, bb = b // 4, b % 4
                    load = 8 * grp + bb
                    arrived(pe, load)
                    for j in range(3):
                        n = per * grp + 3 * bb + j
                        room(n)
                        for m in range(4):
                            last = pe.transpose(tp[n % 2][:, m * P:(m + 1) * P], ring[load % 3][:, 4 * j + m, :], ident[:])
                        last.then_inc(turned, 1)

                def scores(b):
                    grp, bb = b // 4, b % 4
                    for j in range(3):
                        n = per * grp + 3 * bb + j
                        pe.wait_ge(kept[n % 2], n // 2 + 1)
                    if bb == 0 and grp > 0:
                        pe.wait_ge(expd, 3 * grp)
                    q = q_rows[:, b, :]
                    r = slice(32 * bb, 32 * bb + 32)
                    k, new_k = kT[:, b % 2], slice(NP + NS * b, NP + NS * b + NS)
                    for at, rhs in ((CMPC, ck[:, b, :]), (0, k[:, 0:512]), (512, k[:, 512:1024]), (1024, qk[:, 6, new_k]),
                                    (WINC, qk[:, 8, new_k]), (1536, k[:, 1024:1536])):
                        to = misc if rhs.shape[-1] == CMP else wide
                        last = pe.matmul(to[r, at:at + rhs.shape[-1]], q, rhs, start=True, stop=True, skip_group_check=True,
                                         tile_position=(0, 32 * bb))
                    last.then_inc(score, 1)

                def group(n, blocks):
                    room(n)
                    for m, (at, w) in enumerate(blocks):
                        last = pe.transpose(tp[n % 2][0:w, m * P:(m + 1) * P], probs[:, at:at + w], ident[:])
                    last.then_inc(turned, 1)

                for grp in range(2):
                    b0, n0 = 4 * grp, per * grp
                    pe.matmul(misc[:, ROWG:ROWG + 24], row_of[:, grp], gates[0:TS, NT, :], start=True, stop=True,
                              skip_group_check=True).then_inc(small_mm, 1) if grp == 0 else None
                    turn_keys(b0)
                    for b in range(b0, b0 + 4):
                        if b < b0 + 3:
                            turn_keys(b + 1)
                        scores(b)
                    if grp == 1:
                        pe.matmul(misc[:, ROWG:ROWG + 24], row_of[:, grp], gates[0:TS, NT, :], start=True, stop=True,
                                  skip_group_check=True).then_inc(small_mm, 1)
                    pe.wait_ge(cmp_p, grp + 1)
                    group(n0 + 12, [(PC, CMP)])
                    pe.wait_ge(kept[(n0 + 12) % 2], (n0 + 12) // 2 + 1)
                    pe.matmul(misc[:, SC0:SC0 + 16], pT[0:CMP, 15], shared[:], start=True, stop=True, skip_group_check=True).then_inc(small_mm, 1)
                    pe.wait_ge(small_kept, grp + 1)
                    pe.matmul(misc[:, SC1:SC1 + 16], same[:], small[:, 3, 0:16], start=True, stop=True, skip_group_check=True).then_inc(small_mm, 1)
                    pe.wait_ge(probs_ready, grp + 1)
                    group(n0 + 13, [(PS_ + m * P, P) for m in range(4)])
                    group(n0 + 14, [(PS_ + m * P, P) for m in range(4, 8)])
                    group(n0 + 15, [(PW + NS + m * P, P) for m in range(4)])
                    group(n0 + 16, [(PS_ + NP, NS), (PW, NS), (PC, CMP)])
                    for n in range(n0 + 13, n0 + 17):
                        pe.wait_ge(kept[n % 2], n // 2 + 1)
                    for b in range(b0, b0 + 4):
                        load = 8 * grp + 4 + b % 4
                        arrived(pe, load)
                        r = slice(32 * (b % 4), 32 * (b % 4) + 32)
                        v = ring[load % 3]
                        terms = [(v[:, j], pT[:, j, r]) for j in range(12)]
                        terms += [(v_new[:, 0, b], pT[0:NS, 12, r]), (v_new[:, 1, b], pT[0:NS, 13, r]), (cv[:, b], pT[0:CMP, 14, r])]
                        for m, (lhsT, rhs) in enumerate(terms):
                            last = pe.matmul(out[:, 32 * b:32 * b + 32], lhsT, rhs, start=m == 0, stop=m == len(terms) - 1,
                                             skip_group_check=True)
                        last.then_inc(pv, 1)

            def keep(eng, copy, which, grp, ns):
                for n in ns:
                    if n % 2 != which:
                        continue
                    eng.wait_ge(turned, n + 1)
                    m = n - per * grp
                    src = tp[n % 2]
                    if m < 12:
                        b = 4 * grp + m // 3
                        if b >= 2:
                            eng.wait_ge(score, b - 1)
                        copy(kT[:, b % 2, 512 * (m % 3):512 * (m % 3) + 512], src[:]).then_inc(kept[which], 1)
                    elif m == 12:
                        copy(pT[0:CMP, 15], src[0:CMP, 0:P]).then_inc(kept[which], 1)
                    elif m < 16:
                        copy(pT[:, 4 * (m - 13):4 * (m - 13) + 4, :].rearrange("p b c -> p (b c)"), src[:]).then_inc(kept[which], 1)
                    else:
                        copy(pT[0:NS, 12:14].rearrange("p b c -> p (b c)"), src[0:NS, 0:2 * P])
                        copy(pT[0:CMP, 14], src[0:CMP, 2 * P:3 * P]).then_inc(kept[which], 1)

            @block.scalar
            def _(act):
                def exp(src, at, n, col):
                    act.activation(probs[:, at:at + n], (wide if col else misc)[:, src:src + n], ACT.Exp, bias=one[:, col:col + 1],
                                   accum_out=one[:, 5 + col:6 + col]).then_inc(expd, 1)

                for grp in range(2):
                    n0 = per * grp
                    keep(act, act.copy, 1, grp, range(n0, n0 + 12))
                    act.wait_ge(ready, 3 * grp + 1)
                    exp(CMPC, PC, CMP, 0)
                    keep(act, act.copy, 1, grp, [n0 + 12])
                    act.wait_ge(ready, 3 * grp + 3)
                    exp(SEL, PS_, NP + NS, 1)
                    exp(WINC, PW, WIN + NS, 2)
                    keep(act, act.copy, 1, grp, range(n0 + 13, n0 + 17))

            @block.vector
            def _(dve):
                ch = Chain(dve, chain)
                dve.wait_ge(zeroed, 1)
                for h in range(2):
                    r = slice(HD * h, HD * h + HD)
                    dve.tensor_copy(q_rows[r, :, 16 * h:16 * h + 16].rearrange("p b (g s) -> p g b s", g=4),
                                    qk[r, 0:4, NP:T].rearrange("p g (b s) -> p g b s", b=NB)).then_inc(q_ready, 1)
                dve.wait_ge(loaded, 16 * 9)
                for grp in range(2):
                    n0 = per * grp
                    mm = 3 * grp
                    keep(dve, dve.tensor_copy, 0, grp, range(n0, n0 + 12))
                    dve.wait_ge(score, 4 * grp + 4)
                    dve.wait_ge(small_mm, mm + 1)
                    ch(dve.tensor_tensor(small[:, 0], misc[:, ROWG:ROWG + 24], hg[:], ALU.mult))
                    ch(dve.tensor_reduce(small[:, 1, 0:3], small[:, 0].rearrange("p (x j) -> p j x", j=3), X, ALU.add))
                    dve.tensor_reduce(one[:, 0:1], misc[:, CMPC:CMPC + CMP], X, ALU.max, negate=True).then_inc(ready, 1)
                    ch(dve.tensor_tensor(wide[:, NP:NP + NS], wide[:, NP:NP + NS], new[:], ALU.add))
                    ch(dve.tensor_tensor(wide[:, WINC:WINC + NS], wide[:, WINC:WINC + NS], new[:], ALU.add))
                    ch(dve.tensor_tensor(wide[:, 1536:1536 + NS], wide[:, 1536:1536 + NS], old[:], ALU.add))
                    dve.tensor_reduce(one[:, 2:3], wide[:, WINC:2048], X, ALU.max, negate=True).then_inc(ready, 1)
                    dve.wait_ge(expd, 3 * grp + 1)
                    ch(dve.reciprocal(one[:, 10:11], one[:, 5:6]))
                    dve.tensor_scalar(probs[:, PC:PC + CMP], probs[:, PC:PC + CMP], one[:, 10:11], None, ALU.mult).then_inc(cmp_p, 1)
                    keep(dve, dve.tensor_copy, 0, grp, [n0 + 12])
                    dve.wait_ge(small_mm, mm + 2)
                    dve.tensor_copy(small[:, 3, 0:16], misc[:, SC0:SC0 + 16]).then_inc(small_kept, 1)
                    dve.wait_ge(small_mm, mm + 3)
                    ch(dve.tensor_copy(small[:, 4, 0:16], misc[:, SC1:SC1 + 16]))
                    ch(dve.tensor_reduce(one[:, 3:4], small[:, 4, 1:15], X, ALU.min))
                    ch(dve.tensor_scalar(small[:, 5, 1:15], small[:, 4, 1:15], one[:, 3:4], None, ALU.is_equal))
                    ch(dve.tensor_tensor(small[:, 5, 1:15], small[:, 5, 1:15], block_no[:, 1:15], ALU.mult))
                    ch(dve.tensor_reduce(one[:, 4:5], small[:, 5, 1:15], X, ALU.max))
                    ch(dve.tensor_scalar(small[:, 6, 0:16], block_no[:], one[:, 4:5], NEG, ALU.is_equal, ALU.mult))
                    sel = wide[:, 0:NP].rearrange("p (m c) -> p m c", m=16)
                    ch(dve.tensor_tensor(sel, sel, small[:, 6, 0:16].unsqueeze(2).to_broadcast([P, 16, HD]), ALU.add))
                    dve.tensor_reduce(one[:, 1:2], wide[:, 0:NP + NS], X, ALU.max, negate=True).then_inc(ready, 1)
                    dve.tensor_scalar(probs[:, PC:PC + CMP], probs[:, PC:PC + CMP], small[:, 1, 0:1], None, ALU.mult)
                    dve.wait_ge(expd, 3 * grp + 3)
                    ch(dve.reciprocal(one[:, 10:12], one[:, 6:8]))
                    dve.tensor_scalar(probs[:, 0:PW], probs[:, 0:PW], one[:, 10:11], small[:, 1, 1:2], ALU.mult, ALU.mult)
                    dve.tensor_scalar(probs[:, PW:PC], probs[:, PW:PC], one[:, 11:12], small[:, 1, 2:3], ALU.mult, ALU.mult).then_inc(probs_ready, 1)
                    keep(dve, dve.tensor_copy, 0, grp, range(n0 + 13, n0 + 17))
                dve.wait_ge(pv, NB)
                for h in range(2):
                    r = slice(HD * h, HD * h + HD)
                    dve.tensor_copy(oT[r, :, NP:T].rearrange("p g (b s) -> p g b s", b=NB),
                                    out[r, 0:256].rearrange("p (b x) -> p b x", b=NB)[:, :, 16 * h:16 * h + 16].rearrange("p b (g s) -> p g b s", g=4))


def merge(nc, i, sem, sb, banks, hi, lo, oT, uv, qk):
    w = i["w_in"][0].rearrange("(k p) n -> p k n", p=P)
    wa = i["w_branch_a"][0].rearrange("(h g d) n -> h d g n", h=2, g=4)
    wb = i["w_branch_b"][0].rearrange("(k p) n -> p k n", p=P)
    with ExitStack() as ctx:
        slots = sb(ctx, "ab_w", [P, 2, 8, P])
        sg = flat(uv[:, 4:8, :]).rearrange("p (r m c t) -> p r m c t", r=2, m=2, c=CH)
        prod = flat(qk[:, 8:10, :])[:, 0:4 * C].rearrange("p (b m t) -> p b m t", b=2, m=2)
        ps = banks(ctx, 7)
        st = SplitStream(sb, sem, ctx, "mg", KD, 3)
        ab_in = [sem(f"ab_w{s}") for s in range(2)]
        ab_done, ab_freed, sg_used, chain, waited = (sem(x) for x in ("ab_done", "ab_freed", "sg_used", "mg_chain", "ab_waited"))
        with nc.Block() as block:
            @block.sync
            def _(sp):
                with sp.Fori(0, 4) as it:
                    for r in range(2):
                        n = 2 * it + r
                        for m, first in enumerate((GA_COL, GB_COL)):
                            st.load_tile(sp, it, 4, 2 * r + m, halves(st.raw[:, m], w[:, :, bass.ds(n * P + first, P)], KD))
                        sp.wait_ge(ab_done, 6 * it + (3 * r + 3))
                        sp.sem_inc(waited, 1)
                        for h in range(2):
                            sp.dma_start(slots[HD * h:HD * h + HD, r, 0:4], wa[h, :, :, bass.ds(n * P, P)]).then_inc(ab_in[r], 16)
                        sp.dma_start(slots[:, r, 4:8], wb[:, :, bass.ds(n * P, P)]).then_inc(ab_in[r], 16)

            @block.gpsimd
            def _(pool):
                st.start_split(pool)
                st.split_weights(pool, 0, 2 * KD, KD)

            @block.tensor
            def _(pe):
                st.start_multiply(pe)
                pe.sem_inc(ab_done, 6)
                with pe.Fori(0, 4) as it:
                    for r in range(2):
                        for m in range(2):
                            st.multiply_tile(pe, it, 4, 2 * r + m, products(ps, hi, lo))
                        pe.wait_ge(ab_in[r], 48 * it + 48)
                        for c in range(CH):
                            b = (3 * r + c) % 2
                            pe.wait_ge(ab_freed, 6 * it + (3 * r + c + 1))
                            for m, x in enumerate((oT, uv)):
                                for k in range(4):
                                    last = pe.matmul(ps[3 + 2 * b + m][:, 0:C], slots[:, r, 4 * m + k], x[:, k, cols(c)], start=k == 0, stop=k == 3)
                            last.then_inc(ab_done, 1)

            @block.scalar
            def _(act):
                st.start_take(act)
                with act.Fori(0, 4) as it:
                    for r in range(2):
                        for m in range(2):
                            def use(n, b, c):
                                act.wait_ge(sg_used, 6 * it + (3 * r + c + 1))
                                return act.activation(sg[:, r, m, c], ps[b][:, 0:C], ACT.Sigmoid)
                            st.take_tile(act, it, 4, 2 * r + m, use)

            @block.vector
            def _(dve):
                dve.sem_inc(ab_freed, 2)
                dve.sem_inc(sg_used, 6)
                dve.sem_inc(chain, 6)
                with dve.Fori(0, 4) as it:
                    for j in range(6):
                        r, c, b = j // 3, j % 3, j % 2
                        dve.wait_ge(ab_done, 6 * it + (j + 7))
                        dve.wait_ge(st.freed, 12 * it + (6 * r + c + 7))
                        dve.wait_ge(chain, 18 * it + (3 * j + 3))
                        for m in range(2):
                            dve.tensor_tensor(prod[:, b, m], sg[:, r, m, c], ps[3 + 2 * b + m][:, 0:C], ALU.mult).then_inc(chain, 1)
                        dve.wait_ge(chain, 18 * it + (3 * j + 8))
                        dve.sem_inc(ab_freed, 1)
                        dve.sem_inc(sg_used, 1)
                        dve.tensor_tensor(flat(qk[:, bass.ds(2 * it + r, 1), cols(c)]), prod[:, b, 0], prod[:, b, 1], ALU.add).then_inc(chain, 1)


def add_product(nc, name, sem, sb, banks, w, src, hi, lo, xT, x_kept=None):
    w = w.rearrange("(k p) n -> p k n", p=P)
    with ExitStack() as ctx:
        ps = banks(ctx, 6)
        st = SplitStream(sb, sem, ctx, name, KD, 6, rounds_on_act=True)
        rounded, split, x_in = (sem(f"{name}_x_{x}") for x in ("rounded", "split", "in"))
        with nc.Block() as block:
            @block.sync
            def _(sp):
                for n in range(2):
                    st.load_tile(sp, 0, 0, n, halves(st.raw[:, n], w[:, :, n * P:(n + 1) * P], KD))
                if x_kept is not None:
                    sp.dma_start(flat(xT[:]), x_kept).then_inc(x_in, 16)
                st.load(sp, 2, KD - 2, lambda n, raw: halves(raw, w[:, :, bass.ds(n * P + 2 * P, P)], KD))

            @block.gpsimd
            def _(pool):
                st.start_split(pool)
                st.split_weights(pool, 0, KD, KD)

            @block.tensor
            def _(pe):
                st.start_multiply(pe)
                st.multiply(pe, 0, KD, products(ps, hi, lo), (split, 1))

            @block.scalar
            def _(act):
                for c in range(CH):
                    act.copy(hi[:, :, cols(c)], src[:, 0:KD, cols(c)]).then_inc(rounded, 1)
                    if c == 0:
                        st.round_tile(act, 0, 0, 0, KD)
                st.each_tile(act, 0, KD, KD, None, lambda it, m, n: None)

            @block.vector
            def _(dve):
                st.start_take(dve)
                for c in range(CH):
                    dve.wait_ge(rounded, c + 1)
                    dve.tensor_tensor(lo[:, :, cols(c)], src[:, 0:KD, cols(c)], hi[:, :, cols(c)].bitcast(F32), ALU.subtract).then_inc(split, 1)
                if x_kept is not None:
                    dve.wait_ge(x_in, 16)

                def use(n, b, c):
                    x = flat(xT[:, bass.ds(n, 1), cols(c)])
                    return dve.tensor_tensor(x, x, ps[b][:, 0:C], ALU.add)
                st.take(dve, 0, KD, use)


def normed_product(nc, name, sem, sb, banks, w, xT, scratch, hi, lo, dst, gains, g, ones):
    w = w.rearrange("(k p) n -> p k n", p=P)
    with ExitStack() as ctx:
        ps = banks(ctx, 6)
        st = SplitStream(sb, sem, ctx, name, KD, 6)
        norm_x = SplitNorm(sem, name, xT, hi, lo, gains[:, g], ones, ps, scratch)
        with nc.Block() as block:
            @block.sync
            def _(sp):
                st.load(sp, 0, KD, lambda n, raw: halves(raw, w[:, :, bass.ds(n * P, P)], KD))

            @block.gpsimd
            def _(pool):
                st.start_split(pool)
                st.split_tile(pool, 0, 0, 0, KD)
                norm_x.gpsimd(pool)
                st.split_tile(pool, 0, 0, 1, KD)
                st.split_weights(pool, 2, KD - 2, KD)

            @block.tensor
            def _(pe):
                st.start_multiply(pe)
                norm_x.tensor(pe)
                st.multiply(pe, 0, KD, products(ps, hi, lo), norm_x.ready)

            @block.scalar
            def _(act):
                st.start_take(act)
                norm_x.scalar(act)
                st.take(act, 0, KD, lambda n, b, c: act.copy(flat(dst[:, bass.ds(n, 1), cols(c)]), ps[b][:, 0:C]))

            @block.vector
            def _(dve):
                norm_x.vector(dve)


def feed_forward(nc, i, sem, sb, banks, hi, lo, xT, gains, g, ones):
    DEPTH = 4
    GROUPS = [(f, min(DEPTH, KF - f)) for f in range(0, KF, DEPTH)]
    wg, wu, wd = (i[n][0].rearrange("(k p) n -> p k n", p=P) for n in ("w_gate", "w_up", "w_down"))
    with ExitStack() as ctx:
        a_hi = sb(ctx, "a_hi", [P, DEPTH, T], F32R)
        a_lo = sb(ctx, "a_lo", [P, DEPTH, T], F32R)
        sg = sb(ctx, "silu", [P, 2, C])
        act_t = sb(ctx, "ff_act", [P, 2, C])
        ps = banks(ctx, 6)
        st = SplitStream(sb, sem, ctx, "ff", 2 * KD, 3, rounds_on_act=True)
        norm_x = SplitNorm(sem, "ffn", xT, hi, lo, gains[:, g], ones, ps[0::2], sb(ctx, "ffn_norm", [P, SplitNorm.SCRATCH]))
        silu, chain = sem("ff_silu"), sem("ff_chain")
        plan, at = [], 0
        for f, size in GROUPS:
            plan.append((at, at + size, f, size))
            at += size + KD
        with nc.Block() as block:
            @block.sync
            def _(sp):
                for up_at, down_at, f, size in plan:
                    st.load(sp, up_at, size, lambda n, raw: [(raw[:, 0:KD], wg[:, :, bass.ds(n * P + f * P, P)]),
                                                            (raw[:, KD:2 * KD], wu[:, :, bass.ds(n * P + f * P, P)])])
                    st.load(sp, down_at, KD, lambda n, raw: halves(raw, wd[:, f:f + size, bass.ds(n * P, P)], size))

            @block.gpsimd
            def _(pool):
                st.start_split(pool)
                st.split_tile(pool, 0, 0, 0, 2 * KD)
                norm_x.gpsimd(pool)
                st.split_tile(pool, 0, 0, 1, 2 * KD)
                for up_at, down_at, f, size in plan:
                    skip = 0 if f else 2
                    st.split_weights(pool, up_at + skip, size - skip, 2 * KD)
                    st.split_weights(pool, down_at, KD, size)

            @block.tensor
            def _(pe):
                st.start_multiply(pe)
                norm_x.tensor(pe)
                for up_at, down_at, f, size in plan:
                    st.multiply(pe, up_at, size, lambda b, c: [
                        (ps[2 * b + m][:, 0:C], m * KD, [(hi[:, k, cols(c)], lo[:, k, cols(c)]) for k in range(KD)]) for m in range(2)],
                                norm_x.ready if f == 0 else None)
                    st.multiply(pe, down_at, KD, products(ps[0::2], a_hi, a_lo, size), (chain, 3, 6 + 3 * CH * (f + size - 1)))

            @block.scalar
            def _(act):
                norm_x.scalar(act, lambda: st.round_tile(act, 0, 0, 0, 2 * KD))
                for up_at, down_at, f, size in plan:
                    def silus(it, m, n):
                        for c in range(CH):
                            j = CH * (m - up_at) + c
                            act.wait_ge(st.done, 6 * it + (CH * up_at + j + 7))
                            act.wait_ge(chain, 18 * it + (3 * (CH * f + j) + 1))
                            act.activation(sg[:, j % 2], ps[2 * c][:, 0:C], ACT.Silu).then_inc(silu, 1)

                    st.each_tile(act, up_at, size, 2 * KD, size, silus)
                    st.each_tile(act, down_at, KD, size, 2 * KD if f + size < KF else None, lambda it, m, n: None)

            @block.vector
            def _(dve):
                dve.sem_inc(chain, 6)
                st.start_take(dve)
                norm_x.vector(dve)
                for up_at, down_at, f, size in plan:
                    with dve.Fori(0, size // 2) as it:
                        for j in range(6):
                            u = CH * f + j
                            a = act_t[:, j % 2]
                            to_hi, to_lo = (x[:, bass.ds(2 * it + j // 3, 1), cols(j % 3)].rearrange("p a t -> p (a t)") for x in (a_hi, a_lo))
                            dve.wait_ge(silu, 6 * it + (u + 1))
                            dve.tensor_tensor(a, sg[:, j % 2], ps[2 * (j % 3) + 1][:, 0:C], ALU.mult).then_inc(chain, 1)
                            dve.wait_ge(chain, 18 * it + (3 * u + 7))
                            dve.sem_inc(st.freed, 1)
                            dve.tensor_copy(to_hi, a).then_inc(chain, 1)
                            dve.wait_ge(chain, 18 * it + (3 * u + 8))
                            dve.tensor_tensor(to_lo, a, to_hi.bitcast(F32), ALU.subtract).then_inc(chain, 1)

                    def use(n, b, c):
                        x = flat(xT[:, bass.ds(n, 1), cols(c)])
                        return dve.tensor_tensor(x, x, ps[2 * b][:, 0:C], ALU.add)
                    st.take(dve, down_at, KD, use)


def memory(nc, i, o, sem, sb, banks, mkT, mv, ident, ones, gains, g):
    with ExitStack() as outer:
        memT = sb(outer, "memT", [P, KD, NM])
        hmT = sb(outer, "hmT", [P, KD, NM])
        with ExitStack() as ctx:
            rows = sb(ctx, "mem_rows", [P, 2, D])
            tp = banks(ctx, 4)
            mem_in, turned = sem("mem_in"), sem("mem_turned")
            with nc.Block() as block:
                @block.sync
                def _(sp):
                    sp.dma_start(rows[:], i["mem_prompt"][0].rearrange("(m p) c -> p m c", p=P)).then_inc(mem_in, 16)

                @block.tensor
                def _(pe):
                    pe.wait_ge(mem_in, 16)
                    for m in range(2):
                        for h in range(2):
                            for k in range(4):
                                last = pe.transpose(tp[2 * m + h][:, k * P:(k + 1) * P], rows[:, m, (4 * h + k) * P:(4 * h + k + 1) * P], ident[:])
                            last.then_inc(turned, 1)

                @block.vector
                def _(dve):
                    for m in range(2):
                        for h in range(2):
                            dve.wait_ge(turned, 2 * m + h + 1)
                            dve.tensor_copy(memT[:, 4 * h:4 * h + 4, m * P:(m + 1) * P], tp[2 * m + h][:].rearrange("p (k c) -> p k c", k=4))
        norm(nc, "mem", sem, sb, banks, memT, hmT, NM, 1, gains, g, ones)
        with ExitStack() as ctx:
            slots = sb(ctx, "mem_w", [P, 2, KD, 512])
            rows = memT[:].rearrange("p k m -> p (k m)").rearrange("p (m c) -> p m c", m=2)
            ps = banks(ctx, 4)
            w_in = [sem(f"mem_w{s}") for s in range(2)]
            done, kept, turned, row_kept, stored = (sem(f"mkv_{x}") for x in ("done", "kept", "turned", "rows", "stored"))
            with nc.Block() as block:
                @block.sync
                def _(sp):
                    for n in range(4):
                        if n >= 2:
                            sp.wait_ge(done, (4, 8)[n - 2])
                        w = i[("w_ck", "w_cv")[n // 2]][0].rearrange("(k p) n -> p k n", p=P)
                        sp.dma_start(slots[:, n % 2], w[:, :, (n % 2) * 512:(n % 2) * 512 + 512]).then_inc(w_in[n % 2], 16)
                    for n, (src, name) in enumerate(((rows, "new_mem_k_p"), (mv, "new_mem_v_p"))):
                        sp.wait_ge(row_kept, 4 * n + 4)
                        sp.dma_start(o[name][0, 0].rearrange("(m p) h d -> p m (h d)", p=P), src[:]).then_inc(stored, 16)
                    sp.wait_ge(stored, 32)

                @block.tensor
                def _(pe):
                    for n in range(8):
                        pe.wait_ge(w_in[n // 4], 16)
                        if n >= 2:
                            pe.wait_ge(kept, n - 1)
                        for k in range(KD):
                            last = pe.matmul(ps[n % 2][:, 0:NM], slots[:, n // 4, k, (n % 4) * P:(n % 4 + 1) * P], hmT[:, k, :],
                                             start=k == 0, stop=k == KD - 1)
                        last.then_inc(done, 1)
                    pe.wait_ge(kept, 8)
                    for m in range(2):
                        for h in range(2):
                            u = 2 * m + h
                            if u >= 2:
                                pe.wait_ge(row_kept, u - 1)
                            for k in range(4):
                                last = pe.transpose(ps[2 + u % 2][:, k * P:(k + 1) * P], mkT[:, 4 * h + k, m * P:(m + 1) * P], ident[:])
                            last.then_inc(turned, 1)
                    for h in range(2):
                        for m in range(2):
                            u = 4 + 2 * h + m
                            pe.wait_ge(w_in[h], 32)
                            pe.wait_ge(row_kept, u - 1)
                            for k in range(KD):
                                last = pe.matmul(ps[2 + u % 2][:], hmT[:, k, m * P:(m + 1) * P], slots[:, h, k, :], start=k == 0, stop=k == KD - 1)
                            last.then_inc(turned, 1)

                @block.scalar
                def _(act):
                    for n in range(8):
                        act.wait_ge(done, n + 1)
                        act.copy(mkT[:, n, :], ps[n % 2][:, 0:NM]).then_inc(kept, 1)

                @block.vector
                def _(dve):
                    for u in range(8):
                        dve.wait_ge(turned, u + 1)
                        if u < 4:
                            dst = rows[:, u // 2, 512 * (u % 2):512 * (u % 2) + 512]
                        else:
                            dst = mv[:, u % 2, 512 * (u // 2 - 2):512 * (u // 2 - 2) + 512]
                        dve.tensor_copy(dst, ps[2 + u % 2][:]).then_inc(row_kept, 1)


CSCALE = (D // 4) ** -0.5


MEM_SLOTS = 6
MEM_LOADS = [(name, 4 * grp + b) for grp in range(2) for name in ("cache_mem_k", "cache_mem_v") for b in range(4)]


def load_memory(sp, i, ring, ring_in, n):
    name, b = MEM_LOADS[n]
    sp.dma_start(ring[:, n % MEM_SLOTS], i[name][0, b].rearrange("(m p) h d -> p m (h d)", p=P)).then_inc(ring_in[n % MEM_SLOTS], 16)


def cross_prompt(nc, i, sem, sb, banks, cqT, qk, mkT, mv, ident, ring, ring_in):
    units = [(t, h) for t in range(NT) for h in range(4)]
    N = len(units)
    with ExitStack() as ctx:
        probs = sb(ctx, "cprobs", [P, 3, NM])
        turned = sb(ctx, "cturned", [P, 2, NM])
        scale = sb(ctx, "cscale", [P, 2, P])
        top_, mx, total, one_over = (sb(ctx, f"cp_{x}", [P, 4]) for x in ("top", "mx", "total", "one_over"))
        ps = banks(ctx, 7)
        score, peak, expd, divided, scaled, pt, pt_kept, pv, out_kept, chain = (
            sem(f"cp_{x}") for x in ("score", "peak", "exp", "divided", "scaled", "pt", "pt_kept", "pv", "out", "chain"))
        with nc.Block() as block:
            @block.sync
            def _(sp):
                for n in range(MEM_SLOTS):
                    load_memory(sp, i, ring, ring_in, n)

            @block.tensor
            def _(pe):
                def scores(u):
                    t, h = units[u]
                    if u >= 3:
                        pe.wait_ge(expd, u - 2)
                    for k in range(2):
                        last = pe.matmul(ps[u % 3][:, 0:NM], cqT[:, 2 * h + k, t * P:(t + 1) * P], mkT[:, 2 * h + k, :], start=k == 0, stop=k == 1)
                    last.then_inc(score, 1)

                def turn(u):
                    pe.wait_ge(scaled, u + 1)
                    if u >= 2:
                        pe.wait_ge(pt_kept, u - 1)
                    for m in range(2):
                        last = pe.matmul(ps[3 + u % 2][:, m * P:(m + 1) * P], probs[:, u % 3, m * P:(m + 1) * P], scale[:, u % 2], start=True, stop=True)
                    last.then_inc(pt, 1)

                def values(u):
                    t, h = units[u]
                    pe.wait_ge(pt_kept, u + 1)
                    if u >= 2:
                        pe.wait_ge(out_kept, u - 1)
                    for k in range(2):
                        for m in range(2):
                            last = pe.matmul(ps[5 + u % 2][:, k * P:(k + 1) * P], mv[:, m, (2 * h + k) * P:(2 * h + k + 1) * P],
                                             turned[:, u % 2, m * P:(m + 1) * P], start=m == 0, stop=m == 1)
                    last.then_inc(pv, 1)

                scores(0)
                scores(1)
                for u in range(N):
                    if u + 2 < N:
                        scores(u + 2)
                    turn(u)
                    if u > 0:
                        values(u - 1)
                values(N - 1)

            @block.gpsimd
            def _(pool):
                for u in range(N):
                    pool.wait_ge(divided, u + 1)
                    if u >= 2:
                        pool.wait_ge(pt, u - 1)
                    pool.tensor_scalar(scale[:, u % 2], ident[:], one_over[:, u % 4:u % 4 + 1], None, ALU.mult).then_inc(scaled, 1)

            @block.scalar
            def _(act):
                def exp(u):
                    act.wait_ge(peak, u + 1)
                    if u >= 3:
                        act.wait_ge(pt, u - 2)
                    act.activation(probs[:, u % 3], ps[u % 3][:, 0:NM], ACT.Exp, bias=mx[:, u % 4:u % 4 + 1], scale=CSCALE,
                                   accum_out=total[:, u % 4:u % 4 + 1]).then_inc(expd, 1)

                exp(0)
                for u in range(N):
                    if u + 1 < N:
                        exp(u + 1)
                    act.wait_ge(pt, u + 1)
                    if u >= 2:
                        act.wait_ge(pv, u - 1)
                    act.copy(turned[:, u % 2], ps[3 + u % 2][:, 0:NM]).then_inc(pt_kept, 1)

            @block.vector
            def _(dve):
                ch = Chain(dve, chain)

                def peaks(u):
                    dve.wait_ge(score, u + 1)
                    ch(dve.tensor_reduce(top_[:, u % 4:u % 4 + 1], ps[u % 3][:, 0:NM], X, ALU.max, negate=True))
                    dve.tensor_scalar(mx[:, u % 4:u % 4 + 1], top_[:, u % 4:u % 4 + 1], CSCALE, None, ALU.mult).then_inc(peak, 1)

                def keep(u):
                    t, h = units[u]
                    dve.wait_ge(pv, u + 1)
                    dve.tensor_copy(qk[:, 2 * h:2 * h + 2, t * P:(t + 1) * P],
                                    ps[5 + u % 2][:, 0:NM].rearrange("p (k c) -> p k c", k=2)).then_inc(out_kept, 1)

                peaks(0)
                peaks(1)
                for u in range(N):
                    dve.wait_ge(expd, u + 1)
                    dve.reciprocal(one_over[:, u % 4:u % 4 + 1], total[:, u % 4:u % 4 + 1]).then_inc(divided, 1)
                    if u + 2 < N:
                        peaks(u + 2)
                    if u > 0:
                        keep(u - 1)
                keep(N - 1)


def cross_sample(nc, i, sem, sb, banks, uv, qk, ident, ring, ring_in):
    with ExitStack() as ctx:
        kT = sb(ctx, "mem_kT", [P, 2, KD, NM])
        q_rows = sb(ctx, "cq_rows", [P, KD, NB, 32])
        probs = sb(ctx, "cs_probs", [P, 2, NM])
        turned = sb(ctx, "cs_turned", [P, 2, 2, P])
        one = sb(ctx, "cs_one", [P, 2, 4])
        tp = banks(ctx, 4)
        sc = banks(ctx, 2)
        out, probs_tp = banks(ctx, 2)
        zeroed, q_ready, keys, score, peak, expd, normed, pt, pt_kept, pv, chain = (
            sem(f"cs_{x}") for x in ("zeroed", "q", "keys", "score", "peak", "exp", "normed", "pt", "pt_kept", "pv", "chain"))
        kept = [sem(f"cs_kept{k}") for k in range(2)]
        with nc.Block() as block:
            @block.sync
            def _(sp):
                for n in range(MEM_SLOTS, len(MEM_LOADS)):
                    before, b = MEM_LOADS[n - MEM_SLOTS]
                    if before == "cache_mem_k":
                        sp.wait_ge(keys, 4 * b + 4)
                    else:
                        sp.wait_ge(pv, b + 1)
                    load_memory(sp, i, ring, ring_in, n)

            @block.gpsimd
            def _(pool):
                pool.memset(q_rows[:], 0.0).then_inc(zeroed, 1)

            @block.tensor
            def _(pe):
                pe.wait_ge(q_ready, KD)
                def turn_keys(b):
                    n = 8 * (b // 4) + b % 4
                    pe.wait_ge(ring_in[n % MEM_SLOTS], 16 * (n // MEM_SLOTS + 1))
                    for x in range(4):
                        if b > 0:
                            pe.wait_ge(kept[x % 2], 2 * b - 1 + x // 2)
                        for k in range(2):
                            for m in range(2):
                                last = pe.transpose(tp[x][:, k * NM + m * P:k * NM + (m + 1) * P],
                                                    ring[:, n % MEM_SLOTS, m, (2 * x + k) * P:(2 * x + k + 1) * P], ident[:])
                        last.then_inc(keys, 1)

                turn_keys(0)
                for grp in range(2):
                    for bb in range(4):
                        b = 4 * grp + bb
                        if b + 1 < NB:
                            turn_keys(b + 1)
                        for x in range(2):
                            pe.wait_ge(kept[x], 2 * b + 2)
                        for k in range(KD):
                            last = pe.matmul(sc[grp][32 * bb:32 * bb + 32, 0:NM], q_rows[:, k, b, :], kT[:, b % 2, k, :], start=k == 0, stop=k == KD - 1,
                                             tile_position=(0, 32 * bb), skip_group_check=True)
                        last.then_inc(score, 1)
                    pe.wait_ge(normed, grp + 1)
                    if grp > 0:
                        pe.wait_ge(pt_kept, grp)
                    for m in range(2):
                        last = pe.transpose(probs_tp[:, m * P:(m + 1) * P], probs[:, grp, m * P:(m + 1) * P], ident[:])
                    last.then_inc(pt, 1)
                    pe.wait_ge(pt_kept, grp + 1)
                    for bb in range(4):
                        b = 4 * grp + bb
                        n = 8 * grp + 4 + bb
                        pe.wait_ge(ring_in[n % MEM_SLOTS], 16 * (n // MEM_SLOTS + 1))
                        for k in range(KD):
                            r = 32 * bb + NS * (k // 2)
                            at = k * TS + NS * b
                            for m in range(2):
                                last = pe.matmul(out[:, at:at + NS], ring[:, n % MEM_SLOTS, m, k * P:(k + 1) * P], turned[:, grp, m, r:r + NS],
                                                 start=m == 0, stop=m == 1, skip_group_check=True)
                        last.then_inc(pv, 1)

            def keep(eng, copy, which):
                for b in range(NB):
                    for x in (which, which + 2):
                        eng.wait_ge(keys, 4 * b + x + 1)
                        if b > 1:
                            eng.wait_ge(score, b - 1)
                        copy(kT[:, b % 2, 2 * x:2 * x + 2, :].rearrange("p k c -> p (k c)"), tp[x][:]).then_inc(kept[which], 1)
                    if b % 4 == 3:
                        yield b // 4

            @block.scalar
            def _(act):
                for grp in keep(act, act.copy, 1):
                    act.wait_ge(peak, grp + 1)
                    act.activation(probs[:, grp], sc[grp][:, 0:NM], ACT.Exp, bias=one[:, grp, 0:1], scale=CSCALE,
                                   accum_out=one[:, grp, 1:2]).then_inc(expd, 1)

            @block.vector
            def _(dve):
                ch = Chain(dve, chain)
                dve.wait_ge(zeroed, 1)
                for k in range(KD):
                    h = k // 2
                    dve.tensor_copy(q_rows[:, k, :, NS * h:NS * h + NS], uv[:, k, NP:T].rearrange("p (b s) -> p b s", b=NB)).then_inc(q_ready, 1)
                for grp in keep(dve, dve.tensor_copy, 0):
                    dve.wait_ge(score, 4 * grp + 4)
                    ch(dve.tensor_reduce(one[:, grp, 2:3], sc[grp][:, 0:NM], X, ALU.max, negate=True))
                    dve.tensor_scalar(one[:, grp, 0:1], one[:, grp, 2:3], CSCALE, None, ALU.mult).then_inc(peak, 1)
                    dve.wait_ge(expd, grp + 1)
                    ch(dve.reciprocal(one[:, grp, 3:4], one[:, grp, 1:2]))
                    dve.tensor_scalar(probs[:, grp], probs[:, grp], one[:, grp, 3:4], None, ALU.mult).then_inc(normed, 1)
                    dve.wait_ge(pt, grp + 1)
                    dve.tensor_copy(turned[:, grp].rearrange("p m c -> p (m c)"), probs_tp[:, 0:NM]).then_inc(pt_kept, 1)
                dve.wait_ge(pv, NB)
                dve.tensor_copy(qk[:, 0:KD, NP:T], out[:, 0:KD * TS].rearrange("p (k t) -> p k t", k=KD))


def finish(nc, i, o, sem, sb, banks, xT, ident):
    with ExitStack() as ctx:
        gain = sb(ctx, "y_gain", [P, D])
        rows = sb(ctx, "y_rows", [P, 3, D])
        y = sb(ctx, "y", [P, 3, D])
        stat = sb(ctx, "y_stat", [P, 2, 2, 6])
        mom = sb(ctx, "y_mom", [P, 2, 3])
        rms = sb(ctx, "y_rms", [P, 4, 2])
        tp = [ctx.enter_context(nc.psum_tensor(f"y_tp{k}", [P, D], F32)) for k in range(4)]
        gain_in, turned, meant, rooted, divided, scaled, done, chain = (
            sem(f"y_{x}") for x in ("gain", "turned", "meant", "rooted", "divided", "scaled", "done", "chain"))
        stored = [sem(f"y_stored{s}") for s in range(3)]

        def n_rows(t):
            return P if t < NT else TS

        with nc.Block() as block:
            @block.tensor
            def _(pe):
                for t in range(NT + 1):
                    if t >= 4:
                        pe.wait_ge(scaled, t - 3)
                    for k in range(KD):
                        last = pe.transpose(tp[t % 4][0:n_rows(t), k * P:(k + 1) * P], xT[:, k, t * P:t * P + n_rows(t)], ident[:])
                    last.then_inc(turned, 1)

            @block.vector
            def _(dve):
                ch = Chain(dve, chain)

                def mean_square(t):
                    r, s = n_rows(t), t % 2
                    dve.wait_ge(turned, t + 1)
                    for h in range(2):
                        last = dve.bn_stats(stat[0:r, s, h], tp[t % 4][0:r, 512 * h:512 * h + 512])
                    ch(last)
                    ch(dve.bn_aggr(mom[0:r, s, 0:2], stat[0:r, s].rearrange("p h x -> p (h x)")))
                    ch(dve.tensor_tensor(mom[0:r, s, 2:3], mom[0:r, s, 0:1], mom[0:r, s, 0:1], ALU.mult))
                    dve.scalar_tensor_tensor(rms[0:r, t % 4, 0:1], mom[0:r, s, 1:2], EPS, mom[0:r, s, 2:3], ALU.add, ALU.add).then_inc(meant, 1)

                mean_square(0)
                for t in range(NT + 1):
                    if t < NT:
                        mean_square(t + 1)
                    r = n_rows(t)
                    dve.wait_ge(rooted, t + 1)
                    dve.reciprocal(rms[0:r, t % 4, 1:2], rms[0:r, t % 4, 0:1]).then_inc(divided, 1)

            @block.scalar
            def _(act):
                def root(t):
                    r = n_rows(t)
                    act.wait_ge(meant, t + 1)
                    act.sqrt(rms[0:r, t % 4, 0:1], rms[0:r, t % 4, 0:1]).then_inc(rooted, 1)

                root(0)
                for t in range(NT + 1):
                    if t < NT:
                        root(t + 1)
                    r = n_rows(t)
                    act.wait_ge(divided, t + 1)
                    if t >= 3:
                        act.wait_ge(done, t - 2)
                    act.mul(rows[0:r, t % 3], tp[t % 4][0:r, :], rms[0:r, t % 4, 1:2]).then_inc(scaled, 1)

            @block.gpsimd
            def _(pool):
                pool.wait_ge(gain_in, 16)
                for t in range(NT + 1):
                    r = n_rows(t)
                    pool.wait_ge(scaled, t + 1)
                    if t >= 3:
                        pool.wait_ge(stored[t % 3], 16 * (t // 3))
                    pool.tensor_tensor(y[0:r, t % 3], rows[0:r, t % 3], gain[0:r], ALU.mult).then_inc(done, 1)

            @block.sync
            def _(sp):
                sp.dma_start(gain[:], i["g_final"].partition_broadcast(P)).then_inc(gain_in, 16)
                for t in range(NT + 1):
                    sp.wait_ge(done, t + 1)
                    dst = o["y_prompt"][0, t * P:(t + 1) * P] if t < NT else o["y_sample"].rearrange("b s c -> (b s) c")
                    sp.dma_start(dst, y[0:n_rows(t), t % 3]).then_inc(stored[t % 3], 16)
                for s in range(3):
                    sp.wait_ge(stored[s], 16 * 3)


KV = (2, HD)
OUTS = [("y_prompt", (1, NP, D)), ("y_sample", (NB, NS, D)),
        ("new_cmp_k_p", (1, 1, NP, *KV)), ("new_cmp_v_p", (1, 1, NP, *KV)),
        ("new_slc_k_p", (1, 1, NP, *KV)), ("new_slc_v_p", (1, 1, NP, *KV)),
        ("new_win_k_p", (1, 1, WIN, *KV)), ("new_win_v_p", (1, 1, WIN, *KV)),
        ("new_mem_k_p", (1, 1, NM, 4, 256)), ("new_mem_v_p", (1, 1, NM, 4, 256)),
        ("new_cmp_k_s", (1, NB, NS, *KV)), ("new_cmp_v_s", (1, NB, NS, *KV)),
        ("new_slc_k_s", (1, NB, NS, *KV)), ("new_slc_v_s", (1, NB, NS, *KV)),
        ("new_win_k_s", (1, NB, WIN, *KV)), ("new_win_v_s", (1, NB, WIN, *KV)),
        ("new_gmlp_v_s", (1, NB, NS, 512))]


def kernel(**inputs):
    import concourse.bacc as bacc
    from concourse.bass_utils import run_bass_kernel_spmd

    nc = bacc.Bacc("TRN2", target_bir_lowering=False, num_devices=1)
    arrays = {k: np.ascontiguousarray(v) for k, v in inputs.items()}
    arrays.update(consts())
    ins = {k: nc.dram_tensor(k, v.shape, mybir.dt.from_np(v.dtype), kind="ExternalInput").ap() for k, v in arrays.items()}
    outs = {n: nc.dram_tensor("out_" + n, s, F32, kind="ExternalOutput").ap() for n, s in OUTS}
    build(nc, ins, outs)
    r = run_bass_kernel_spmd(nc, [arrays], core_ids=[0])
    return tuple(r.results[0]["out_" + n] for n, _ in OUTS)
```
